# Optimizing a Trainium2 kernel written in Bass

```python
import jax, jax.numpy as jnp
from jax import lax
import numpy as np
import math

D_MODEL = 1024
BATCH = 1
SEQ = 512
DEPTH = 2

MEM_LEN = 256
BRANCH_WIDTH = D_MODEL // 2
N_BRANCH = 4

RWKV_HEAD_DIM = 64
RWKV_HEADS = BRANCH_WIDTH // RWKV_HEAD_DIM
RWKV_LORA = 64
RWKV_GN_EPS = 64e-5

MLA_NOPE = 64
MLA_ROPE = 32
MLA_V = 64
MLA_HEADS = BRANCH_WIDTH // MLA_V
MLA_Q_LORA = 3 * D_MODEL // 8
MLA_KV_LORA = D_MODEL // 4
ROPE_THETA = 10000.0
Q_BLOCK = 128

CONV_KERNEL = 31

XATTN_HEADS = 4
XATTN_HEAD_DIM = BRANCH_WIDTH // XATTN_HEADS

DEEPNORM_ALPHA = (2.0 * DEPTH) ** 0.25
DEEPNORM_BETA = (8.0 * DEPTH) ** -0.25
LN_EPS = 1e-5
RMS_EPS = 1e-6
MASK_VALUE = -1e30

RWKV_SHIFT_COLS = 3 * BRANCH_WIDTH + 2 * RWKV_LORA
SPLIT_SIZES = (
    RWKV_SHIFT_COLS, BRANCH_WIDTH,
    MLA_Q_LORA, MLA_KV_LORA, MLA_ROPE, BRANCH_WIDTH,
    2 * BRANCH_WIDTH, BRANCH_WIDTH,
    BRANCH_WIDTH, BRANCH_WIDTH,
    N_BRANCH * D_MODEL,
)
SPLIT_POINTS = tuple(int(s) for s in np.cumsum(SPLIT_SIZES)[:-1])
IN_COLS = int(sum(SPLIT_SIZES))


def _layer_norm(x, g, b):
    xf = x.astype(jnp.float32)
    mu = jnp.mean(xf, -1, keepdims=True)
    var = jnp.mean(jnp.square(xf - mu), -1, keepdims=True)
    return ((xf - mu) * lax.rsqrt(var + LN_EPS)).astype(x.dtype) * g + b

def _rms_norm(x, g):
    xf = x.astype(jnp.float32)
    y = xf * lax.rsqrt(jnp.mean(jnp.square(xf), -1, keepdims=True) + RMS_EPS)
    return y.astype(x.dtype) * g

def _rope(x, cos, sin):
    half = x.shape[-1] // 2
    x1, x2 = x[..., :half], x[..., half:]
    return jnp.concatenate([x1 * cos - x2 * sin, x1 * sin + x2 * cos], axis=-1)

def _rwkv7_branch(p, gate, mu, w0, w2, a0, a2, k_k, k_a, r_k, lnx_g, lnx_b):
    B, S, _ = p.shape
    H, N, W = RWKV_HEADS, RWKV_HEAD_DIM, BRANCH_WIDTH
    p_prev = jnp.pad(p, ((0, 0), (1, 0), (0, 0)))[:, :-1]
    p = p + mu * (p_prev - p)
    r, k, v, wl, al = jnp.split(p, (W, 2 * W, 3 * W, 3 * W + RWKV_LORA), axis=-1)
    w_log = -jax.nn.softplus(-(w0 + jnp.tanh(wl) @ w2)) - 0.5
    decay = jnp.exp(-jnp.exp(w_log.astype(jnp.float32)))
    a = jax.nn.sigmoid(a0 + al @ a2)

    def heads(t):
        return t.reshape(B, S, H, N).astype(jnp.float32)

    kk = heads(k * k_k)
    kk = kk / jnp.maximum(jnp.linalg.norm(kk, axis=-1, keepdims=True), 1e-12)
    k = k * (1.0 + (a - 1.0) * k_a)
    r_h, k_h, v_h, a_h, w_h = heads(r), heads(k), heads(v), heads(a), heads(decay)
    xs = tuple(jnp.moveaxis(t, 1, 0) for t in (r_h, w_h, k_h, v_h, -kk, kk * a_h))

    def step(state, inp):
        r_t, w_t, k_t, v_t, a_t, b_t = inp
        sa = jnp.einsum('bhvk,bhk->bhv', state, a_t)
        state = (state * w_t[:, :, None, :] + sa[..., None] * b_t[:, :, None, :]
                 + v_t[..., None] * k_t[:, :, None, :])
        return state, jnp.einsum('bhvk,bhk->bhv', state, r_t)

    s0 = jnp.zeros((B, H, N, N), jnp.float32)
    _, y = lax.scan(step, s0, xs)
    y = jnp.moveaxis(y, 0, 1)
    y_mu = jnp.mean(y, -1, keepdims=True)
    y_var = jnp.mean(jnp.square(y - y_mu), -1, keepdims=True)
    y = ((y - y_mu) * lax.rsqrt(y_var + RWKV_GN_EPS)).reshape(B, S, W) * lnx_g + lnx_b
    bonus = jnp.sum(r_h * k_h * r_k, axis=-1, keepdims=True) * v_h
    y = y + bonus.reshape(B, S, W)
    return y.astype(gate.dtype) * jax.nn.silu(gate)

def _causal_block_attention(q, k, v, scale):
    B, S, H, Dq = q.shape
    nb = S // Q_BLOCK
    qb = jnp.moveaxis(q.reshape(B, nb, Q_BLOCK, H, Dq), 1, 0)
    key_idx = jnp.arange(S)

    def one_block(args):
        q_blk, i = args
        s = jnp.einsum('bqhd,bkhd->bhqk', q_blk, k).astype(jnp.float32) * scale
        q_idx = i * Q_BLOCK + jnp.arange(Q_BLOCK)
        s = jnp.where(key_idx[None, :] <= q_idx[:, None], s, MASK_VALUE)
        pr = jax.nn.softmax(s, axis=-1).astype(v.dtype)
        return jnp.einsum('bhqk,bkhd->bqhd', pr, v)

    o = lax.map(one_block, (qb, jnp.arange(nb)))
    return jnp.moveaxis(o, 0, 1).reshape(B, S, H, v.shape[-1])

def _mla_branch(q_lat, kv_lat, k_pe, gate, cos, sin, q_norm, w_uq, kv_norm, w_ukv):
    B, S, _ = q_lat.shape
    H = MLA_HEADS
    q = (_rms_norm(q_lat, q_norm) @ w_uq).reshape(B, S, H, MLA_NOPE + MLA_ROPE)
    kv = (_rms_norm(kv_lat, kv_norm) @ w_ukv).reshape(B, S, H, MLA_NOPE + MLA_V)
    q_nope, q_pe = q[..., :MLA_NOPE], q[..., MLA_NOPE:]
    k_nope, v = kv[..., :MLA_NOPE], kv[..., MLA_NOPE:]
    q_pe = _rope(q_pe, cos[:, :, None, :], sin[:, :, None, :])
    k_pe = _rope(k_pe, cos, sin)
    q_full = jnp.concatenate([q_nope, q_pe], axis=-1)
    k_full = jnp.concatenate(
        [k_nope, jnp.broadcast_to(k_pe[:, :, None, :], (B, S, H, MLA_ROPE))], axis=-1)
    o = _causal_block_attention(q_full, k_full, v, (MLA_NOPE + MLA_ROPE) ** -0.5)
    return o.reshape(B, S, BRANCH_WIDTH) * jax.nn.silu(gate)

def _conformer_conv_branch(u, gate, conv_w, conv_b, ln_g, ln_b):
    val, glu_gate = jnp.split(u, 2, axis=-1)
    h = val * jax.nn.sigmoid(glu_gate)
    h = lax.conv_general_dilated(
        h, conv_w[:, None, :], window_strides=(1,), padding=[(CONV_KERNEL - 1, 0)],
        dimension_numbers=('NWC', 'WIO', 'NWC'), feature_group_count=BRANCH_WIDTH) + conv_b
    h = jax.nn.silu(_layer_norm(h, ln_g, ln_b))
    return h * jax.nn.silu(gate)

def _memory_xattn_branch(q, gate, mem, w_mem_kv):
    B, S, _ = q.shape
    M = mem.shape[1]
    kv = mem @ w_mem_kv
    k = kv[..., :BRANCH_WIDTH].reshape(B, M, XATTN_HEADS, XATTN_HEAD_DIM)
    v = kv[..., BRANCH_WIDTH:].reshape(B, M, XATTN_HEADS, XATTN_HEAD_DIM)
    qh = q.reshape(B, S, XATTN_HEADS, XATTN_HEAD_DIM)
    s = jnp.einsum('bshd,bmhd->bhsm', qh, k).astype(jnp.float32) * XATTN_HEAD_DIM ** -0.5
    pr = jax.nn.softmax(s, axis=-1).astype(v.dtype)
    o = jnp.einsum('bhsm,bmhd->bshd', pr, v).reshape(B, S, BRANCH_WIDTH)
    return o * jax.nn.silu(gate)

def first_inputs(seed: int = 0) -> dict:
    key = jax.random.key(seed)
    ks = jax.random.split(key, 32)
    f32 = jnp.float32
    L, D, W = DEPTH, D_MODEL, BRANCH_WIDTH

    def nrm(k, shape, scale):
        return jax.random.normal(k, shape, f32) * scale

    x = jax.random.normal(ks[0], (BATCH, SEQ, D), f32)
    mem = jax.random.normal(ks[1], (BATCH, MEM_LEN, D), f32)
    start = jax.random.randint(ks[2], (BATCH, 1), 0, 4096, dtype=jnp.int32)
    positions = start + jnp.arange(SEQ, dtype=jnp.int32)[None, :]
    return {
        "x": x,
        "mem": mem,
        "positions": positions,
        "w_in": nrm(ks[3], (L, D, IN_COLS), D ** -0.5),
        "b_gate": nrm(ks[4], (L, N_BRANCH, D), 0.1),
        "rwkv_mu": jax.random.uniform(ks[5], (L, RWKV_SHIFT_COLS), f32),
        "rwkv_w0": jax.random.uniform(ks[6], (L, W), f32, -6.0, 0.0),
        "rwkv_w2": nrm(ks[7], (L, RWKV_LORA, W), 0.5 * RWKV_LORA ** -0.5),
        "rwkv_a0": nrm(ks[8], (L, W), 0.1),
        "rwkv_a2": nrm(ks[9], (L, RWKV_LORA, W), 0.5 * RWKV_LORA ** -0.5),
        "rwkv_k_k": 0.85 + nrm(ks[10], (L, W), 0.05),
        "rwkv_k_a": 1.0 + nrm(ks[11], (L, W), 0.05),
        "rwkv_r_k": nrm(ks[12], (L, RWKV_HEADS, RWKV_HEAD_DIM), 0.3),
        "rwkv_lnx_g": 1.0 + nrm(ks[13], (L, W), 0.02),
        "rwkv_lnx_b": nrm(ks[14], (L, W), 0.02),
        "mla_q_norm": 1.0 + nrm(ks[15], (L, MLA_Q_LORA), 0.02),
        "mla_w_uq": nrm(ks[16], (L, MLA_Q_LORA, MLA_HEADS * (MLA_NOPE + MLA_ROPE)), MLA_Q_LORA ** -0.5),
        "mla_kv_norm": 1.0 + nrm(ks[17], (L, MLA_KV_LORA), 0.02),
        "mla_w_ukv": nrm(ks[18], (L, MLA_KV_LORA, MLA_HEADS * (MLA_NOPE + MLA_V)), MLA_KV_LORA ** -0.5),
        "conv_w": nrm(ks[19], (L, CONV_KERNEL, W), CONV_KERNEL ** -0.5),
        "conv_b": nrm(ks[20], (L, W), 0.02),
        "conv_ln_g": 1.0 + nrm(ks[21], (L, W), 0.02),
        "conv_ln_b": nrm(ks[22], (L, W), 0.02),
        "xattn_w_mem_kv": nrm(ks[23], (L, D, 2 * W), D ** -0.5),
        "w_o_branch": nrm(ks[24], (L, N_BRANCH, W, D), DEEPNORM_BETA * W ** -0.5),
        "w_out": nrm(ks[25], (L, D, D), DEEPNORM_BETA * D ** -0.5),
        "ln_g": 1.0 + nrm(ks[26], (L, D), 0.02),
        "ln_b": nrm(ks[27], (L, D), 0.02),
    }

def first_block(x, mem, positions, w_in, b_gate, rwkv_mu, rwkv_w0, rwkv_w2, rwkv_a0, rwkv_a2,
              rwkv_k_k, rwkv_k_a, rwkv_r_k, rwkv_lnx_g, rwkv_lnx_b, mla_q_norm, mla_w_uq,
              mla_kv_norm, mla_w_ukv, conv_w, conv_b, conv_ln_g, conv_ln_b, xattn_w_mem_kv,
              w_o_branch, w_out, ln_g, ln_b):
    B, S, D = x.shape
    inv_freq = ROPE_THETA ** (-jnp.arange(0, MLA_ROPE, 2, dtype=jnp.float32) / MLA_ROPE)
    ang = positions.astype(jnp.float32)[..., None] * inv_freq
    cos = jnp.cos(ang).astype(x.dtype)
    sin = jnp.sin(ang).astype(x.dtype)
    for l in range(DEPTH):
        h = x @ w_in[l]
        (rw_p, rw_g, q_lat, kv_lat, k_pe, mla_g, conv_u, conv_g, xq, xg,
         merge) = jnp.split(h, SPLIT_POINTS, axis=-1)
        y_rwkv = _rwkv7_branch(rw_p, rw_g, rwkv_mu[l], rwkv_w0[l], rwkv_w2[l], rwkv_a0[l],
                               rwkv_a2[l], rwkv_k_k[l], rwkv_k_a[l], rwkv_r_k[l],
                               rwkv_lnx_g[l], rwkv_lnx_b[l])
        y_mla = _mla_branch(q_lat, kv_lat, k_pe, mla_g, cos, sin, mla_q_norm[l], mla_w_uq[l],
                            mla_kv_norm[l], mla_w_ukv[l])
        y_conv = _conformer_conv_branch(conv_u, conv_g, conv_w[l], conv_b[l], conv_ln_g[l],
                                        conv_ln_b[l])
        y_mem = _memory_xattn_branch(xq, xg, mem, xattn_w_mem_kv[l])
        branches = jnp.stack([y_rwkv, y_mla, y_conv, y_mem], axis=2)
        proj = jnp.einsum('bsnc,ncd->bsnd', branches, w_o_branch[l])
        gates = jax.nn.sigmoid(merge.reshape(B, S, N_BRANCH, D) + b_gate[l])
        merged = jnp.sum(gates * proj, axis=2)
        out = merged @ w_out[l]
        x = _layer_norm(DEEPNORM_ALPHA * x + out, ln_g[l], ln_b[l])
    return x


RET_HEADS = 4
RET_QK_DIM = 64
RET_V_DIM = 128
RET_CHUNK = 128
DIFF_HEADS = 4
DIFF_HEAD_DIM = 64
DIFF_V_DIM = 2 * DIFF_HEAD_DIM
FFN_HIDDEN = ((int(math.ceil(8 * D_MODEL / 3)) + 255) // 256) * 256
NORM_EPS = 1e-6

RET_Q_W = RET_HEADS * RET_QK_DIM
RET_V_W = RET_HEADS * RET_V_DIM
DIFF_QK_W = DIFF_HEADS * 2 * DIFF_HEAD_DIM
DIFF_V_W = DIFF_HEADS * DIFF_V_DIM
IN_SPLITS = [RET_Q_W, RET_Q_W, RET_V_W, RET_V_W, DIFF_QK_W, DIFF_QK_W, DIFF_V_W]
IN_WIDTH = sum(IN_SPLITS)
MIX_WIDTH = RET_V_W + DIFF_V_W


def rmsnorm(x, g):
    xf = x.astype(jnp.float32)
    y = xf * lax.rsqrt(jnp.mean(xf * xf, axis=-1, keepdims=True) + NORM_EPS)
    return (y * g.astype(jnp.float32)).astype(x.dtype)

def retention_gammas():
    return 1.0 - jnp.exp2(-5.0 - jnp.arange(RET_HEADS, dtype=jnp.float32))

def retention_chunkwise(q, k, v):
    B, S, H, dk = q.shape
    dv = v.shape[-1]
    C = RET_CHUNK
    N = S // C
    dt = q.dtype
    log_g = jnp.log(retention_gammas())
    k = k * jnp.asarray(dk ** -0.5, dt)
    q = q.reshape(B, N, C, H, dk)
    k = k.reshape(B, N, C, H, dk)
    v = v.reshape(B, N, C, H, dv)
    idx = jnp.arange(C, dtype=jnp.float32)
    rel = idx[:, None] - idx[None, :]
    decay = jnp.where(rel[None] >= 0,
                      jnp.exp(jnp.maximum(rel, 0.0)[None] * log_g[:, None, None]),
                      0.0).astype(dt)
    s = jnp.einsum('bnchd,bnshd->bnhcs', q, k) * decay
    inner = jnp.einsum('bnhcs,bnshe->bnche', s, v)
    k_decay = jnp.exp((C - 1 - idx)[:, None] * log_g[None, :]).astype(dt)
    kv = jnp.einsum('bnshd,bnshe->nbhde', k * k_decay[:, :, None], v)
    g_chunk = jnp.exp(C * log_g).astype(dt)[None, :, None, None]

    def step(state, kv_n):
        return g_chunk * state + kv_n, state

    _, states = lax.scan(step, jnp.zeros((B, H, dk, dv), dt), kv)
    q_decay = jnp.exp((idx + 1.0)[:, None] * log_g[None, :]).astype(dt)
    cross = jnp.einsum('bnchd,nbhde->bnche', q * q_decay[:, :, None], states)
    return (inner + cross).reshape(B, S, H, dv)

def alibi_slopes(n):
    return jnp.exp2(-8.0 * jnp.arange(1, n + 1, dtype=jnp.float32) / n)

def diff_attention(q, k, v, lam):
    S = q.shape[1]
    d = q.shape[-1]
    scale = d ** -0.5
    slopes = alibi_slopes(q.shape[2])
    outs = []
    for i in range(S // Q_BLOCK):
        q0 = i * Q_BLOCK
        kend = q0 + Q_BLOCK
        qb = q[:, q0:kend]
        kb = k[:, :kend]
        vb = v[:, :kend]
        s = jnp.einsum('bqhjd,bkhjd->bhjqk', qb, kb).astype(jnp.float32) * scale
        dist = (q0 + jnp.arange(Q_BLOCK, dtype=jnp.float32))[:, None] - jnp.arange(kend, dtype=jnp.float32)[None, :]
        s = s - slopes[None, :, None, None, None] * dist
        s = jnp.where(dist >= 0, s, -jnp.inf)
        p = jax.nn.softmax(s, axis=-1)
        a = p[:, :, 0] - lam * p[:, :, 1]
        outs.append(jnp.einsum('bhqk,bkhe->bqhe', a.astype(vb.dtype), vb))
    return jnp.concatenate(outs, axis=1)

def second_inputs(seed: int = 0) -> dict:
    key = jax.random.key(seed)
    ks = jax.random.split(key, 16)
    f = jnp.float32

    def nrm(k, shape, scale):
        return jax.random.normal(k, shape, f) * scale

    def gain(k, shape):
        return 1.0 + 0.02 * jax.random.normal(k, shape, f)

    return {
        "x": jax.random.normal(ks[0], (BATCH, SEQ, D_MODEL), f),
        "attn_norm": gain(ks[1], (DEPTH, D_MODEL)),
        "w_in": nrm(ks[2], (DEPTH, D_MODEL, IN_WIDTH), D_MODEL ** -0.5),
        "ret_norm": gain(ks[3], (DEPTH, RET_V_DIM)),
        "lambda_q1": nrm(ks[4], (DEPTH, DIFF_HEAD_DIM), 0.1),
        "lambda_k1": nrm(ks[5], (DEPTH, DIFF_HEAD_DIM), 0.1),
        "lambda_q2": nrm(ks[6], (DEPTH, DIFF_HEAD_DIM), 0.1),
        "lambda_k2": nrm(ks[7], (DEPTH, DIFF_HEAD_DIM), 0.1),
        "diff_norm": gain(ks[8], (DEPTH, DIFF_V_DIM)),
        "w_out": nrm(ks[9], (DEPTH, MIX_WIDTH, D_MODEL), MIX_WIDTH ** -0.5),
        "ffn_norm": gain(ks[10], (DEPTH, D_MODEL)),
        "w_gate": nrm(ks[11], (DEPTH, D_MODEL, FFN_HIDDEN), D_MODEL ** -0.5),
        "w_up": nrm(ks[12], (DEPTH, D_MODEL, FFN_HIDDEN), D_MODEL ** -0.5),
        "w_down": nrm(ks[13], (DEPTH, FFN_HIDDEN, D_MODEL), FFN_HIDDEN ** -0.5),
        "final_norm": gain(ks[14], (D_MODEL,)),
    }

def second_block(x, attn_norm, w_in, ret_norm, lambda_q1, lambda_k1, lambda_q2, lambda_k2,
              diff_norm, w_out, ffn_norm, w_gate, w_up, w_down, final_norm):
    B, S, _ = x.shape
    offsets = np.cumsum(IN_SPLITS)[:-1].tolist()
    h = x
    for l in range(DEPTH):
        u = rmsnorm(h, attn_norm[l])
        proj = u @ w_in[l]
        rq, rk, rv, rg, dq, dk, dv = jnp.split(proj, offsets, axis=-1)

        ret = retention_chunkwise(rq.reshape(B, S, RET_HEADS, RET_QK_DIM),
                                  rk.reshape(B, S, RET_HEADS, RET_QK_DIM),
                                  rv.reshape(B, S, RET_HEADS, RET_V_DIM))
        ret = rmsnorm(ret, ret_norm[l]).reshape(B, S, RET_V_W)
        ret = jax.nn.silu(rg) * ret

        lam_init = 0.8 - 0.6 * math.exp(-0.3 * l)
        lam = (jnp.exp(jnp.sum(lambda_q1[l].astype(jnp.float32) * lambda_k1[l].astype(jnp.float32)))
               - jnp.exp(jnp.sum(lambda_q2[l].astype(jnp.float32) * lambda_k2[l].astype(jnp.float32)))
               + lam_init)
        dif = diff_attention(dq.reshape(B, S, DIFF_HEADS, 2, DIFF_HEAD_DIM),
                             dk.reshape(B, S, DIFF_HEADS, 2, DIFF_HEAD_DIM),
                             dv.reshape(B, S, DIFF_HEADS, DIFF_V_DIM), lam)
        dif = (rmsnorm(dif, diff_norm[l]) * (1.0 - lam_init)).reshape(B, S, DIFF_V_W)

        mix = jnp.concatenate([ret, dif], axis=-1)
        h = h + mix @ w_out[l]

        u = rmsnorm(h, ffn_norm[l])
        h = h + (jax.nn.silu(u @ w_gate[l]) * (u @ w_up[l])) @ w_down[l]
    return rmsnorm(h, final_norm)


def setup_inputs(seed=0):
    out = dict(first_inputs(seed))
    for name, value in second_inputs(seed + 1).items():
        if name != "x":
            out[name + "_2"] = value
    return out


def reference(
    x, mem, positions, w_in, b_gate, rwkv_mu, rwkv_w0, rwkv_w2, rwkv_a0, rwkv_a2, rwkv_k_k,
    rwkv_k_a, rwkv_r_k, rwkv_lnx_g, rwkv_lnx_b, mla_q_norm, mla_w_uq, mla_kv_norm, mla_w_ukv,
    conv_w, conv_b, conv_ln_g, conv_ln_b, xattn_w_mem_kv, w_o_branch, w_out, ln_g, ln_b,
    attn_norm_2, w_in_2, ret_norm_2, lambda_q1_2, lambda_k1_2, lambda_q2_2, lambda_k2_2,
    diff_norm_2, w_out_2, ffn_norm_2, w_gate_2, w_up_2, w_down_2, final_norm_2,
):
    x = first_block(
        x, mem, positions, w_in, b_gate, rwkv_mu, rwkv_w0, rwkv_w2, rwkv_a0, rwkv_a2, rwkv_k_k,
        rwkv_k_a, rwkv_r_k, rwkv_lnx_g, rwkv_lnx_b, mla_q_norm, mla_w_uq, mla_kv_norm,
        mla_w_ukv, conv_w, conv_b, conv_ln_g, conv_ln_b, xattn_w_mem_kv, w_o_branch, w_out,
        ln_g, ln_b,
    )
    return second_block(
        x, attn_norm_2, w_in_2, ret_norm_2, lambda_q1_2, lambda_k1_2, lambda_q2_2, lambda_k2_2,
        diff_norm_2, w_out_2, ffn_norm_2, w_gate_2, w_up_2, w_down_2, final_norm_2,
    )


_drawn_inputs = setup_inputs


def setup_inputs(seed=0):
    import zlib

    import numpy as np

    out = dict(_drawn_inputs(seed))
    spreads = {}
    factors = {'mem': 3.601,
     'b_gate': 7.395,
     'rwkv_w2': 8.0,
     'rwkv_a0': 7.907,
     'rwkv_k_k': 8.0,
     'rwkv_k_a': 6.112,
     'rwkv_lnx_g': 8.0,
     'rwkv_lnx_b': 8.0,
     'mla_q_norm': 8.0,
     'mla_w_uq': 2.848,
     'mla_kv_norm': 8.0,
     'conv_b': 8.0,
     'conv_ln_g': 8.0,
     'conv_ln_b': 8.0,
     'xattn_w_mem_kv': 3.452,
     'ret_norm_2': 5.109,
     'diff_norm_2': 4.023,
     'ffn_norm_2': 2.953,
     'final_norm_2': 2.848}
    for name, (base, spread) in spreads.items():
        noise = np.random.default_rng([zlib.crc32(name.encode()), seed]).standard_normal(out[name].shape)
        drawn = base * np.exp(spread * noise) if base else spread * noise
        out[name] = __import__('jax').numpy.asarray(drawn.astype(out[name].dtype))
    for name, factor in factors.items():
        out[name] = (out[name] * factor).astype(out[name].dtype)
    return out
```

```python
from contextlib import ExitStack
import math

import numpy as np
import concourse.bass as bass
from concourse import mybir

P = 128
T = 512
NT = T // P
D = 1024
KD = D // P
W = 512
NW = W // P
DEPTH = 2
MEM = 256
GW = 1024
SPLIT_SLOTS = 2
STAGE_SLOTS = 2
TAPS = 31
F32 = mybir.dt.float32
F32R = mybir.dt.float32r
I32 = mybir.dt.int32
ALU = mybir.AluOpType
ACT = mybir.ActivationFunctionType
AX = mybir.AxisListType.X
MASKED = -1e30
ALPHA = (2.0 * DEPTH) ** 0.25
KAPPA = math.exp(-0.5) / 2
CH = P
FFN = 2816
ARENA = 18200
NF = FFN // P

_P1 = [("mu", 13), ("w0", 4), ("a0", 4), ("k_k", 4), ("k_a", 4), ("r_k", 4), ("lnx_g", 4),
       ("lnx_b", 4), ("q_norm", 3), ("kv_norm", 2), ("conv_w", NW * TAPS), ("conv_b", 4),
       ("cln_g", 4), ("cln_b", 4), ("b_gate", 32), ("ln_g", 8), ("ln_b", 8), ("inv_freq", 1)]
_P2 = [("attn_norm", 8), ("ret_norm", 1), ("diff_norm", 1), ("ffn_norm", 8), ("lam", 4),
       ("lam_init", 1), ("lam_rest", 1), ("final_norm", 8), ("log_gamma", 4), ("slope", 4)]


def offsets(spec):
    at, out = 0, {}
    for name, n in spec:
        out[name] = (at, n)
        at += n
    return out, at


PC1, NP1 = offsets(_P1)
PC2, NP2 = offsets(_P2)
G1 = 8 + 4 + 6 + 4 + 8 + 16 + 12 + 2 + 36 + 4 + 12 + 8
G2 = 12 + 12 + 8 + 2 * NF + 24


class Sems:

    def __init__(self, nc, ctx, prefix=""):
        self.nc, self.ctx, self.prefix, self.all = nc, ctx, prefix, {}

    def __getitem__(self, name):
        if name not in self.all:
            self.all[name] = self.ctx.enter_context(self.nc.semaphore(self.prefix + name))
        return self.all[name]


def helpers(S):
    def give(eng, *names):
        for name in names:
            eng.sem_inc(S[name], 1)

    def fin(eng, own, ins, *names):
        ins.then_inc(S[own], 1)
        eng.wait_ge(S[own], 1)
        eng.sem_inc(S[own], -1)
        give(eng, *names)

    return give, fin


def weight_loader(sp, S, stage, stream, groups):
    with sp.Fori(0, groups // STAGE_SLOTS) as g:
        for s in range(STAGE_SLOTS):
            sp.wait_ge(S[f"stage{s}_free"], 1)
            sp.sem_inc(S[f"stage{s}_free"], -1)
            sp.dma_start(stage[:, s, :], stream[bass.ds(g * STAGE_SLOTS + s, 1)].rearrange("a p n -> p (a n)"))\
              .then_inc(S[f"stage{s}_full"], 16)
    sp.wait_ge(S["stage0_free"], 1)
    sp.sem_inc(S["stage0_free"], -1)
    sp.dma_start(stage[:, 0, :], stream[groups]).then_inc(S["stage0_full"], 16)


def weight_remainders(pool, S, give, fin, stage, wh, wl, groups):
    for s in range(STAGE_SLOTS):
        give(pool, f"stage{s}_free")
    give(pool, "w0_free")
    with pool.Fori(0, groups // STAGE_SLOTS) as g:
        for s in range(STAGE_SLOTS):
            pool.wait_ge(S[f"hi{s}_ready"], 1)
            pool.sem_inc(S[f"hi{s}_ready"], -1)
            fin(pool, "pool_self", pool.tensor_tensor(wl[:, s, :], stage[:, s, :], wh[:, s, :].bitcast(F32),
                                                      ALU.subtract), f"w{s}_ready", f"stage{s}_free")
    pool.wait_ge(S["hi0_ready"], 1)
    pool.sem_inc(S["hi0_ready"], -1)


def rounder(act, S, stage, wh):
    slot = [0]

    def round_next():
        s = slot[0]
        slot[0] = 1 - s
        act.wait_ge(S[f"stage{s}_full"], 16)
        act.sem_inc(S[f"stage{s}_full"], -16)
        act.wait_ge(S[f"w{s}_free"], 1)
        act.sem_inc(S[f"w{s}_free"], -1)
        act.activation(wh[:, s, :], stage[:, s, :], ACT.Copy).then_inc(S[f"hi{s}_ready"], 1)

    return round_next


class Projector:

    def __init__(self, pe, S, wh, wl):
        self.pe, self.S, self.wh, self.wl, self.slot, self.release = pe, S, wh, wl, 1, None

    def group(self):
        self.release = f"w{self.slot}_free"
        self.slot = 1 - self.slot
        self.pe.wait_ge(self.S[f"w{self.slot}_ready"], 1)
        self.pe.sem_inc(self.S[f"w{self.slot}_ready"], -1)
        return self.wh[:, self.slot, :], self.wl[:, self.slot, :]

    def product(self, out, terms, done=None, more=False, first=True):
        steps = [(a, b) for (ah, al), (bh, bl) in terms for a, b in ((ah, bh), (ah, bl), (al, bh))]
        for n, (a, b) in enumerate(steps):
            ins = self.pe.matmul(out, a, b, start=first and n == 0, stop=not more and n == len(steps) - 1)
            if n == 0 and self.release:
                ins.then_inc(self.S[self.release], 1)
                self.release = None
        if done:
            ins.then_inc(self.S[done], 1)

    def channels(self, out, w, x, kt, width, c0=0, cn=P, done=None, k0=0, more=False, first=True):
        wh, wl = w
        self.product(out, [((wh[:, k * width + c0:k * width + c0 + cn], wl[:, k * width + c0:k * width + c0 + cn]),
                            (x[0][:, k0 + k, :], x[1][:, k0 + k, :])) for k in range(kt)], done, more, first)


def first_block(nc, S, x_dram, mem_dram, pos_dram, par_dram, lora_dram, stream, hT):
    give, fin = helpers(S)
    with ExitStack() as ctx:
        def sb(name, shape, dt=F32):
            return ctx.enter_context(nc.sbuf_tensor(name + "_1", shape, dt))

        bank = [ctx.enter_context(nc.psum_tensor(f"bank{i}_1", [P, 512], F32)) for i in range(8)]
        g0, g1 = bank[0], bank[1]
        A = bank[2:]
        stage = sb("stage", [P, STAGE_SLOTS, GW])
        wh = sb("wh", [P, SPLIT_SLOTS, GW], F32R)
        wl = sb("wl", [P, SPLIT_SLOTS, GW], F32R)
        xh = sb("xh", [P, KD, T], F32R)
        xl = sb("xl", [P, KD, T], F32R)
        yh = sb("yh", [P, 12, T], F32R)
        yl = sb("yl", [P, 12, T], F32R)
        par = sb("par", [P, NP1])
        der = sb("der", [P, 64])
        ones = sb("ones", [P, P])
        ident = sb("ident", [P, P])
        halves = sb("halves", [P, P])
        future = sb("future", [P, P])
        after = sb("after", [P, 2, P])
        before = sb("before", [P, P])
        level = sb("level", [P, 7, 2, P], mybir.dt.uint8)
        rotm = sb("rotm", [P, 32])
        eps = sb("eps", [P, 4])
        tmp = sb("tmp", [P, 2, T])
        sq = sb("sq", [P, 2, T])
        rstd = sb("rstd", [P, T])
        arena = sb("arena", [P, ARENA])

        class Carve:

            def __init__(self, at=0):
                self.at = at

            def __call__(self, *shape):
                n = int(np.prod(shape))
                v = arena[:, self.at:self.at + n]
                self.at += n
                assert self.at <= ARENA, self.at
                if len(shape) == 2:
                    v = v.rearrange("p (a b) -> p a b", b=shape[1])
                if len(shape) == 3:
                    v = v.rearrange("p (a b c) -> p a b c", b=shape[1], c=shape[2])
                return v

        c = Carve()
        hb = c(NW, T + 32)
        cacc = c(NW, T)
        cgate = c(NW, T)
        c = Carve(c.at)
        y32 = c(NW, T)
        Q = c(T)
        PT = c(NT, T)
        gate = c(T)
        K = c(T)
        probs = c(2, T)
        st = c(16)
        V = c(NT, 64)
        mgate = c(NW, T)
        kr = c(T)
        trig = c(2, T)
        causal = kr
        c = Carve(NW * (T + 32) + 2 * NW * T)
        lsq = c(5, T)
        lat = c(5, T)
        memf = Carve(0)(KD, MEM)
        xprobs = probs.rearrange("p a (b m) -> p (a b) m", m=MEM)
        xPT = PT[:, 0:2, :]
        xV = V.rearrange("p a b -> p (a b)").rearrange("p (a b) -> p a b", b=P)
        c = Carve()
        RKV = c(12, T)
        R, RK_, RV = RKV[:, 0:4, :], RKV[:, 4:8, :], RKV[:, 8:12, :]
        KK = c(NW, T)
        BB = c(NW, T)
        TH = c(NW, T)
        rgate = TH
        flat = tmp[:].rearrange("p a b -> p (a b)")
        AR = flat[:, 0:512].rearrange("p (a b c) -> p a b c", a=2, b=2)
        Bt = flat[:, 512:768].rearrange("p (a b) -> p a b", a=2)
        Kt = flat[:, 768:1024].rearrange("p (a b) -> p a b", a=2)
        EP = rstd[:, 0:2 * (P + 1)].rearrange("p (a b) -> p a b", a=2)
        Sm = rstd[:, 260:388].rearrange("p (a b) -> p a b", a=2)
        emid = rstd[:, 388:390]
        TM = c(6, P)
        UM = c(4, 4 * P)
        Tm = c(4, P)
        XZ = c(4, 2, P)
        Qs = c(4, P)
        QC = c(2, P + 1)
        St = c(NW, 64)
        rhs_s = Bt[:, :, :].rearrange("p a b -> p (a b)")
        sa_s = Kt[:, :, :].rearrange("p a b -> p (a b)")
        rkc = Qs[:, 0:2, :]
        EM = XZ[:, 0, :, :]
        QD = XZ[:, 1:4, :, :].rearrange("p a b c -> p (a b c)")[:, 0:2 * (P + 1)].rearrange("p (a b) -> p a b", b=P + 1)
        Vc = c(2, P)
        wa = UM[:, 0, :]
        lora = UM[:, 1, :]

        def col(name, i=0, n=1):
            a = PC1[name][0]
            return par[:, a + i:a + i + n] if isinstance(i, int) else par[:, bass.ds(i + a, n)]

        def tile(t, i):
            return t[:, i, :] if isinstance(i, int) else t[:, bass.ds(i, 1), :].rearrange("p a t -> p (a t)")

        block = ctx.enter_context(nc.Block())

        @block.sync
        def _(sp):
            weight_loader(sp, S, stage, stream, DEPTH * G1)

        @block.gpsimd
        def _(pool):
            def op(ins, *names):
                fin(pool, "pool_self", ins, *names)

            def select(t, pattern, base, mult, compare=ALU.is_ge, fill=0.0, *names):
                op(pool.affine_select(out=t, in_=t, compare_op=compare, fill=fill, base=base, pattern=pattern,
                                      channel_multiplier=mult), *names)

            op(pool.memset(ones[:], 1.0))
            op(pool.memset(ident[:], 0.0))
            select(ident[:], [[-1, P]], 0, 1, ALU.not_equal, 1.0)
            op(pool.memset(halves[:], 1.0))
            select(halves[:, 0:64], [[0, 64]], 63, -1)
            select(halves[:, 64:P], [[0, 64]], -64, 1)
            op(pool.memset(future[:], 0.0))
            select(future[:], [[-1, P]], 0, 1, ALU.is_ge, MASKED)
            op(pool.memset(after[:], 1.0))
            select(after[:, 0, :], [[1, P]], -1, -1)
            select(after[:, 1, :], [[1, P]], 0, -1)
            op(pool.memset(before[:], 1.0))
            select(before[:], [[-1, P]], -1, 1)
            op(pool.memset(rotm[:], 0.0))
            select(rotm[64:96, :], [[-1, 32]], -16, 1, ALU.not_equal, -1.0)
            select(rotm[64:96, :], [[-1, 32]], 16, 1, ALU.not_equal, 1.0)
            for n in range(7):
                b = 1 << n
                m = arena[:, 0:2 * P].rearrange("p (o j h c) -> p o j h c", o=2, h=2, c=b)
                op(pool.memset(arena[:, 0:2 * P], 0.0))
                for o in range(2):
                    v = m[:, o, :, o, :]
                    op(pool.memset(v, 1.0))
                    lo = b * (1 - o)
                    pat = [[-2 * b, P // (2 * b)], [0, b]]
                    select(v, pat, -lo, 1)
                    select(v, [[2 * b, P // (2 * b)], [0, b]], lo + b - 1, -1)
                op(pool.tensor_copy(level[:, n, :, :].rearrange("p a b -> p (a b)"), arena[:, 0:2 * P]))
            give(pool, "consts_pe", "consts_act", "consts_dve")
            weight_remainders(pool, S, give, fin, stage, wh, wl, DEPTH * G1)

        @block.tensor
        def _(pe):
            pe.wait_ge(S["consts_pe"], 1)
            pe.sem_inc(S["consts_pe"], -1)
            proj = Projector(pe, S, wh, wl)
            X = (xh, xl)

            def gates():
                with pe.Fori(0, NW // 2):
                    for s, g in enumerate((g0, g1)):
                        pe.wait_ge(S[f"g{s}_free"], 1)
                        pe.sem_inc(S[f"g{s}_free"], -1)
                        proj.channels(g[:], proj.group(), X, KD, P, done="gate_proj")

            def total(out, tiles, want, done, matrix=ones):
                pe.wait_ge(S[want], 1)
                pe.sem_inc(S[want], -1)
                for n, t in enumerate(tiles):
                    ins = pe.matmul(out, matrix[:], t, start=n == 0, stop=n == len(tiles) - 1)
                ins.then_inc(S[done], 1)

            def layer_norm(tiles):
                total(A[0][:], tiles, "ln_in", "ln_sum")
                for i in range(len(tiles)):
                    pe.wait_ge(S[f"sq{i % 2}_ready"], 1)
                    pe.sem_inc(S[f"sq{i % 2}_ready"], -1)
                    pe.matmul(A[1][:], ones[:], sq[:, i % 2, :], start=i == 0, stop=i == len(tiles) - 1)\
                      .then_inc(S[f"sq{i % 2}_used"], 1)

            def merge(branch, slot, d):
                for s, g in enumerate((g0, g1)):
                    pe.wait_ge(S[f"g{s}_free"], 1)
                    pe.sem_inc(S[f"g{s}_free"], -1)
                    proj.channels(g[:], proj.group(), X, KD, P, done="merge_gate")
                w = proj.group()
                for s, g in enumerate((g0, g1)):
                    pe.wait_ge(S[f"g{s}_free"], 1)
                    pe.sem_inc(S[f"g{s}_free"], -1)
                    proj.channels(g[:], w, (yh[:, 4 * slot:4 * slot + 4, :], yl[:, 4 * slot:4 * slot + 4, :]), NW,
                                  2 * P, c0=s * P, done="merge_proj")

            def mla_head(a):
                h, lo = proj.group()
                q = (h[:, 0:288], lo[:, 0:288])
                kv = (h[:, 288:544], lo[:, 288:544])
                pe.wait_ge(S["g0_free"], 1)
                pe.sem_inc(S["g0_free"], -1)
                proj.channels(g0[0:96, :], q, (yh[:, 4:7, :], yl[:, 4:7, :]), 3, 96, cn=96, done="q_proj")
                pe.wait_ge(S["g1_free"], 1)
                pe.sem_inc(S["g1_free"], -1)
                proj.channels(g1[:], kv, (yh[:, 8:10, :], yl[:, 8:10, :]), 2, P, done="k_proj")
                pe.wait_ge(S["a5_free"], 1)
                pe.sem_inc(S["a5_free"], -1)
                for t in range(NT):
                    cs = slice(t * P, (t + 1) * P)
                    proj.product(A[5][:, 64 * t:64 * t + 64],
                                 [((yh[:, 8 + k, cs], yl[:, 8 + k, cs]),
                                   tuple(w[:, k * P + 64:(k + 1) * P] for w in kv)) for k in range(2)],
                                 "v_proj" if t == NT - 1 else None)
                pe.wait_ge(S["q_raw"], 1)
                pe.sem_inc(S["q_raw"], -1)
                pe.wait_ge(S["a4_free"], 1)
                pe.sem_inc(S["a4_free"], -1)
                pe.matmul(A[4][64:96, :], rotm[64:96, :], Q[64:96, :], start=True, stop=True).then_inc(S["q_rot"], 1)
                pe.wait_ge(S["qk_ready"], 1)
                pe.sem_inc(S["qk_ready"], -1)
                pe.wait_ge(S["k_ready"], 1)
                pe.sem_inc(S["k_ready"], -1)

                def scores(t):
                    n = (t + 1) * P
                    pe.wait_ge(S[f"a{t % 2}_free"], 1)
                    pe.sem_inc(S[f"a{t % 2}_free"], -1)
                    pe.matmul(A[t % 2][:, 0:n], Q[0:96, t * P:n], K[0:96, 0:n], start=True, stop=True)\
                      .then_inc(S["scores"], 1)

                scores(0)
                for t in range(NT):
                    if t + 1 < NT:
                        scores(t + 1)
                    pe.wait_ge(S["probs_ready"], 1)
                    pe.sem_inc(S["probs_ready"], -1)
                    pe.wait_ge(S["a4_free"], 1)
                    pe.sem_inc(S["a4_free"], -1)
                    for i in range(t + 1):
                        ins = pe.transpose(A[4][:, i * P:(i + 1) * P], probs[:, t % 2, i * P:(i + 1) * P], ident[:])
                    ins.then_inc(S["probs_turned"], 1)
                pe.wait_ge(S["v_ready"], 1)
                pe.sem_inc(S["v_ready"], -1)
                pe.wait_ge(S["weights_ready"], 1)
                pe.sem_inc(S["weights_ready"], -1)
                pe.wait_ge(S["a5_free"], 1)
                pe.sem_inc(S["a5_free"], -1)
                for i in range(NT):
                    ins = pe.matmul(A[5][64 * a:64 * a + 64, i * P:T], V[:, i, :], PT[:, i, i * P:T],
                                    start=i == 0, stop=i == NT - 1)
                ins.then_inc(S["head_out"], 1)

            def rwkv_half(g, fill):
                r = [slice(64 * (j % 2), 64 * (j % 2) + 64) for j in range(4)]
                pe.wait_ge(S["ab_ready"], 1)
                pe.sem_inc(S["ab_ready"], -1)
                for j in range(4):
                    pe.wait_ge(S[f"a{j}_free"], 1)
                    pe.sem_inc(S[f"a{j}_free"], -1)
                    x = AR[r[j], j // 2, :, :].rearrange("p a b -> p (a b)")
                    pe.matmul(A[j][:, 0:256], Bt[r[j], j // 2, :], x, start=True, stop=True)
                    pe.matmul(A[j][:, 256:512], Kt[r[j], j // 2, :], x, start=True, stop=True)\
                      .then_inc(S["um_out"], 1)
                for p in range(2):
                    pe.wait_ge(S[f"a{4 + p}_free"], 1)
                    pe.sem_inc(S[f"a{4 + p}_free"], -1)
                    for i in range(2):
                        j = 2 * i + p
                        ins = pe.matmul(A[4 + p][:, i * P:(i + 1) * P], AR[r[j], i, 0, :], Bt[r[j], i, :],
                                        start=True, stop=True)
                    ins.then_inc(S["t_out"], 1)
                fill(0)
                pe.wait_ge(S["a0_free"], 1)
                pe.sem_inc(S["a0_free"], -1)
                for i in range(2):
                    pe.transpose(A[0][:, i * P:(i + 1) * P], Vc[:, i, :], ident[:])
                    ins = pe.transpose(A[0][:, (2 + i) * P:(3 + i) * P], Bt[:, i, :], ident[:])
                ins.then_inc(S["turned"], 1)
                pe.wait_ge(S["a1_free"], 1)
                pe.sem_inc(S["a1_free"], -1)
                for i in range(2):
                    pe.transpose(A[1][:, i * P:(i + 1) * P], Kt[:, i, :], ident[:])
                ins = pe.matmul(A[1][:, 256:512], halves[:], rkc.rearrange("p a b -> p (a b)"), start=True, stop=True)
                ins.then_inc(S["turned"], 1)
                pe.wait_ge(S["xz_ready"], 1)
                pe.sem_inc(S["xz_ready"], -1)
                for n in range(1, 7):
                    pe.wait_ge(S["a4_free"], 1)
                    pe.sem_inc(S["a4_free"], -1)
                    for j in range(4):
                        ins = pe.matmul(A[4][:, j * P:(j + 1) * P], Tm[:, j, :], XZ[:, j, 1, :], start=True, stop=True)
                    ins.then_inc(S["uz_out"], 1)
                    fill(n)
                    pe.wait_ge(S["uz_ready"], 1)
                    pe.sem_inc(S["uz_ready"], -1)
                    for p, b in ((0, 5), (1, 3)):
                        pe.wait_ge(S[f"a{b}_free"], 1)
                        pe.sem_inc(S[f"a{b}_free"], -1)
                        for q in range(2):
                            j = 2 * p + q
                            pe.matmul(A[b][:, q * 256:q * 256 + P], Qs[:, j, :], XZ[:, j, 0, :], start=True, stop=True)
                            ins = pe.matmul(A[b][:, q * 256 + P:q * 256 + 256], XZ[:, j, 0, :], Qs[:, j, :],
                                            start=True, stop=True)
                        ins.then_inc(S["fill_out"], 1)
                    pe.wait_ge(S["xz_ready"], 1)
                    pe.sem_inc(S["xz_ready"], -1)
                pe.wait_ge(S["turned_ready"], 1)
                pe.sem_inc(S["turned_ready"], -1)
                for p in range(2):
                    pe.wait_ge(S[f"a{2 + p}_free"], 1)
                    pe.sem_inc(S[f"a{2 + p}_free"], -1)
                    for j in (p, p + 2):
                        o = A[2 + p][:, 32 * (j - p):32 * (j - p) + 64]
                        pe.matmul(o, UM[:, j, 256:384], TM[:, j // 2, r[j]], start=True, stop=False)
                        ins = pe.matmul(o, AR[r[j], j // 2, 0, :], Sm[r[j], j // 2, :], start=False, stop=True)
                    ins.then_inc(S["rhs_out"], 1)
                pe.wait_ge(S["rhs_ready"], 1)
                pe.sem_inc(S["rhs_ready"], -1)
                pe.wait_ge(S["a0_free"], 1)
                pe.sem_inc(S["a0_free"], -1)
                for j in range(4):
                    ins = pe.matmul(A[0][:, 64 * j:64 * j + 64], XZ[:, j, 1, :], rhs_s[:, 64 * j:64 * j + 64],
                                    start=True, stop=True)
                ins.then_inc(S["sa_out"], 1)
                fill(7)
                pe.wait_ge(S["sa_ready"], 1)
                pe.sem_inc(S["sa_ready"], -1)
                pe.wait_ge(S["a4_free"], 1)
                pe.sem_inc(S["a4_free"], -1)
                for j in range(4):
                    o = A[4][r[j], (j // 2) * P:(j // 2 + 1) * P]
                    pe.matmul(o, sa_s[:, 64 * j:64 * j + 64], UM[:, j, 128:256], start=True, stop=False)
                    pe.matmul(o, TM[:, j // 2, r[j]], UM[:, j, 384:512], start=False, stop=False)
                    ins = pe.matmul(o, Sm[r[j], j // 2, :], AR[r[j], j // 2, 1, :], start=False, stop=True)
                ins.then_inc(S["y_out"], 1)
                pe.wait_ge(S["a5_free"], 1)
                pe.sem_inc(S["a5_free"], -1)
                for j in range(4):
                    o = A[5][r[j], (j // 2) * 64:(j // 2 + 1) * 64]
                    pe.matmul(o, TM[:, 2 + j // 2, r[j]], sa_s[:, 64 * j:64 * j + 64], start=True, stop=False)
                    ins = pe.matmul(o, TM[:, 4 + j // 2, r[j]], TM[:, j // 2, r[j]], start=False, stop=True)
                ins.then_inc(S["state_out"], 1)

            with pe.Fori(0, DEPTH) as layer:
                pe.wait_ge(S["x_ready"], 1)
                pe.sem_inc(S["x_ready"], -1)
                with pe.Fori(0, NW):
                    pe.wait_ge(S["g0_free"], 1)
                    pe.sem_inc(S["g0_free"], -1)
                    proj.channels(g0[:], proj.group(), X, KD, P, done="val_proj")
                    pe.wait_ge(S["g1_free"], 1)
                    pe.sem_inc(S["g1_free"], -1)
                    proj.channels(g1[:], proj.group(), X, KD, P, done="gate_proj")
                gates()
                layer_norm([cacc[:, i, :] for i in range(NW)])
                for i in range(6):
                    pe.wait_ge(S[f"g{i % 2}_free"], 1)
                    pe.sem_inc(S[f"g{i % 2}_free"], -1)
                    proj.channels((g0, g1)[i % 2][:], proj.group(), X, KD, P, done="lat_proj")
                total(A[0][:], [lsq[:, i, :] for i in range(3)], "lat_sq", "lat_sum")
                total(A[1][:], [lsq[:, i, :] for i in (3, 4)], "lat_sq", "lat_sum")
                pe.wait_ge(S["kr_pe"], 1)
                pe.sem_inc(S["kr_pe"], -1)
                pe.matmul(A[4][64:96, :], rotm[64:96, :], kr[64:96, :], start=True, stop=True).then_inc(S["k_rot"], 1)
                gates()
                pe.wait_ge(S["lat_ready"], 1)
                pe.sem_inc(S["lat_ready"], -1)
                with pe.Fori(0, NW):
                    mla_head(0)
                    mla_head(1)
                pe.wait_ge(S["mem_ready"], 1)
                pe.sem_inc(S["mem_ready"], -1)
                with pe.Fori(0, NW):
                    pe.wait_ge(S["g0_free"], 1)
                    pe.sem_inc(S["g0_free"], -1)
                    proj.channels(g0[:], proj.group(), X, KD, P, done="q_proj")
                    pe.wait_ge(S["g1_free"], 1)
                    pe.sem_inc(S["g1_free"], -1)
                    proj.channels(g1[:], proj.group(), X, KD, P, done="gate_proj")
                    pe.wait_ge(S["g0_free"], 1)
                    pe.sem_inc(S["g0_free"], -1)
                    mh, ml = (y[:, 4:8, :].rearrange("p a (b m) -> p (a b) m", m=MEM) for y in (yh, yl))
                    proj.channels(g0[:, 0:MEM], proj.group(), (mh, ml), KD, P, done="k_proj")
                    pe.wait_ge(S["g1_free"], 1)
                    pe.sem_inc(S["g1_free"], -1)
                    h, lo = proj.group()
                    for t in range(2):
                        cs = slice(t * P, (t + 1) * P)
                        proj.product(g1[:, cs], [((mh[:, k, cs], ml[:, k, cs]),
                                                  (h[:, k * P:(k + 1) * P], lo[:, k * P:(k + 1) * P]))
                                                 for k in range(KD)], "v_proj" if t == 1 else None)
                    pe.wait_ge(S["qk_ready"], 1)
                    pe.sem_inc(S["qk_ready"], -1)
                    for b in range(2):
                        pe.wait_ge(S[f"a{b}_free"], 1)
                        pe.sem_inc(S[f"a{b}_free"], -1)
                        for t in (2 * b, 2 * b + 1):
                            ins = pe.matmul(A[b][:, (t % 2) * MEM:(t % 2 + 1) * MEM], Q[:, t * P:(t + 1) * P],
                                            K[:, 0:MEM], start=True, stop=True)
                        ins.then_inc(S["scores"], 1)
                    pe.wait_ge(S["probs_ready"], 1)
                    pe.sem_inc(S["probs_ready"], -1)
                    for i in range(2):
                        pe.wait_ge(S[f"a{2 + i}_free"], 1)
                        pe.sem_inc(S[f"a{2 + i}_free"], -1)
                        for t in range(NT):
                            ins = pe.transpose(A[2 + i][:, t * P:(t + 1) * P], xprobs[:, t, i * P:(i + 1) * P],
                                               ident[:])
                        ins.then_inc(S["probs_turned"], 1)
                    pe.wait_ge(S["v_ready"], 1)
                    pe.sem_inc(S["v_ready"], -1)
                    pe.wait_ge(S["weights_ready"], 1)
                    pe.sem_inc(S["weights_ready"], -1)
                    pe.wait_ge(S["a4_free"], 1)
                    pe.sem_inc(S["a4_free"], -1)
                    for i in range(2):
                        ins = pe.matmul(A[4][:], xV[:, i, :], xPT[:, i, :], start=i == 0, stop=i == 1)
                    ins.then_inc(S["head_out"], 1)
                with pe.Fori(0, 6):
                    for s, g in enumerate((g0, g1)):
                        pe.wait_ge(S[f"g{s}_free"], 1)
                        pe.sem_inc(S[f"g{s}_free"], -1)
                        proj.channels(g[:], proj.group(), X, KD, P, done="rw_proj")
                pe.wait_ge(S["g0_free"], 1)
                pe.sem_inc(S["g0_free"], -1)
                proj.channels(g0[:], proj.group(), X, NW, P, more=True)
                proj.channels(g0[:], proj.group(), X, NW, P, done="rw_proj", k0=NW, first=False)
                pe.wait_ge(S["wa_ready"], 1)
                pe.sem_inc(S["wa_ready"], -1)
                for i in range(NW):
                    pe.wait_ge(S["a0_free"], 1)
                    pe.sem_inc(S["a0_free"], -1)
                    pe.matmul(A[0][:], lora[0:64, i * P:(i + 1) * P], wa[0:64, :], start=True, stop=True)\
                      .then_inc(S["lora_w"], 1)
                    pe.wait_ge(S["a1_free"], 1)
                    pe.sem_inc(S["a1_free"], -1)
                    pe.matmul(A[1][:], lora[64:P, i * P:(i + 1) * P], wa[64:P, :], start=True, stop=True)\
                      .then_inc(S["lora_a"], 1)
                    total(A[2][:], [sq[:, 0, :]], "kk_sq", "kk_sum", halves)
                with pe.Fori(0, NT // 2) as cc:
                    for u in range(2):
                        chunk = cc * 2 + u
                        cs = bass.ds(chunk * P, P)
                        for g in range(2):
                            rwkv_half(g, lambda n: None)
                        for b, slot in ((1, 2), (2, 0), (3, 1)):
                            merge(b, slot, chunk)
                for i in range(NW):
                    total(A[0][:], [R[:, i, :]], "gn_in", "gn_sum", halves)
                    total(A[1][:], [sq[:, 0, :]], "gn_sq", "gn_sumsq", halves)
                gates()
                pe.wait_ge(S["y_ready"], 1)
                pe.sem_inc(S["y_ready"], -1)
                with pe.Fori(0, 2):
                    for u in range(2):
                        merge(0, 0, None)
                pe.wait_ge(S["merged_ready"], 1)
                pe.sem_inc(S["merged_ready"], -1)
                with pe.Fori(0, KD // 2):
                    for s, g in enumerate((g0, g1)):
                        pe.wait_ge(S[f"g{s}_free"], 1)
                        pe.sem_inc(S[f"g{s}_free"], -1)
                        proj.channels(g[:], proj.group(), (yh, yl), KD, P, done="out_proj")
                layer_norm([hT[:, i, :] for i in range(KD)])

        @block.scalar
        def _(act):
            round_next = rounder(act, S, stage, wh)
            half = lambda t, i: t[:, i:i + 1] if isinstance(i, int) else t[:, bass.ds(i, 1)]

            def op(ins, *names):
                fin(act, "act_self", ins, *names)

            def gates(n=2):
                with act.Fori(0, n):
                    for s, g in enumerate((g0, g1)):
                        round_next()
                        act.wait_ge(S["gate_proj"], 1)
                        act.sem_inc(S["gate_proj"], -1)
                        act.wait_ge(S[f"sq{s}_used"], 1)
                        act.sem_inc(S[f"sq{s}_used"], -1)
                        act.activation(sq[:, s, :], g[:], ACT.Tanh, scale=0.5).then_inc(S["tanh_ready"], 1)

            def root(src, n, e):
                act.activation(rstd[:], src, ACT.Sqrt, scale=1.0 / n, bias=eps[:, e:e + 1]).then_inc(S["root"], 1)

            def norm_squares(tiles, n):
                for i, t in enumerate(tiles):
                    act.wait_ge(S["centered"], 1)
                    act.sem_inc(S["centered"], -1)
                    act.wait_ge(S[f"sq{i % 2}_used"], 1)
                    act.sem_inc(S[f"sq{i % 2}_used"], -1)
                    act.activation(sq[:, i % 2, :], t, ACT.Square).then_inc(S[f"sq{i % 2}_ready"], 1)
                act.wait_ge(S["sq0_used"], 1)
                act.sem_inc(S["sq0_used"], -1)
                act.wait_ge(S["sq1_used"], 1)
                act.sem_inc(S["sq1_used"], -1)
                root(A[1][:], n, 0)
                give(act, "sq0_used", "sq1_used")

            def upper(dst, want, src=None, scale=1.0):
                act.wait_ge(S[want], 1)
                act.sem_inc(S[want], -1)
                act.activation(dst, src, ACT.Copy, scale=scale).then_inc(S["hi_ready"], 1)

            def mla_head(a):
                round_next()
                act.wait_ge(S["q_proj"], 1)
                act.sem_inc(S["q_proj"], -1)
                act.wait_ge(S["qk_free"], 1)
                act.sem_inc(S["qk_free"], -1)
                op(act.activation(Q[0:96, :], g0[0:96, :], ACT.Copy, scale=96 ** -0.5), "g0_free", "q_raw", "q_dve")
                act.wait_ge(S["k_proj"], 1)
                act.sem_inc(S["k_proj"], -1)
                op(act.activation(K[0:64, :], g1[0:64, :], ACT.Copy), "g1_free", "k_ready")
                act.wait_ge(S["v_proj"], 1)
                act.sem_inc(S["v_proj"], -1)
                act.wait_ge(S["v_free"], 1)
                act.sem_inc(S["v_free"], -1)
                op(act.activation(V.rearrange("p a b -> p (a b)"), A[5][:, 0:256], ACT.Copy), "a5_free", "v_ready")

                def exponential(t):
                    act.wait_ge(S["max_ready"], 1)
                    act.sem_inc(S["max_ready"], -1)
                    act.activation(probs[:, t % 2, 0:(t + 1) * P], probs[:, t % 2, 0:(t + 1) * P], ACT.Exp,
                                   bias=st[:, t % 2:t % 2 + 1], accum_out=st[:, 2 + t % 2:3 + t % 2])\
                       .then_inc(S["exp_ready"], 1)

                exponential(0)
                for t in range(NT):
                    if t + 1 < NT:
                        exponential(t + 1)
                    n = (t + 1) * P
                    act.wait_ge(S["probs_turned"], 1)
                    act.sem_inc(S["probs_turned"], -1)
                    op(act.activation(PT[:, 0:t + 1, t * P:n], A[4][:, 0:n].rearrange("p (a b) -> p a b", b=P),
                                      ACT.Copy), "a4_free", f"probs{t % 2}_free",
                       *(["weights_ready"] if t == NT - 1 else []))

            def merge(branch, d0):
                for s, g in enumerate((g0, g1)):
                    round_next()
                    act.wait_ge(S["merge_gate"], 1)
                    act.sem_inc(S["merge_gate"], -1)
                    act.wait_ge(S[f"sq{s}_used"], 1)
                    act.sem_inc(S[f"sq{s}_used"], -1)
                    op(act.activation(sq[:, s, :], g[:], ACT.Tanh, scale=0.5,
                                      bias=der[:, bass.ds(d0 + (32 + 8 * branch + s), 1)]), f"g{s}_free",
                       "tanh_ready")
                round_next()

            def rwkv_half(g, cs, fill):
                act.wait_ge(S["qd_ready"], 1)
                act.sem_inc(S["qd_ready"], -1)
                act.activation(emid[:, 0:2], QC[:, :, 64], ACT.Exp, scale=-KAPPA)
                act.activation(EP[:, :, :], QD[:, :, :], ACT.Exp, scale=-KAPPA)
                act.activation(EM[:, :, :], QD[:, :, 1:], ACT.Exp, scale=KAPPA)
                op(act.activation(Vc[:, :, :], RV[:, 2 * g:2 * g + 2, cs], ACT.Copy), "exp_ready")
                fill(0)
                act.wait_ge(S["turned"], 1)
                act.sem_inc(S["turned"], -1)
                op(act.activation(TM[:, 0:4, :].rearrange("p a b -> p (a b)"), A[0][:], ACT.Copy), "a0_free")
                act.wait_ge(S["turned"], 1)
                act.sem_inc(S["turned"], -1)
                op(act.activation(TM[:, 4:6, :].rearrange("p a b -> p (a b)"), A[1][:, 0:256], ACT.Copy),
                   "bonus_sum", "turned_ready")
                for n in range(1, 7):
                    act.wait_ge(S["uz_out"], 1)
                    act.sem_inc(S["uz_out"], -1)
                    op(act.activation(Qs[:, :, :].rearrange("p a b -> p (a b)"), A[4][:], ACT.Copy), "a4_free",
                       "uz_ready")
                    fill(n)
                for p in range(2):
                    act.wait_ge(S["rhs_out"], 1)
                    act.sem_inc(S["rhs_out"], -1)
                    op(act.activation(rhs_s.rearrange("p (a b) -> p a b", b=64)[:, p:4:2, :],
                                      A[2 + p][:, 0:P].rearrange("p (a b) -> p a b", b=64), ACT.Copy),
                       f"a{2 + p}_free", *(["rhs_ready"] if p else []))
                act.wait_ge(S["sa_out"], 1)
                act.sem_inc(S["sa_out"], -1)
                op(act.activation(sa_s, A[0][:, 0:256], ACT.Copy), "a0_free", "sa_ready")
                fill(7)
                act.wait_ge(S["y_out"], 1)
                act.sem_inc(S["y_out"], -1)
                op(act.activation(R[:, 2 * g:2 * g + 2, cs], A[4][:, 0:256].rearrange("p (a b) -> p a b", b=P),
                                  ACT.Copy), "a4_free", "y_written")

            act.dma_start(hT[:], x_dram.rearrange("(k p) t -> p k t", p=P)).then_inc(S["x_in"], 16)
            act.wait_ge(S["x_in"], 16)
            act.sem_inc(S["x_in"], -16)
            give(act, "sq0_used", "sq1_used")
            act.activation(xh[:], hT[:], ACT.Copy).then_inc(S["hi_ready"], 1)
            act.wait_ge(S["consts_act"], 1)
            act.sem_inc(S["consts_act"], -1)
            round_next()
            with act.Fori(0, DEPTH) as layer:
                act.wait_ge(S["par_free"], 1)
                act.sem_inc(S["par_free"], -1)
                act.dma_start(par[:], par_dram[bass.ds(layer, 1)].rearrange("a p n -> p (a n)"))\
                   .then_inc(S["par_full"], 16)
                act.wait_ge(S["par_full"], 16)
                act.sem_inc(S["par_full"], -16)
                give(act, "par_dve")
                act.wait_ge(S["derived"], 1)
                act.sem_inc(S["derived"], -1)
                with act.Fori(0, NW):
                    round_next()
                    round_next()
                    act.wait_ge(S["gate_proj"], 1)
                    act.sem_inc(S["gate_proj"], -1)
                    act.wait_ge(S["sq0_used"], 1)
                    act.sem_inc(S["sq0_used"], -1)
                    act.activation(sq[:, 0, :], g1[:], ACT.Tanh, scale=0.5).then_inc(S["tanh_ready"], 1)
                gates()
                norm_squares([cacc[:, i, :] for i in range(NW)], W)
                for i in range(NW):
                    act.wait_ge(S["scaled"], 1)
                    act.sem_inc(S["scaled"], -1)
                    op(act.activation(cacc[:, i, :], cacc[:, i, :], ACT.Identity, scale=col("cln_g", i),
                                      bias=col("cln_b", i)))
                    act.wait_ge(S[f"sq{i % 2}_used"], 1)
                    act.sem_inc(S[f"sq{i % 2}_used"], -1)
                    act.activation(sq[:, i % 2, :], cacc[:, i, :], ACT.Tanh, scale=0.5)\
                       .then_inc(S["tanh_ready"], 1)
                    upper(yh[:, i, :], "tmp_ready", tmp[:, i % 2, :])
                for i in range(6):
                    g = (g0, g1)[i % 2]
                    round_next()
                    act.wait_ge(S["lat_proj"], 1)
                    act.sem_inc(S["lat_proj"], -1)
                    if i < 5:
                        op(act.activation(lsq[:, i, :], g[:], ACT.Square), *(["lat_sq"] if i in (2, 4) else []))
                    op(act.activation(lat[:, i, :] if i < 5 else kr[:], g[:], ACT.Copy), f"g{i % 2}_free",
                       *(["kr_pe", "kr_dve"] if i == 5 else []))
                act.dma_start(probs[64:96, 0, :].bitcast(I32), bass.AP(pos_dram.tensor, pos_dram.offset, [[0, 32], [1, T]])).then_inc(S["pos_in"], 16)
                act.wait_ge(S["pos_in"], 16)
                act.sem_inc(S["pos_in"], -16)
                give(act, "pos_dve")
                act.wait_ge(S["angle"], 1)
                act.sem_inc(S["angle"], -1)
                op(act.activation(trig[64:96, 1, :], probs[64:96, 0, :], ACT.Sin))
                op(act.activation(trig[64:96, 0, :], probs[64:96, 0, :], ACT.Abs))
                op(act.activation(trig[64:96, 0, :], trig[64:96, 0, :], ACT.Sin, scale=-1.0, bias=eps[64:96, 3:4]),
                   "trig_ready")
                for n, i0, count in ((384, 0, 3), (256, 3, 2)):
                    act.wait_ge(S["lat_sum"], 1)
                    act.sem_inc(S["lat_sum"], -1)
                    root(A[n == 256][:], n, 1)
                    for i in range(i0, i0 + count):
                        upper(yh[:, (4 if i < 3 else 5) + i, :], "tmp_ready", tmp[:, i % 2, :])
                gates()
                act.dma_start(memf, mem_dram.rearrange("(k p) m -> p k m", p=P)).then_inc(S["mem_in"], 16)
                with act.Fori(0, NW):
                    mla_head(0)
                    mla_head(1)
                upper(yh[:, 8:12, :], "y32_ready", y32)
                act.wait_ge(S["mem_in"], 16)
                act.sem_inc(S["mem_in"], -16)
                act.activation(yh[:, 4:8, :].rearrange("p a t -> p (a t)"), memf.rearrange("p a t -> p (a t)"),
                               ACT.Copy).then_inc(S["hi_ready"], 1)
                with act.Fori(0, NW):
                    round_next()
                    act.wait_ge(S["q_proj"], 1)
                    act.sem_inc(S["q_proj"], -1)
                    act.wait_ge(S["qk_free"], 1)
                    act.sem_inc(S["qk_free"], -1)
                    op(act.activation(Q, g0[:], ACT.Copy, scale=128 ** -0.5), "g0_free")
                    round_next()
                    act.wait_ge(S["gate_proj"], 1)
                    act.sem_inc(S["gate_proj"], -1)
                    act.wait_ge(S["sq0_used"], 1)
                    act.sem_inc(S["sq0_used"], -1)
                    act.activation(sq[:, 0, :], g1[:], ACT.Tanh, scale=0.5).then_inc(S["tanh_ready"], 1)
                    round_next()
                    act.wait_ge(S["k_proj"], 1)
                    act.sem_inc(S["k_proj"], -1)
                    op(act.activation(K[:, 0:MEM], g0[:, 0:MEM], ACT.Copy), "g0_free", "qk_ready")
                    round_next()
                    act.wait_ge(S["v_proj"], 1)
                    act.sem_inc(S["v_proj"], -1)
                    act.wait_ge(S["v_free"], 1)
                    act.sem_inc(S["v_free"], -1)
                    op(act.activation(xV[:, :, :].rearrange("p a b -> p (a b)"), g1[:, 0:MEM], ACT.Copy), "g1_free",
                       "v_ready")
                    for b in range(2):
                        act.wait_ge(S["max_ready"], 1)
                        act.sem_inc(S["max_ready"], -1)
                        for t in (2 * b, 2 * b + 1):
                            ins = act.activation(xprobs[:, t, :], A[b][:, (t % 2) * MEM:(t % 2 + 1) * MEM], ACT.Exp,
                                                 bias=st[:, t:t + 1], accum_out=st[:, 4 + t:5 + t])
                        op(ins, f"a{b}_free")
                    give(act, "exp_ready")
                    for i in range(2):
                        act.wait_ge(S["probs_turned"], 1)
                        act.sem_inc(S["probs_turned"], -1)
                        op(act.activation(xPT[:, i, :], A[2 + i][:], ACT.Copy), f"a{2 + i}_free",
                           *(["weights_ready"] if i else []))
                upper(yh[:, 4:8, :], "y32_ready", y32)
                with act.Fori(0, 6) as i:
                    for s, g in enumerate((g0, g1)):
                        round_next()
                        act.wait_ge(S["rw_proj"], 1)
                        act.sem_inc(S["rw_proj"], -1)
                        op(act.activation(tile(RKV, i * 2 + s), g[:], ACT.Copy, scale=half(der, i * 2 + s)),
                           "part_ready")
                round_next()
                round_next()
                act.wait_ge(S["rw_proj"], 1)
                act.sem_inc(S["rw_proj"], -1)
                op(act.activation(wa, g0[:], ACT.Copy, scale=der[:, 12:13]), "part_ready")
                act.dma_start(lora, lora_dram[bass.ds(layer, 1)].rearrange("a p n -> p (a n)"))\
                   .then_inc(S["lora_in"], 16)
                act.wait_ge(S["lora_in"], 16)
                act.sem_inc(S["lora_in"], -16)
                act.wait_ge(S["wa_mixed"], 1)
                act.sem_inc(S["wa_mixed"], -1)
                op(act.activation(wa[0:64, :], wa[0:64, :], ACT.Tanh), "wa_ready")
                for i in range(NW):
                    act.wait_ge(S["lora_w"], 1)
                    act.sem_inc(S["lora_w"], -1)
                    op(act.activation(TH[:, i, :], A[0][:], ACT.Tanh, scale=0.5, bias=der[:, 13 + i:14 + i]),
                       "a0_free")
                    act.wait_ge(S["lora_a"], 1)
                    act.sem_inc(S["lora_a"], -1)
                    op(act.activation(BB[:, i, :], A[1][:], ACT.Tanh, scale=0.5, bias=der[:, 17 + i:18 + i]),
                       "a1_free", "a_ready")
                    act.wait_ge(S["kk_ready"], 1)
                    act.sem_inc(S["kk_ready"], -1)
                    act.wait_ge(S["sq0_used"], 1)
                    act.sem_inc(S["sq0_used"], -1)
                    act.activation(sq[:, 0, :], KK[:, i, :], ACT.Square).then_inc(S["kk_sq"], 1)
                    act.wait_ge(S["kk_sum"], 1)
                    act.sem_inc(S["kk_sum"], -1)
                    act.activation(rstd[:], A[2][:], ACT.Sqrt).then_inc(S["root"], 1)
                    give(act, "sq0_used")
                with act.Fori(0, NT // 2) as cc:
                    for u in range(2):
                        chunk = cc * 2 + u
                        for g in range(2):
                            rwkv_half(g, bass.ds(chunk * P, P), lambda n: None)
                        for b in (1, 2, 3):
                            merge(b, chunk * 2)
                for i in range(NW):
                    act.wait_ge(S["centered"], 1)
                    act.sem_inc(S["centered"], -1)
                    act.wait_ge(S["sq0_used"], 1)
                    act.sem_inc(S["sq0_used"], -1)
                    act.activation(sq[:, 0, :], R[:, i, :], ACT.Square).then_inc(S["gn_sq"], 1)
                    act.wait_ge(S["gn_sumsq"], 1)
                    act.sem_inc(S["gn_sumsq"], -1)
                    root(A[1][:], 64, 2)
                    give(act, "sq0_used")
                    act.wait_ge(S["scaled"], 1)
                    act.sem_inc(S["scaled"], -1)
                    act.activation(R[:, i, :], R[:, i, :], ACT.Identity, scale=col("lnx_g", i),
                                   bias=col("lnx_b", i)).then_inc(S["affine"], 1)
                gates()
                upper(yh[:, 0:4, :], "y32_ready", R)
                with act.Fori(0, 2) as i:
                    for u in range(2):
                        merge(0, i * 4 + 2 * u)
                upper(yh[:, 0:8, :], "y32_ready", hT[:], 0.5)
                with act.Fori(0, KD // 2):
                    round_next()
                    round_next()
                norm_squares([hT[:, i, :] for i in range(KD)], D)
                for i in range(KD):
                    act.wait_ge(S["scaled"], 1)
                    act.sem_inc(S["scaled"], -1)
                    op(act.activation(hT[:, i, :], hT[:, i, :], ACT.Identity, scale=col("ln_g", i),
                                      bias=col("ln_b", i)))
                    act.activation(xh[:, i, :], hT[:, i, :], ACT.Copy).then_inc(S["hi_ready"], 1)

        @block.vector
        def _(dve):
            def op(ins, *names):
                fin(dve, "dve_self", ins, *names)

            def stt(out, in0, scalar, in1, op0, op1, *names):
                op(dve.scalar_tensor_tensor(out=out, in0=in0, scalar=scalar, in1=in1, op0=op0, op1=op1), *names)

            def tt(out, a, b, alu, *names):
                op(dve.tensor_tensor(out, a, b, alu), *names)

            def ts(out, a, s1, s2, op0, op1, *names):
                op(dve.tensor_scalar(out, a, s1, s2, op0, op1) if s2 is not None
                   else dve.tensor_scalar(out, a, s1, None, op0), *names)

            def spread(v, n):
                return bass.AP(v.tensor, v.offset, [*v.ap, [0, n]])

            def again(v, n):
                return bass.AP(v.tensor, v.offset, [v.ap[0], [0, n], *v.ap[1:]])

            def gates(dst):
                with dve.Fori(0, NW // 2) as i:
                    for s, g in enumerate((g0, g1)):
                        dve.wait_ge(S["tanh_ready"], 1)
                        dve.sem_inc(S["tanh_ready"], -1)
                        stt(tile(dst, i * 2 + s), sq[:, s, :], 1.0, g[:], ALU.add, ALU.mult, f"g{s}_free",
                            f"sq{s}_used")

            def lower(h, lo, src, *names, scale=None):
                dve.wait_ge(S["hi_ready"], 1)
                dve.sem_inc(S["hi_ready"], -1)
                if scale is None:
                    tt(lo, src, h.bitcast(F32), ALU.subtract, *names)
                else:
                    stt(lo, src, scale, h.bitcast(F32), ALU.mult, ALU.subtract, *names)

            def layer_norm(tiles, n):
                give(dve, "ln_in")
                dve.wait_ge(S["ln_sum"], 1)
                dve.sem_inc(S["ln_sum"], -1)
                for t in tiles:
                    stt(t, A[0][:], -1.0 / n, t, ALU.mult, ALU.add, "centered")
                dve.wait_ge(S["root"], 1)
                dve.sem_inc(S["root"], -1)
                op(dve.reciprocal(rstd[:], rstd[:]))
                for t in tiles:
                    tt(t, t, rstd[:], ALU.mult, "scaled")

            def mla_head(a, i):
                rows = slice(64 * a, 64 * a + 64)
                dve.wait_ge(S["q_dve"], 1)
                dve.sem_inc(S["q_dve"], -1)
                dve.wait_ge(S["q_rot"], 1)
                dve.sem_inc(S["q_rot"], -1)
                tt(tmp[64:96, 1, :], Q[64:96, :], trig[64:96, 0, :], ALU.mult)
                tt(tmp[64:96, 0, :], A[4][64:96, :], trig[64:96, 1, :], ALU.mult, "a4_free")
                tt(Q[64:96, :], tmp[64:96, 1, :], tmp[64:96, 0, :], ALU.add, "qk_ready")

                def maximum(t):
                    n = (t + 1) * P
                    dve.wait_ge(S["scores"], 1)
                    dve.sem_inc(S["scores"], -1)
                    dve.wait_ge(S[f"probs{t % 2}_free"], 1)
                    dve.sem_inc(S[f"probs{t % 2}_free"], -1)
                    op(dve.tensor_tensor_reduce(probs[:, t % 2, 0:n], A[t % 2][:, 0:n], causal[:, T - n:T], 1.0,
                                                -3e38, ALU.add, ALU.max, st[:, 4 + t % 2:5 + t % 2]),
                       f"a{t % 2}_free", *(["qk_free"] if t == NT - 1 else []))
                    ts(st[:, t % 2:t % 2 + 1], st[:, 4 + t % 2:5 + t % 2], -1.0, None, ALU.mult, None, "max_ready")

                maximum(0)
                for t in range(NT):
                    if t + 1 < NT:
                        maximum(t + 1)
                    n = (t + 1) * P
                    dve.wait_ge(S["exp_ready"], 1)
                    dve.sem_inc(S["exp_ready"], -1)
                    op(dve.reciprocal(st[:, 6:7], st[:, 2 + t % 2:3 + t % 2]))
                    ts(probs[:, t % 2, 0:n], probs[:, t % 2, 0:n], st[:, 6:7], None, ALU.mult, None, "probs_ready")
                dve.wait_ge(S["head_out"], 1)
                dve.sem_inc(S["head_out"], -1)
                stt(y32[rows, bass.ds(i, 1), :].rearrange("p a t -> p (a t)"), A[5][rows, :], 0.5,
                    mgate[rows, bass.ds(i, 1), :].rearrange("p a t -> p (a t)"), ALU.mult, ALU.mult, "a5_free",
                    "v_free")

            def merge(d0, first=False):
                for s, g in enumerate((g0, g1)):
                    dve.wait_ge(S["tanh_ready"], 1)
                    dve.sem_inc(S["tanh_ready"], -1)
                    dve.wait_ge(S["merge_proj"], 1)
                    dve.sem_inc(S["merge_proj"], -1)
                    h = tile(hT, d0 + s)
                    if first:
                        stt(h, sq[:, s, :], 1.0, g[:], ALU.add, ALU.mult, f"g{s}_free", f"sq{s}_used")
                    else:
                        stt(sq[:, s, :], sq[:, s, :], 1.0, g[:], ALU.add, ALU.mult, f"g{s}_free")
                        tt(h, h, sq[:, s, :], ALU.add, f"sq{s}_used")

            def rwkv_half(g, cs, fill):
                two = slice(2 * g, 2 * g + 2)
                for i in range(2):
                    op(dve.tensor_tensor_scan(QC[:, i, 1:], TH[:, 2 * g + i, cs], ones[:], 0.0, ALU.add, ALU.add))
                mid = QC[:, :, 64]
                tt(QD[:, :, :], QC[:, :, :], spread(mid, P + 1), ALU.subtract, "qd_ready")
                dve.wait_ge(S["exp_ready"], 1)
                dve.sem_inc(S["exp_ready"], -1)
                for i in range(2):
                    ts(Sm[:, i, :], St[:, 2 * g + i, :], emid[:, i:i + 1], None, ALU.mult, None)
                stt(AR[:, :, 0, :], KK[:, two, cs], -1.0, EP[:, :, 0:P], ALU.mult, ALU.mult)
                tt(AR[:, :, 1, :], R[:, two, cs], EP[:, :, 1:], ALU.mult)
                stt(Bt[:, :, :], BB[:, two, cs], 0.5, EM[:, :, :], ALU.mult, ALU.mult)
                tt(Kt[:, :, :], RK_[:, two, cs], EM[:, :, :], ALU.mult)
                tt(rkc, R[:, two, cs], RK_[:, two, cs], ALU.mult)
                tt(rkc, rkc, spread(col("r_k", 2 * g, 2), P), ALU.mult, "ab_ready")
                a2 = after[:, :, :].rearrange("p a b -> p (a b)")
                for j in range(4):
                    dve.wait_ge(S["um_out"], 1)
                    dve.sem_inc(S["um_out"], -1)
                    tt(UM[:, j, :].rearrange("p (a b) -> p a b", a=2), A[j][:].rearrange("p (a b) -> p a b", a=2),
                       again(a2, 2), ALU.mult, f"a{j}_free")
                for p in range(2):
                    dve.wait_ge(S["t_out"], 1)
                    dve.sem_inc(S["t_out"], -1)
                    tt(Tm[:, p:4:2, :], A[4 + p][:, 0:256].rearrange("p (a b) -> p a b", a=2), again(before[:], 2),
                       ALU.mult, f"a{4 + p}_free")
                op(dve.tensor_copy(XZ[:, :, :, :].rearrange("p a b c -> p (a b) c"), again(ident[:], 8)))
                op(dve.copy_predicated(XZ[:, :, 0, :], again(level[:, 0, 0, :], 4), Tm[:, :, :]))
                op(dve.copy_predicated(XZ[:, :, 1, :], again(level[:, 0, 1, :], 4), UM[:, :, 0:P]), "xz_ready")
                fill(0)
                dve.wait_ge(S["bonus_sum"], 1)
                dve.sem_inc(S["bonus_sum"], -1)
                tt(RK_[:, two, cs], A[1][:, 256:512].rearrange("p (a b) -> p a b", a=2), Vc[:, :, :], ALU.mult,
                   "a1_free")
                for n in range(1, 7):
                    m = level[:, n, :, :].rearrange("p a b -> p (a b)")
                    for p, b in ((0, 5), (1, 3)):
                        dve.wait_ge(S["fill_out"], 1)
                        dve.sem_inc(S["fill_out"], -1)
                        op(dve.copy_predicated(XZ[:, 2 * p:2 * p + 2, :, :].rearrange("p a b c -> p a (b c)"),
                                               again(m, 2), A[b][:].rearrange("p (a b) -> p a b", a=2)),
                           f"a{b}_free", *(["xz_ready"] if p else []))
                    fill(n)
                fill(7)
                dve.wait_ge(S["y_written"], 1)
                dve.sem_inc(S["y_written"], -1)
                dve.wait_ge(S["state_out"], 1)
                dve.sem_inc(S["state_out"], -1)
                tt(Sm[:, :, :], A[5][:, 0:P].rearrange("p (a b) -> p a b", b=64), Sm[:, :, :], ALU.add, "a5_free")
                for i in range(2):
                    ts(St[:, 2 * g + i, :], Sm[:, i, :], EP[:, i, P:P + 1], None, ALU.mult, None)

            for n, v in enumerate((1e-5, 1e-6, 64e-5, math.pi / 2)):
                op(dve.memset(eps[:, n:n + 1], v))
            lower(xh[:], xl[:], hT[:], "x_ready")
            dve.wait_ge(S["consts_dve"], 1)
            dve.sem_inc(S["consts_dve"], -1)
            give(dve, "g0_free", "g1_free", "par_free", "qk_free", "v_free", "probs0_free", "probs1_free",
                 *(f"a{i}_free" for i in range(6)))
            with dve.Fori(0, DEPTH) as layer:
                dve.wait_ge(S["par_dve"], 1)
                dve.sem_inc(S["par_dve"], -1)
                ts(der[:, 0:13], col("mu", 0, 13), -1.0, 1.0, ALU.mult, ALU.add)
                ts(der[:, 13:17], col("w0", 0, 4), 0.5, None, ALU.mult, None)
                ts(der[:, 17:21], col("a0", 0, 4), 0.5, None, ALU.mult, None)
                ts(der[:, 21:25], col("k_a", 0, 4), 0.5, None, ALU.mult, None)
                ts(der[:, 25:29], col("k_a", 0, 4), -0.5, 1.0, ALU.mult, ALU.add)
                ts(der[:, 32:64], col("b_gate", 0, 32), 0.5, None, ALU.mult, None, "derived")
                op(dve.memset(hb[:, :, 0:TAPS - 1], 0.0))
                with dve.Fori(0, NW) as i:
                    dve.wait_ge(S["val_proj"], 1)
                    dve.sem_inc(S["val_proj"], -1)
                    dve.wait_ge(S["tanh_ready"], 1)
                    dve.sem_inc(S["tanh_ready"], -1)
                    stt(hb[:, bass.ds(i, 1), TAPS - 1:TAPS - 1 + T].rearrange("p a t -> p (a t)"), sq[:, 0, :], 1.0,
                        g0[:], ALU.add, ALU.mult, "g0_free", "g1_free", "sq0_used")
                gates(cgate)
                with dve.Fori(0, NW // 2) as i:
                    for k in range(TAPS):
                        for s in range(2):
                            src = hb[:, bass.ds(i * 2 + s, 1), k:k + T].rearrange("p a t -> p (a t)")
                            w = col("conv_w", (i * 2 + s) * TAPS + k)
                            dst = tile(cacc, i * 2 + s)
                            if k == 0:
                                dve.tensor_scalar(dst, src, w, None, ALU.mult).then_inc(S["tap"], 1)
                            else:
                                dve.wait_ge(S["tap"], 1)
                                dve.sem_inc(S["tap"], -1)
                                dve.scalar_tensor_tensor(out=dst, in0=src, scalar=w, in1=dst, op0=ALU.mult,
                                                         op1=ALU.add).then_inc(S["tap"], 1)
                    dve.wait_ge(S["tap"], 2)
                    dve.sem_inc(S["tap"], -2)
                    for s in range(2):
                        dst = tile(cacc, i * 2 + s)
                        ts(dst, dst, 0.5, col("conv_b", i * 2 + s), ALU.mult, ALU.add)
                layer_norm([cacc[:, i, :] for i in range(NW)], W)
                for i in range(NW):
                    t = tmp[:, i % 2, :]
                    dve.wait_ge(S["tanh_ready"], 1)
                    dve.sem_inc(S["tanh_ready"], -1)
                    stt(t, sq[:, i % 2, :], 1.0, cacc[:, i, :], ALU.add, ALU.mult, f"sq{i % 2}_used")
                    stt(t, t, 0.25, cgate[:, i, :], ALU.mult, ALU.mult, "tmp_ready")
                    lower(yh[:, i, :], yl[:, i, :], t)
                dve.wait_ge(S["pos_dve"], 1)
                dve.sem_inc(S["pos_dve"], -1)
                ang, red = probs[64:96, 0, :], trig[64:96, 1, :]
                op(dve.tensor_copy(red, ang.bitcast(I32)))
                ts(ang, red, par[64:96, PC1["inv_freq"][0]:PC1["inv_freq"][0] + 1], None, ALU.mult, None)
                magic, part1, part2 = 1.5 * 2 ** 23, 6.28125, 8117 / 2 ** 22
                ts(red, ang, 1 / (2 * math.pi), magic, ALU.mult, ALU.add)
                ts(red, red, -magic, None, ALU.add, None)
                for part in (part1, part2, 2 * math.pi - part1 - part2):
                    stt(ang, red, -part, ang, ALU.mult, ALU.add)
                ts(ang, ang, 3.1415925, -3.1415925, ALU.min, ALU.max, "angle")
                for i0, count, gain in ((0, 3, "q_norm"), (3, 2, "kv_norm")):
                    dve.wait_ge(S["root"], 1)
                    dve.sem_inc(S["root"], -1)
                    op(dve.reciprocal(rstd[:], rstd[:]))
                    for i in range(i0, i0 + count):
                        t, y = tmp[:, i % 2, :], (4 if i < 3 else 5) + i
                        stt(t, lat[:, i, :], col(gain, i - i0), rstd[:], ALU.mult, ALU.mult, "tmp_ready")
                        lower(yh[:, y, :], yl[:, y, :], t)
                dve.wait_ge(S["trig_ready"], 1)
                dve.sem_inc(S["trig_ready"], -1)
                dve.wait_ge(S["kr_dve"], 1)
                dve.sem_inc(S["kr_dve"], -1)
                dve.wait_ge(S["k_rot"], 1)
                dve.sem_inc(S["k_rot"], -1)
                tt(tmp[64:96, 1, :], kr[64:96, :], trig[64:96, 0, :], ALU.mult)
                tt(tmp[64:96, 0, :], A[4][64:96, :], trig[64:96, 1, :], ALU.mult)
                tt(K[64:96, :], tmp[64:96, 1, :], tmp[64:96, 0, :], ALU.add, "lat_ready")
                op(dve.memset(causal[:, 0:T - P], 0.0))
                op(dve.tensor_copy(causal[:, T - P:T], future[:]))
                gates(mgate)
                with dve.Fori(0, NW) as i:
                    mla_head(0, i)
                    mla_head(1, i)
                give(dve, "y32_ready")
                lower(yh[:, 8:12, :], yl[:, 8:12, :], y32)
                dve.wait_ge(S["hi_ready"], 1)
                dve.sem_inc(S["hi_ready"], -1)
                op(dve.tensor_tensor(yl[:, 4:8, :].rearrange("p a t -> p (a t)"),
                                     memf.rearrange("p a t -> p (a t)"),
                                     yh[:, 4:8, :].rearrange("p a t -> p (a t)").bitcast(F32), ALU.subtract),
                   "mem_ready")
                with dve.Fori(0, NW) as i:
                    dve.wait_ge(S["tanh_ready"], 1)
                    dve.sem_inc(S["tanh_ready"], -1)
                    stt(gate, sq[:, 0, :], 1.0, g1[:], ALU.add, ALU.mult, "g1_free", "sq0_used")
                    for b in range(2):
                        dve.wait_ge(S["scores"], 1)
                        dve.sem_inc(S["scores"], -1)
                        op(dve.tensor_reduce(st[:, 8 + 2 * b:10 + 2 * b], A[b][:].rearrange("p (a m) -> p a m", a=2),
                                             AX, ALU.max))
                        ts(st[:, 2 * b:2 * b + 2], st[:, 8 + 2 * b:10 + 2 * b], -1.0, None, ALU.mult, None,
                           "max_ready")
                    dve.wait_ge(S["exp_ready"], 1)
                    dve.sem_inc(S["exp_ready"], -1)
                    op(dve.reciprocal(st[:, 12:16], st[:, 4:8]))
                    tt(xprobs[:, :, :], xprobs[:, :, :], spread(st[:, 12:16], MEM), ALU.mult, "probs_ready")
                    dve.wait_ge(S["head_out"], 1)
                    dve.sem_inc(S["head_out"], -1)
                    stt(tile(y32, i), A[4][:], 0.5, gate, ALU.mult, ALU.mult, "a4_free", "qk_free", "v_free")
                give(dve, "y32_ready")
                lower(yh[:, 4:8, :], yl[:, 4:8, :], y32)
                with dve.Fori(0, 6) as i:
                    for s, g in enumerate((g0, g1)):
                        dve.wait_ge(S["part_ready"], 1)
                        dve.sem_inc(S["part_ready"], -1)
                        t = RKV[:, bass.ds(i * 2 + s, 1), 1:T].rearrange("p a t -> p (a t)")
                        stt(t, g[:, 0:T - 1], col("mu", i * 2 + s), t, ALU.mult, ALU.add, f"g{s}_free")
                dve.wait_ge(S["part_ready"], 1)
                dve.sem_inc(S["part_ready"], -1)
                stt(wa[:, 1:T], g0[:, 0:T - 1], col("mu", 12), wa[:, 1:T], ALU.mult, ALU.add, "g0_free", "wa_mixed")
                for i in range(NW):
                    ts(KK[:, i, :], RK_[:, i, :], col("k_k", i), None, ALU.mult, None, "kk_ready")
                    dve.wait_ge(S["a_ready"], 1)
                    dve.sem_inc(S["a_ready"], -1)
                    ts(tmp[:, 0, :], BB[:, i, :], der[:, 21 + i:22 + i], der[:, 25 + i:26 + i], ALU.mult, ALU.add)
                    tt(RK_[:, i, :], RK_[:, i, :], tmp[:, 0, :], ALU.mult)
                    dve.wait_ge(S["root"], 1)
                    dve.sem_inc(S["root"], -1)
                    ts(rstd[:], rstd[:], 1e-12, None, ALU.max, None)
                    op(dve.reciprocal(rstd[:], rstd[:]))
                    tt(KK[:, i, :], KK[:, i, :], rstd[:], ALU.mult)
                    stt(BB[:, i, :], BB[:, i, :], 1.0, KK[:, i, :], ALU.add, ALU.mult, "a2_free")
                op(dve.memset(St[:, :, :], 0.0))
                op(dve.memset(QC[:, :, 0:1], 0.0))
                with dve.Fori(0, NT // 2) as cc:
                    for u in range(2):
                        chunk = cc * 2 + u
                        for g in range(2):
                            rwkv_half(g, bass.ds(chunk * P, P), lambda n: None)
                        for b in (1, 2, 3):
                            merge(chunk * 2, b == 1)
                for i in range(NW):
                    give(dve, "gn_in")
                    dve.wait_ge(S["gn_sum"], 1)
                    dve.sem_inc(S["gn_sum"], -1)
                    stt(R[:, i, :], A[0][:], -1.0 / 64, R[:, i, :], ALU.mult, ALU.add, "centered")
                    dve.wait_ge(S["root"], 1)
                    dve.sem_inc(S["root"], -1)
                    op(dve.reciprocal(rstd[:], rstd[:]))
                    tt(R[:, i, :], R[:, i, :], rstd[:], ALU.mult, "scaled")
                    dve.wait_ge(S["affine"], 1)
                    dve.sem_inc(S["affine"], -1)
                    tt(R[:, i, :], R[:, i, :], RK_[:, i, :], ALU.add)
                gates(rgate)
                stt(R, R, 0.5, rgate[:, :, :], ALU.mult, ALU.mult, "y32_ready")
                lower(yh[:, 0:4, :], yl[:, 0:4, :], R, "y_ready")
                with dve.Fori(0, 2) as i:
                    for u in range(2):
                        merge(i * 4 + 2 * u)
                give(dve, "y32_ready")
                lower(yh[:, 0:8, :], yl[:, 0:8, :], hT[:], "merged_ready", scale=0.5)
                with dve.Fori(0, KD // 2) as m:
                    for s, g in enumerate((g0, g1)):
                        dve.wait_ge(S["out_proj"], 1)
                        dve.sem_inc(S["out_proj"], -1)
                        h = tile(hT, m * 2 + s)
                        stt(h, tile(xh, m * 2 + s).bitcast(F32), ALPHA, g[:], ALU.mult, ALU.add, f"g{s}_free")
                        stt(h, tile(xl, m * 2 + s).bitcast(F32), ALPHA, h, ALU.mult, ALU.add)
                layer_norm([hT[:, i, :] for i in range(KD)], D)
                for i in range(KD):
                    lower(xh[:, i, :], xl[:, i, :], hT[:, i, :])
                give(dve, "x_ready", "par_free")


def second_block(nc, S, par_dram, stream, out, hT):
    give, fin = helpers(S)
    with ExitStack() as ctx:
        def sb(name, shape, dt=F32):
            return ctx.enter_context(nc.sbuf_tensor(name + "_2", shape, dt))

        bank = [ctx.enter_context(nc.psum_tensor(f"bank{i}_2", [P, 512], F32)) for i in range(8)]
        g0, g1 = bank[0], bank[1]
        A = bank[2:]
        stage = sb("stage", [P, STAGE_SLOTS, GW])
        wh = sb("wh", [P, SPLIT_SLOTS, GW], F32R)
        wl = sb("wl", [P, SPLIT_SLOTS, GW], F32R)
        uh = sb("uh", [P, KD, T], F32R)
        ul = sb("ul", [P, KD, T], F32R)
        hidh = sb("hidh", [P, NF, T], F32R)
        hidl = sb("hidl", [P, NF, T], F32R)
        par = sb("par", [P, NP2])
        der = sb("der", [P, 16])
        ones = sb("ones", [P, P])
        ident = sb("ident", [P, P])
        near = sb("near", [P, T])
        ago = sb("ago", [P, T])
        tmp = sb("tmp", [P, 2, T])
        sq = sb("sq", [P, 2, T])
        rstd = sb("rstd", [P, T])
        gam = sb("gam", [P, T])
        Q = sb("Q", [P, T])
        K = sb("K", [P, T])
        V = sb("V", [P, NT, P])
        gate = sb("gate", [P, T])
        PT = sb("PT", [P, NT, T])
        pr = sb("pr", [P, 2, T])
        st = sb("st", [P, 8])

        def col(name, i=0, n=1):
            a = PC2[name][0]
            return par[:, a + i:a + i + n] if isinstance(i, int) else par[:, bass.ds(i + a, n)]

        block = ctx.enter_context(nc.Block())

        @block.sync
        def _(sp):
            weight_loader(sp, S, stage, stream, DEPTH * G2)
            sp.wait_ge(S["out_ready"], 1)
            sp.sem_inc(S["out_ready"], -1)
            sp.dma_start(out.rearrange("(k p) t -> p k t", p=P), hT[:]).then_inc(S["out_done"], 16)
            sp.wait_ge(S["out_done"], 16)
            sp.sem_inc(S["out_done"], -16)

        @block.gpsimd
        def _(pool):
            fin(pool, "pool_self", pool.memset(ones[:], 1.0))
            fin(pool, "pool_self", pool.memset(ident[:], 0.0))
            fin(pool, "pool_self", pool.affine_select(out=ident[:], in_=ident[:], compare_op=ALU.not_equal,
                                                      fill=1.0, base=0, pattern=[[-1, P]], channel_multiplier=1))
            fin(pool, "pool_self", pool.iota(near[:], [[1, T]], base=P - T, channel_multiplier=-1,
                                             allow_small_or_imprecise_dtypes=True))
            fin(pool, "pool_self", pool.affine_select(out=near[:], in_=near[:], compare_op=ALU.is_ge, fill=MASKED,
                                                      base=T - P, pattern=[[-1, T]], channel_multiplier=1))
            fin(pool, "pool_self", pool.iota(ago[:], [[-1, T]], base=0, channel_multiplier=1,
                                             allow_small_or_imprecise_dtypes=True))
            fin(pool, "pool_self", pool.affine_select(out=ago[:], in_=ago[:], compare_op=ALU.is_ge, fill=MASKED,
                                                      base=0, pattern=[[1, T]], channel_multiplier=-1),
                "consts_pe", "consts_act", "consts_dve")
            weight_remainders(pool, S, give, fin, stage, wh, wl, DEPTH * G2)

        @block.tensor
        def _(pe):
            pe.wait_ge(S["consts_pe"], 1)
            pe.sem_inc(S["consts_pe"], -1)
            proj = Projector(pe, S, wh, wl)

            def norm_sum():
                for i in range(KD):
                    pe.wait_ge(S[f"sq{i % 2}_ready"], 1)
                    pe.sem_inc(S[f"sq{i % 2}_ready"], -1)
                    pe.matmul(A[0][:], ones[:], sq[:, i % 2, :], start=i == 0, stop=i == KD - 1)\
                      .then_inc(S[f"sq{i % 2}_used"], 1)

            def values(out_bank):
                h, lo = proj.group()
                for t in range(NT):
                    c = slice(t * P, (t + 1) * P)
                    proj.product(out_bank[:, c], [((uh[:, k, c], ul[:, k, c]),
                                                   (h[:, k * P:(k + 1) * P], lo[:, k * P:(k + 1) * P]))
                                                  for k in range(KD)], "v_proj" if t == NT - 1 else None)

            def head_norm():
                pe.wait_ge(S["head_sq_ready"], 1)
                pe.sem_inc(S["head_sq_ready"], -1)
                pe.matmul(A[5][:], ones[:], sq[:, 0, :], start=True, stop=True).then_inc(S["head_sumsq"], 1)

            def weighted_values():
                pe.wait_ge(S["head_out_free"], 1)
                pe.sem_inc(S["head_out_free"], -1)
                for i in range(NT):
                    n = pe.matmul(A[4][:, i * P:T], V[:, i, :], PT[:, i, i * P:T], start=i == 0, stop=i == NT - 1)
                n.then_inc(S["head_out"], 1)

            with pe.Fori(0, DEPTH) as layer:
                pe.wait_ge(S["lam_prod"], 1)
                pe.sem_inc(S["lam_prod"], -1)
                pe.matmul(A[1][:, 0:2], ones[0:64, :], der[0:64, 8:10], start=True, stop=True)\
                  .then_inc(S["lam_sums"], 1)
                norm_sum()
                pe.wait_ge(S["u_ready"], 1)
                pe.sem_inc(S["u_ready"], -1)
                with pe.Fori(0, 2) as pair:
                    pe.wait_ge(S["g0_free"], 1)
                    pe.sem_inc(S["g0_free"], -1)
                    proj.channels(g0[:], proj.group(), (uh, ul), KD, P, done="q_proj")
                    pe.wait_ge(S["g1_free"], 1)
                    pe.sem_inc(S["g1_free"], -1)
                    proj.channels(g1[:], proj.group(), (uh, ul), KD, P, done="k_proj")
                    for a in range(2):
                        r = slice(64 * a, 64 * a + 64)
                        pe.wait_ge(S["g0_free"], 1)
                        pe.sem_inc(S["g0_free"], -1)
                        values(g0)
                        pe.wait_ge(S["g1_free"], 1)
                        pe.sem_inc(S["g1_free"], -1)
                        proj.channels(g1[:], proj.group(), (uh, ul), KD, P, done="gate_proj")
                        if a == 0:
                            pe.wait_ge(S["qk_ready"], 1)
                            pe.sem_inc(S["qk_ready"], -1)
                        for i in range(NT):
                            pe.wait_ge(S[f"a{i}_free"], 1)
                            pe.sem_inc(S[f"a{i}_free"], -1)
                            pe.matmul(A[i][:, i * P:T], K[r, i * P:(i + 1) * P], Q[r, i * P:T], start=True,
                                      stop=True).then_inc(S["scores"], 1)
                        pe.wait_ge(S["v_ready"], 1)
                        pe.sem_inc(S["v_ready"], -1)
                        pe.wait_ge(S["weights_ready"], 1)
                        pe.sem_inc(S["weights_ready"], -1)
                        weighted_values()
                        head_norm()
                with pe.Fori(0, 2) as pair:
                    for a in range(2):
                        pe.wait_ge(S["g0_free"], 1)
                        pe.sem_inc(S["g0_free"], -1)
                        proj.channels(g0[:], proj.group(), (uh, ul), KD, P, done="q_proj")
                        pe.wait_ge(S["g1_free"], 1)
                        pe.sem_inc(S["g1_free"], -1)
                        proj.channels(g1[:], proj.group(), (uh, ul), KD, P, done="k_proj")
                        pe.wait_ge(S["g0_free"], 1)
                        pe.sem_inc(S["g0_free"], -1)
                        values(g0)
                        pe.wait_ge(S["qk_ready"], 1)
                        pe.sem_inc(S["qk_ready"], -1)

                        def scores(t):
                            n = (t + 1) * P
                            for j in range(2):
                                b = 2 * (t % 2) + j
                                pe.wait_ge(S[f"a{b}_free"], 1)
                                pe.sem_inc(S[f"a{b}_free"], -1)
                                pe.matmul(A[b][:, 0:n], Q[64 * j:64 * j + 64, t * P:n], K[64 * j:64 * j + 64, 0:n],
                                          start=True, stop=True).then_inc(S["scores"], 1)

                        scores(0)
                        for t in range(NT):
                            if t + 1 < NT:
                                scores(t + 1)
                            pe.wait_ge(S["probs_ready"], 1)
                            pe.sem_inc(S["probs_ready"], -1)
                            pe.wait_ge(S["a5_free"], 1)
                            pe.sem_inc(S["a5_free"], -1)
                            for i in range(t + 1):
                                n = pe.transpose(A[5][:, i * P:(i + 1) * P], pr[:, 0, i * P:(i + 1) * P], ident[:])
                            n.then_inc(S["probs_turned"], 1)
                        pe.wait_ge(S["v_ready"], 1)
                        pe.sem_inc(S["v_ready"], -1)
                        pe.wait_ge(S["weights_ready"], 1)
                        pe.sem_inc(S["weights_ready"], -1)
                        weighted_values()
                        pe.wait_ge(S["a5_free"], 1)
                        pe.sem_inc(S["a5_free"], -1)
                        head_norm()
                pe.wait_ge(S["mix_ready"], 1)
                pe.sem_inc(S["mix_ready"], -1)
                with pe.Fori(0, KD // 2) as m:
                    for s, g in enumerate((g0, g1)):
                        pe.wait_ge(S[f"g{s}_free"], 1)
                        pe.sem_inc(S[f"g{s}_free"], -1)
                        proj.channels(g[:], proj.group(), (hidh, hidl), KD, P, done="out_proj")
                norm_sum()
                pe.wait_ge(S["u_ready"], 1)
                pe.sem_inc(S["u_ready"], -1)
                with pe.Fori(0, NF // 2) as f:
                    for s in range(2):
                        pe.wait_ge(S["g0_free"], 1)
                        pe.sem_inc(S["g0_free"], -1)
                        proj.channels(g0[:], proj.group(), (uh, ul), KD, P, done="gate_proj")
                        pe.wait_ge(S["g1_free"], 1)
                        pe.sem_inc(S["g1_free"], -1)
                        proj.channels(g1[:], proj.group(), (uh, ul), KD, P, done="up_proj")
                pe.wait_ge(S["hidden_ready"], 1)
                pe.sem_inc(S["hidden_ready"], -1)
                with pe.Fori(0, KD // 2) as m:
                    for s, g in enumerate((g0, g1)):
                        pe.wait_ge(S[f"g{s}_free"], 1)
                        pe.sem_inc(S[f"g{s}_free"], -1)
                        for c, n in enumerate((8, 8, NF - 16)):
                            proj.channels(g[:], proj.group(), (hidh, hidl), n, P, done="down_proj" if c == 2 else None,
                                          k0=8 * c, more=c < 2, first=c == 0)
            norm_sum()

        @block.scalar
        def _(act):
            act.wait_ge(S["consts_act"], 1)
            act.sem_inc(S["consts_act"], -1)
            for n in ("sq0_used", "sq1_used"):
                give(act, n)

            round_next = rounder(act, S, stage, wh)
            round_next()

            def squares():
                for i in range(KD):
                    act.wait_ge(S[f"sq{i % 2}_used"], 1)
                    act.sem_inc(S[f"sq{i % 2}_used"], -1)
                    act.activation(sq[:, i % 2, :], hT[:, i, :], ACT.Square).then_inc(S[f"sq{i % 2}_ready"], 1)

            def root(src, n):
                act.activation(rstd[:], src, ACT.Sqrt, scale=1.0 / n, bias=EPS_COL).then_inc(S["root"], 1)

            def normed():
                act.wait_ge(S["h_ready_act"], 1)
                act.sem_inc(S["h_ready_act"], -1)
                squares()
                act.wait_ge(S["sq0_used"], 1)
                act.sem_inc(S["sq0_used"], -1)
                act.wait_ge(S["sq1_used"], 1)
                act.sem_inc(S["sq1_used"], -1)
                root(A[0][:], D)
                for n in ("sq0_used", "sq1_used"):
                    give(act, n)
                for i in range(KD):
                    act.wait_ge(S[f"tmp{i % 2}_ready"], 1)
                    act.sem_inc(S[f"tmp{i % 2}_ready"], -1)
                    act.activation(uh[:, i, :], tmp[:, i % 2, :], ACT.Copy).then_inc(S["hi_ready"], 1)

            def head(a_is_ret):
                act.wait_ge(S["head_out"], 1)
                act.sem_inc(S["head_out"], -1)
                act.wait_ge(S["sq0_used"], 1)
                act.sem_inc(S["sq0_used"], -1)
                act.wait_ge(S["sq1_used"], 1)
                act.sem_inc(S["sq1_used"], -1)
                act.activation(sq[:, 0, :], A[4][:], ACT.Square).then_inc(S["head_sq_ready"], 1)
                act.wait_ge(S["head_sumsq"], 1)
                act.sem_inc(S["head_sumsq"], -1)
                root(A[5][:], P)
                give(act, "sq0_used")
                give(act, "sq1_used")

            eps = der[:, 10:11]
            EPS_COL = eps
            with act.Fori(0, DEPTH) as layer:
                act.wait_ge(S["par_free"], 1)
                act.sem_inc(S["par_free"], -1)
                act.dma_start(par[:], par_dram[bass.ds(layer, 1)].rearrange("a p n -> p (a n)"))\
                   .then_inc(S["par_full"], 16)
                act.wait_ge(S["par_full"], 16)
                act.sem_inc(S["par_full"], -16)
                give(act, "par_dve")
                act.wait_ge(S["lam_sums"], 1)
                act.sem_inc(S["lam_sums"], -1)
                act.activation(der[:, 0:2], A[1][:, 0:2], ACT.Exp).then_inc(S["lam_exp"], 1)
                normed()
                with act.Fori(0, 2) as pair:
                    round_next()
                    act.wait_ge(S["q_proj"], 1)
                    act.sem_inc(S["q_proj"], -1)
                    act.wait_ge(S["qk_free"], 1)
                    act.sem_inc(S["qk_free"], -1)
                    fin(act, "act_self", act.activation(Q[:], g0[:], ACT.Copy, scale=64 ** -0.5), "g0_free")
                    round_next()
                    act.wait_ge(S["k_proj"], 1)
                    act.sem_inc(S["k_proj"], -1)
                    fin(act, "act_self", act.activation(K[:], g1[:], ACT.Copy), "g1_free", "qk_ready")
                    for a in range(2):
                        act.wait_ge(S["gam_free"], 1)
                        act.sem_inc(S["gam_free"], -1)
                        act.activation(gam[:], ago[:], ACT.Exp, scale=col("log_gamma", pair * 2 + a))\
                           .then_inc(S["gam_ready"], 1)
                        round_next()
                        act.wait_ge(S["v_proj"], 1)
                        act.sem_inc(S["v_proj"], -1)
                        act.wait_ge(S["v_free"], 1)
                        act.sem_inc(S["v_free"], -1)
                        fin(act, "act_self", act.activation(V[:].rearrange("p a b -> p (a b)"), g0[:], ACT.Copy),
                            "g0_free", "v_ready")
                        round_next()
                        act.wait_ge(S["gate_proj"], 1)
                        act.sem_inc(S["gate_proj"], -1)
                        act.wait_ge(S["tmp1_free"], 1)
                        act.sem_inc(S["tmp1_free"], -1)
                        act.activation(tmp[:, 1, :], g1[:], ACT.Tanh, scale=0.5).then_inc(S["tanh_ready"], 1)
                        head(True)
                        act.wait_ge(S["tmp0_ready"], 1)
                        act.sem_inc(S["tmp0_ready"], -1)
                        act.activation(hidh[:, bass.ds(pair * 2 + a, 1), :].rearrange("p a t -> p (a t)"),
                                       tmp[:, 0, :], ACT.Copy).then_inc(S["hi_ready"], 1)
                with act.Fori(0, 2) as pair:
                    for a in range(2):
                        round_next()
                        act.wait_ge(S["q_proj"], 1)
                        act.sem_inc(S["q_proj"], -1)
                        act.wait_ge(S["qk_free"], 1)
                        act.sem_inc(S["qk_free"], -1)
                        fin(act, "act_self", act.activation(Q[:], g0[:], ACT.Copy, scale=64 ** -0.5), "g0_free")
                        round_next()
                        act.wait_ge(S["k_proj"], 1)
                        act.sem_inc(S["k_proj"], -1)
                        fin(act, "act_self", act.activation(K[:], g1[:], ACT.Copy), "g1_free", "qk_ready")
                        round_next()
                        act.wait_ge(S["v_proj"], 1)
                        act.sem_inc(S["v_proj"], -1)
                        act.wait_ge(S["v_free"], 1)
                        act.sem_inc(S["v_free"], -1)
                        fin(act, "act_self", act.activation(V[:].rearrange("p a b -> p (a b)"), g0[:], ACT.Copy),
                            "g0_free", "v_ready")
                        for t in range(NT):
                            n = (t + 1) * P
                            for j in range(2):
                                act.wait_ge(S["max_ready"], 1)
                                act.sem_inc(S["max_ready"], -1)
                                act.activation(pr[:, j, 0:n], pr[:, j, 0:n], ACT.Exp, bias=st[:, j:j + 1],
                                               accum_out=st[:, 2 + j:3 + j]).then_inc(S["exp_ready"], 1)
                            act.wait_ge(S["probs_turned"], 1)
                            act.sem_inc(S["probs_turned"], -1)
                            fin(act, "act_self",
                                act.activation(PT[:, 0:t + 1, t * P:n],
                                               A[5][:, 0:n].rearrange("p (a b) -> p a b", b=P), ACT.Copy),
                                "a5_free", "pr0_free", *(["weights_ready"] if t == NT - 1 else []))
                        head(False)
                        give(act, "a5_free")
                        act.wait_ge(S["tmp0_ready"], 1)
                        act.sem_inc(S["tmp0_ready"], -1)
                        act.activation(hidh[:, bass.ds(pair * 2 + a + 4, 1), :].rearrange("p a t -> p (a t)"),
                                       tmp[:, 0, :], ACT.Copy).then_inc(S["hi_ready"], 1)
                with act.Fori(0, KD // 2) as m:
                    round_next()
                    round_next()
                normed()
                with act.Fori(0, NF // 2) as f:
                    for s in range(2):
                        round_next()
                        act.wait_ge(S["gate_proj"], 1)
                        act.sem_inc(S["gate_proj"], -1)
                        act.wait_ge(S["tmp1_free"], 1)
                        act.sem_inc(S["tmp1_free"], -1)
                        act.activation(tmp[:, 1, :], g0[:], ACT.Tanh, scale=0.5).then_inc(S["tanh_ready"], 1)
                        round_next()
                        act.wait_ge(S["tmp0_ready"], 1)
                        act.sem_inc(S["tmp0_ready"], -1)
                        act.activation(hidh[:, bass.ds(f * 2 + s, 1), :].rearrange("p a t -> p (a t)"),
                                       tmp[:, 0, :], ACT.Copy).then_inc(S["hi_ready"], 1)
                with act.Fori(0, KD // 2) as m:
                    for _ in range(6):
                        round_next()
            act.wait_ge(S["h_ready_act"], 1)
            act.sem_inc(S["h_ready_act"], -1)
            squares()
            act.wait_ge(S["sq0_used"], 1)
            act.sem_inc(S["sq0_used"], -1)
            act.wait_ge(S["sq1_used"], 1)
            act.sem_inc(S["sq1_used"], -1)
            root(A[0][:], D)

        @block.vector
        def _(dve):
            dve.wait_ge(S["consts_dve"], 1)
            dve.sem_inc(S["consts_dve"], -1)
            fin(dve, "dve_self", dve.memset(der[:, 10:11], 1e-6))
            for n in ("g0_free", "g1_free", "par_free", "qk_free", "v_free", "gam_free", "tmp1_free", "head_out_free",
                      "a0_free", "a1_free", "a2_free", "a3_free", "a5_free", "pr0_free", "h_ready_act"):
                give(dve, n)

            def dve_op(ins, *names):
                fin(dve, "dve_self", ins, *names)

            def lower(dst_h, dst_l, src, *names):
                dve.wait_ge(S["hi_ready"], 1)
                dve.sem_inc(S["hi_ready"], -1)
                dve_op(dve.tensor_tensor(dst_l, src, dst_h.bitcast(F32), ALU.subtract), *names)

            def normed(gain):
                dve.wait_ge(S["root"], 1)
                dve.sem_inc(S["root"], -1)
                dve_op(dve.reciprocal(rstd[:], rstd[:]))
                for i in range(KD):
                    dve_op(dve.scalar_tensor_tensor(out=tmp[:, i % 2, :], in0=hT[:, i, :], scalar=col(gain, i),
                                                    in1=rstd[:], op0=ALU.mult, op1=ALU.mult), f"tmp{i % 2}_ready")
                    if i:
                        lower(uh[:, i - 1, :], ul[:, i - 1, :], tmp[:, (i - 1) % 2, :])
                lower(uh[:, KD - 1, :], ul[:, KD - 1, :], tmp[:, (KD - 1) % 2, :], "u_ready")

            def head(gain, gated, tile):
                dve.wait_ge(S["root"], 1)
                dve.sem_inc(S["root"], -1)
                dve_op(dve.reciprocal(rstd[:], rstd[:]))
                dve_op(dve.scalar_tensor_tensor(out=tmp[:, 0, :], in0=A[4][:], scalar=gain, in1=rstd[:],
                                                op0=ALU.mult, op1=ALU.mult), "head_out_free",
                       *([] if gated else ["tmp0_ready"]))
                if gated:
                    dve_op(dve.scalar_tensor_tensor(out=tmp[:, 0, :], in0=tmp[:, 0, :], scalar=0.5, in1=gate[:],
                                                    op0=ALU.mult, op1=ALU.mult), "tmp0_ready")
                t = [x[:, bass.ds(tile, 1), :].rearrange("p a t -> p (a t)") for x in (hidh, hidl)]
                lower(t[0], t[1], tmp[:, 0, :])

            with dve.Fori(0, DEPTH) as layer:
                dve.wait_ge(S["par_dve"], 1)
                dve.sem_inc(S["par_dve"], -1)
                lam = PC2["lam"][0]
                dve_op(dve.tensor_tensor(der[0:64, 8:10], par[0:64, lam:lam + 3:2], par[0:64, lam + 1:lam + 4:2],
                                         ALU.mult), "lam_prod")
                dve.wait_ge(S["lam_exp"], 1)
                dve.sem_inc(S["lam_exp"], -1)
                dve_op(dve.tensor_tensor(der[:, 2:3], der[:, 1:2], der[:, 0:1], ALU.subtract))
                dve_op(dve.tensor_tensor(der[:, 3:4], der[:, 2:3], col("lam_init"), ALU.subtract))
                dve_op(dve.tensor_tensor(der[:, 4:5], col("diff_norm"), col("lam_rest"), ALU.mult))
                normed("attn_norm")
                with dve.Fori(0, 2) as pair:
                    for a in range(2):
                        dve.wait_ge(S["tanh_ready"], 1)
                        dve.sem_inc(S["tanh_ready"], -1)
                        dve_op(dve.scalar_tensor_tensor(out=gate[:], in0=tmp[:, 1, :], scalar=1.0, in1=g1[:],
                                                        op0=ALU.add, op1=ALU.mult), "g1_free", "tmp1_free")
                        dve.wait_ge(S["gam_ready"], 1)
                        dve.sem_inc(S["gam_ready"], -1)
                        for i in range(NT):
                            dve.wait_ge(S["scores"], 1)
                            dve.sem_inc(S["scores"], -1)
                            dve_op(dve.tensor_tensor(PT[:, i, i * P:T], A[i][:, i * P:T], gam[:, 0:T - i * P],
                                                     ALU.mult), f"a{i}_free",
                                   *(["gam_free", "weights_ready"] + ["qk_free"] * a if i == NT - 1 else []))
                        head(col("ret_norm"), True, pair * 2 + a)
                        give(dve, "v_free")
                with dve.Fori(0, 2) as pair:
                    for a in range(2):
                        for t in range(NT):
                            n = (t + 1) * P
                            dve.wait_ge(S["pr0_free"], 1)
                            dve.sem_inc(S["pr0_free"], -1)
                            for j in range(2):
                                dve.wait_ge(S["scores"], 1)
                                dve.sem_inc(S["scores"], -1)
                                b = 2 * (t % 2) + j
                                dve_op(dve.scalar_tensor_tensor(
                                    out=pr[:, j, 0:n], in0=near[:, T - n:T], scalar=col("slope", pair * 2 + a),
                                    in1=A[b][:, 0:n], op0=ALU.mult, op1=ALU.add), f"a{b}_free",
                                    *(["qk_free"] if (t, j) == (NT - 1, 1) else []))
                                dve_op(dve.tensor_reduce(st[:, 6:7], pr[:, j, 0:n], AX, ALU.max))
                                dve_op(dve.tensor_scalar(st[:, j:j + 1], st[:, 6:7], -1.0, None, ALU.mult), "max_ready")
                            dve.wait_ge(S["exp_ready"], 1)
                            dve.sem_inc(S["exp_ready"], -1)
                            dve.wait_ge(S["exp_ready"], 1)
                            dve.sem_inc(S["exp_ready"], -1)
                            dve_op(dve.reciprocal(st[:, 4:6], st[:, 2:4]))
                            dve_op(dve.tensor_tensor(st[:, 5:6], st[:, 5:6], der[:, 3:4], ALU.mult))
                            dve_op(dve.tensor_scalar(pr[:, 0, 0:n], pr[:, 0, 0:n], st[:, 4:5], None, ALU.mult))
                            dve_op(dve.scalar_tensor_tensor(out=pr[:, 0, 0:n], in0=pr[:, 1, 0:n], scalar=st[:, 5:6],
                                                            in1=pr[:, 0, 0:n], op0=ALU.mult, op1=ALU.add),
                                   "probs_ready")
                        head(der[:, 4:5], False, pair * 2 + a + 4)
                        give(dve, "v_free")
                give(dve, "mix_ready")
                with dve.Fori(0, KD // 2) as m:
                    for s, g in enumerate((g0, g1)):
                        dve.wait_ge(S["out_proj"], 1)
                        dve.sem_inc(S["out_proj"], -1)
                        h = hT[:, bass.ds(m * 2 + s, 1), :].rearrange("p a t -> p (a t)")
                        dve_op(dve.tensor_tensor(h, g[:], h, ALU.add), f"g{s}_free")
                give(dve, "h_ready_act")
                normed("ffn_norm")
                with dve.Fori(0, NF // 2) as f:
                    for s in range(2):
                        dve.wait_ge(S["tanh_ready"], 1)
                        dve.sem_inc(S["tanh_ready"], -1)
                        dve_op(dve.scalar_tensor_tensor(out=gate[:], in0=tmp[:, 1, :], scalar=1.0, in1=g0[:],
                                                        op0=ALU.add, op1=ALU.mult), "g0_free", "tmp1_free")
                        dve.wait_ge(S["up_proj"], 1)
                        dve.sem_inc(S["up_proj"], -1)
                        dve_op(dve.scalar_tensor_tensor(out=tmp[:, 0, :], in0=g1[:], scalar=0.5, in1=gate[:],
                                                        op0=ALU.mult, op1=ALU.mult), "g1_free", "tmp0_ready")
                        lower(hidh[:, bass.ds(f * 2 + s, 1), :].rearrange("p a t -> p (a t)"),
                              hidl[:, bass.ds(f * 2 + s, 1), :].rearrange("p a t -> p (a t)"), tmp[:, 0, :])
                give(dve, "hidden_ready")
                with dve.Fori(0, KD // 2) as m:
                    for s, g in enumerate((g0, g1)):
                        dve.wait_ge(S["down_proj"], 1)
                        dve.sem_inc(S["down_proj"], -1)
                        h = hT[:, bass.ds(m * 2 + s, 1), :].rearrange("p a t -> p (a t)")
                        dve_op(dve.tensor_tensor(h, g[:], h, ALU.add), f"g{s}_free")
                give(dve, "h_ready_act", "par_free")
            dve.wait_ge(S["root"], 1)
            dve.sem_inc(S["root"], -1)
            dve_op(dve.reciprocal(rstd[:], rstd[:]))
            for i in range(KD):
                dve_op(dve.scalar_tensor_tensor(out=hT[:, i, :], in0=hT[:, i, :], scalar=col("final_norm", i),
                                                in1=rstd[:], op0=ALU.mult, op1=ALU.mult))
            give(dve, "out_ready")


def k_tiles(w, c0, cn=P):
    n, k = w.shape[0], w.shape[1]
    return w[:, :, c0:c0 + cn].reshape(n, k // P, P, cn).transpose(0, 2, 1, 3).reshape(n, P, k // P * cn)


def as_group(a):
    return np.pad(a, ((0, 0), (0, 0), (0, GW - a.shape[2])))


def columns(v):
    return v.reshape(v.shape[0], -1, P).transpose(0, 2, 1)


def pad_stream(s):
    return np.concatenate([s.reshape(-1, P, GW), np.zeros((1, P, GW), np.float32)])


def first_stream(w_in, w_uq, w_ukv, w_mem, w_o, w_out):
    r, o = 0, 1664
    q, kv, kpe, mg, cu, cg, xq, xg, mrg = 2176, 2560, 2816, 2848, 3360, 4384, 4896, 5408, 5920
    x = lambda c0: k_tiles(w_in, c0)
    groups = []
    for i in range(NW):
        groups += [x(cu + P * i), x(cu + W + P * i)]
    groups += [x(cg + P * i) for i in range(NW)]
    groups += [x(q + P * i) for i in range(3)] + [x(kv + P * i) for i in range(2)]
    groups.append(k_tiles(np.concatenate([w_in[:, :, kpe:kpe + 32]] * 4, 2), 0))
    groups += [x(mg + P * i) for i in range(NW)]
    for h in range(8):
        groups.append(as_group(np.concatenate([k_tiles(w_uq, 96 * h, 96), k_tiles(w_ukv, P * h)], 2)))
    for h in range(4):
        groups += [x(xq + P * h), x(xg + P * h), k_tiles(w_mem, P * h), k_tiles(w_mem, W + P * h)]
    groups += [x(P * i) for i in range(12)]
    groups += [as_group(k_tiles(w_in[:, k:k + W], 1536)) for k in (0, W)]

    def merge(n, d):
        return [x(mrg + D * n + P * d), x(mrg + D * n + P * (d + 1)), k_tiles(w_o[:, n], P * d, 2 * P)]

    for chunk in range(NT):
        for n in (1, 2, 3):
            groups += merge(n, 2 * chunk)
    groups += [x(o + P * i) for i in range(NW)]
    for d in range(0, KD, 2):
        groups += merge(0, d)
    groups += [k_tiles(w_out, P * m) for m in range(KD)]
    assert len(groups) == G1
    return pad_stream(np.stack(groups, 1))


def first_params(mu, w0, a0, k_k, k_a, r_k, lnx_g, lnx_b, q_norm, kv_norm, conv_w, conv_b, cln_g, cln_b, b_gate,
                 ln_g, ln_b):
    taps = conv_w.reshape(DEPTH, TAPS, NW, P).transpose(0, 3, 2, 1).reshape(DEPTH, P, NW * TAPS)
    inv_freq = np.float32(10000.0) ** (-np.arange(0, 32, 2, dtype=np.float32) / np.float32(32))
    freq = np.broadcast_to(np.tile(inv_freq, P // 16)[None, :, None], (DEPTH, P, 1))
    cols = [columns(mu), columns(w0), columns(a0), columns(k_k), columns(k_a), columns(r_k.reshape(DEPTH, W)),
            columns(lnx_g), columns(lnx_b), columns(q_norm), columns(kv_norm), taps, columns(conv_b), columns(cln_g),
            columns(cln_b), columns(b_gate.reshape(DEPTH, -1)), columns(ln_g), columns(ln_b), freq]
    return np.ascontiguousarray(np.concatenate(cols, 2), dtype=np.float32)


def second_stream(w_in, w_out, w_gate, w_up, w_down):
    groups = []
    for pair in range(2):
        groups += [k_tiles(w_in, P * pair), k_tiles(w_in, 256 + P * pair)]
        for h in (2 * pair, 2 * pair + 1):
            groups += [k_tiles(w_in, 512 + P * h), k_tiles(w_in, 1024 + P * h)]
    for h in range(4):
        groups += [k_tiles(w_in, 1536 + 512 * i + P * h) for i in range(3)]
    groups += [k_tiles(w_out, P * m) for m in range(KD)]
    for f in range(NF):
        groups += [k_tiles(w_gate, P * f), k_tiles(w_up, P * f)]
    for m in range(KD):
        groups += [as_group(k_tiles(w_down[:, k:k + GW], P * m)) for k in range(0, FFN, GW)]
    assert len(groups) == G2
    s = np.stack(groups, 1)
    return pad_stream(s)


def second_params(attn_norm, ret_norm, diff_norm, ffn_norm, lam, final_norm):
    lam_init = np.array([0.8 - 0.6 * math.exp(-0.3 * i) for i in range(DEPTH)])
    full = lambda v: np.broadcast_to(np.asarray(v, np.float32).reshape(DEPTH, 1, -1), (DEPTH, P, np.size(v) // DEPTH))
    log_gamma = np.tile(-np.log1p(-np.exp2(-5.0 - np.arange(4))), (DEPTH, 1))
    slope = np.tile(np.exp2(-2.0 * np.arange(1, 5)), (DEPTH, 1))
    lams = np.concatenate([np.stack(lam, 2), np.zeros((DEPTH, 64, 4), np.float32)], 1)
    cols = [columns(attn_norm), columns(ret_norm), columns(diff_norm), columns(ffn_norm), lams, full(lam_init),
            full(1.0 - lam_init), np.repeat(columns(final_norm[None]), DEPTH, 0), full(log_gamma), full(slope)]
    return np.ascontiguousarray(np.concatenate(cols, 2), dtype=np.float32)


def build(nc, x, mem, positions, params1, lora, stream1, params2, stream2, out):
    with ExitStack() as ctx:
        hT = ctx.enter_context(nc.sbuf_tensor("hT", [P, KD, T], F32))
        with ExitStack() as first:
            S = Sems(nc, first, "first_")
            first_block(nc, S, x, mem, positions, params1, lora, stream1, hT)
            with nc.Block() as block:
                @block.gpsimd
                def _(pool):
                    for sem in S.all.values():
                        pool.sem_clear(sem)
        second_block(nc, Sems(nc, ctx, "second_"), params2, stream2, out, hT)


def kernel(**inputs):
    import concourse.bacc as bacc
    from concourse.bass_utils import run_bass_kernel_spmd

    v = {n: np.asarray(a) for n, a in inputs.items()}
    arrays = {
        "x": np.ascontiguousarray(v["x"][0].T),
        "mem": np.ascontiguousarray(v["mem"][0].T),
        "positions": v["positions"],
        "params1": first_params(*(v[n] for n in (
            "rwkv_mu", "rwkv_w0", "rwkv_a0", "rwkv_k_k", "rwkv_k_a", "rwkv_r_k", "rwkv_lnx_g", "rwkv_lnx_b",
            "mla_q_norm", "mla_kv_norm", "conv_w", "conv_b", "conv_ln_g", "conv_ln_b", "b_gate", "ln_g", "ln_b"))),
        "lora": np.ascontiguousarray(np.concatenate([v["rwkv_w2"], v["rwkv_a2"]], 1)),
        "stream1": first_stream(*(v[n] for n in ("w_in", "mla_w_uq", "mla_w_ukv", "xattn_w_mem_kv", "w_o_branch",
                                                 "w_out"))),
        "params2": second_params(*(v[n + "_2"] for n in ("attn_norm", "ret_norm", "diff_norm", "ffn_norm")),
                                 [v[f"lambda_{n}_2"] for n in ("q1", "k1", "q2", "k2")], v["final_norm_2"]),
        "stream2": second_stream(*(v[n + "_2"] for n in ("w_in", "w_out", "w_gate", "w_up", "w_down"))),
    }
    nc = bacc.Bacc("TRN2", target_bir_lowering=False, num_devices=1)
    args = [nc.dram_tensor(f"in_{n}", a.shape, mybir.dt.from_np(a.dtype), kind="ExternalInput").ap()
            for n, a in arrays.items()]
    out = nc.dram_tensor("out_x", (D, T), F32, kind="ExternalOutput").ap()
    build(nc, *args, out)
    r = run_bass_kernel_spmd(nc, [{f"in_{n}": a for n, a in arrays.items()}], core_ids=[0])
    return np.ascontiguousarray(r.results[0]["out_x"].T)[None]
```

```python
from contextlib import ExitStack
import math

import numpy as np
import concourse.bass as bass
from concourse import mybir

P = 128
T = 512
NT = T // P
D = 1024
KD = D // P
W = 512
NW = W // P
DEPTH = 2
MEM = 256
GW = 1024
SPLIT_SLOTS = 2
STAGE_SLOTS = 2
TAPS = 31
F32 = mybir.dt.float32
F32R = mybir.dt.float32r
I32 = mybir.dt.int32
ALU = mybir.AluOpType
ACT = mybir.ActivationFunctionType
AX = mybir.AxisListType.X
MASKED = -1e30
ALPHA = (2.0 * DEPTH) ** 0.25
KAPPA = math.exp(-0.5) / 2
CH = P
FFN = 2816
ARENA = 18200
NF = FFN // P

_P1 = [("mu", 13), ("w0", 4), ("a0", 4), ("k_k", 4), ("k_a", 4), ("r_k", 4), ("lnx_g", 4),
       ("lnx_b", 4), ("q_norm", 3), ("kv_norm", 2), ("conv_w", NW * TAPS), ("conv_b", 4),
       ("cln_g", 4), ("cln_b", 4), ("b_gate", 32), ("ln_g", 8), ("ln_b", 8), ("inv_freq", 1)]
_P2 = [("attn_norm", 8), ("ret_norm", 1), ("diff_norm", 1), ("ffn_norm", 8), ("lam", 4),
       ("lam_init", 1), ("lam_rest", 1), ("final_norm", 8), ("log_gamma", 4), ("slope", 4)]


def offsets(spec):
    at, out = 0, {}
    for name, n in spec:
        out[name] = (at, n)
        at += n
    return out, at


PC1, NP1 = offsets(_P1)
PC2, NP2 = offsets(_P2)
G1 = 8 + 4 + 6 + 4 + 8 + 16 + 12 + 2 + 36 + 4 + 12 + 8
G2 = 12 + 12 + 8 + 2 * NF + 24


class Sems:

    def __init__(self, nc, ctx, prefix=""):
        self.nc, self.ctx, self.prefix, self.all = nc, ctx, prefix, {}

    def __getitem__(self, name):
        if name not in self.all:
            self.all[name] = self.ctx.enter_context(self.nc.semaphore(self.prefix + name))
        return self.all[name]


def helpers(S):
    def give(eng, *names):
        for name in names:
            eng.sem_inc(S[name], 1)

    def fin(eng, own, ins, *names):
        ins.then_inc(S[own], 1)
        eng.wait_ge(S[own], 1)
        eng.sem_inc(S[own], -1)
        give(eng, *names)

    return give, fin


def weight_loader(sp, S, stage, stream, groups):
    with sp.Fori(0, groups // STAGE_SLOTS) as g:
        for s in range(STAGE_SLOTS):
            sp.wait_ge(S[f"stage{s}_free"], 1)
            sp.sem_inc(S[f"stage{s}_free"], -1)
            sp.dma_start(stage[:, s, :], stream[bass.ds(g * STAGE_SLOTS + s, 1)].rearrange("a p n -> p (a n)"))\
              .then_inc(S[f"stage{s}_full"], 16)
    sp.wait_ge(S["stage0_free"], 1)
    sp.sem_inc(S["stage0_free"], -1)
    sp.dma_start(stage[:, 0, :], stream[groups]).then_inc(S["stage0_full"], 16)


def weight_remainders(pool, S, give, fin, stage, wh, wl, groups):
    for s in range(STAGE_SLOTS):
        give(pool, f"stage{s}_free")
    give(pool, "w0_free")
    with pool.Fori(0, groups // STAGE_SLOTS) as g:
        for s in range(STAGE_SLOTS):
            pool.wait_ge(S[f"hi{s}_ready"], 1)
            pool.sem_inc(S[f"hi{s}_ready"], -1)
            fin(pool, "pool_self", pool.tensor_tensor(wl[:, s, :], stage[:, s, :], wh[:, s, :].bitcast(F32),
                                                      ALU.subtract), f"w{s}_ready", f"stage{s}_free")
    pool.wait_ge(S["hi0_ready"], 1)
    pool.sem_inc(S["hi0_ready"], -1)


def rounder(act, S, stage, wh):
    slot = [0]

    def round_next():
        s = slot[0]
        slot[0] = 1 - s
        act.wait_ge(S[f"stage{s}_full"], 16)
        act.sem_inc(S[f"stage{s}_full"], -16)
        act.wait_ge(S[f"w{s}_free"], 1)
        act.sem_inc(S[f"w{s}_free"], -1)
        act.activation(wh[:, s, :], stage[:, s, :], ACT.Copy).then_inc(S[f"hi{s}_ready"], 1)

    return round_next


class Projector:

    def __init__(self, pe, S, wh, wl):
        self.pe, self.S, self.wh, self.wl, self.slot, self.release = pe, S, wh, wl, 1, None

    def group(self):
        self.release = f"w{self.slot}_free"
        self.slot = 1 - self.slot
        self.pe.wait_ge(self.S[f"w{self.slot}_ready"], 1)
        self.pe.sem_inc(self.S[f"w{self.slot}_ready"], -1)
        return self.wh[:, self.slot, :], self.wl[:, self.slot, :]

    def product(self, out, terms, done=None, more=False, first=True):
        steps = [(a, b) for (ah, al), (bh, bl) in terms for a, b in ((ah, bh), (ah, bl), (al, bh))]
        for n, (a, b) in enumerate(steps):
            ins = self.pe.matmul(out, a, b, start=first and n == 0, stop=not more and n == len(steps) - 1)
            if n == 0 and self.release:
                ins.then_inc(self.S[self.release], 1)
                self.release = None
        if done:
            ins.then_inc(self.S[done], 1)

    def channels(self, out, w, x, kt, width, c0=0, cn=P, done=None, k0=0, more=False, first=True):
        wh, wl = w
        self.product(out, [((wh[:, k * width + c0:k * width + c0 + cn], wl[:, k * width + c0:k * width + c0 + cn]),
                            (x[0][:, k0 + k, :], x[1][:, k0 + k, :])) for k in range(kt)], done, more, first)


def first_block(nc, S, x_dram, mem_dram, pos_dram, par_dram, lora_dram, stream, hT):
    give, fin = helpers(S)
    with ExitStack() as ctx:
        def sb(name, shape, dt=F32):
            return ctx.enter_context(nc.sbuf_tensor(name + "_1", shape, dt))

        bank = [ctx.enter_context(nc.psum_tensor(f"bank{i}_1", [P, 512], F32)) for i in range(8)]
        g0, g1 = bank[0], bank[1]
        A = bank[2:]
        stage = sb("stage", [P, STAGE_SLOTS, GW])
        wh = sb("wh", [P, SPLIT_SLOTS, GW], F32R)
        wl = sb("wl", [P, SPLIT_SLOTS, GW], F32R)
        xh = sb("xh", [P, KD, T], F32R)
        xl = sb("xl", [P, KD, T], F32R)
        yh = sb("yh", [P, 12, T], F32R)
        yl = sb("yl", [P, 12, T], F32R)
        par = sb("par", [P, NP1])
        der = sb("der", [P, 64])
        ones = sb("ones", [P, P])
        ident = sb("ident", [P, P])
        halves = sb("halves", [P, P])
        future = sb("future", [P, P])
        after = sb("after", [P, 2, P])
        before = sb("before", [P, P])
        level = sb("level", [P, 7, 2, P], mybir.dt.uint8)
        rotm = sb("rotm", [P, 32])
        eps = sb("eps", [P, 4])
        tmp = sb("tmp", [P, 2, T])
        sq = sb("sq", [P, 2, T])
        rstd = sb("rstd", [P, T])
        arena = sb("arena", [P, ARENA])

        class Carve:

            def __init__(self, at=0):
                self.at = at

            def __call__(self, *shape):
                n = int(np.prod(shape))
                v = arena[:, self.at:self.at + n]
                self.at += n
                assert self.at <= ARENA, self.at
                if len(shape) == 2:
                    v = v.rearrange("p (a b) -> p a b", b=shape[1])
                if len(shape) == 3:
                    v = v.rearrange("p (a b c) -> p a b c", b=shape[1], c=shape[2])
                return v

        c = Carve()
        hb = c(NW, T + 32)
        cacc = c(NW, T)
        cgate = c(NW, T)
        lsq = c(5, T)
        lat = c(5, T)
        lat_end = c.at
        c = Carve()
        y32 = c(NW, T)
        Qh = [c(T) for a in range(2)]
        PTh = [c(NT, T) for a in range(2)]
        probs = c(4 * T)
        probsh = [[probs[:, 7 * P * a + 3 * P * u:7 * P * a + 3 * P * u + (3 + u) * P] for u in range(2)]
                  for a in range(2)]
        c.at -= 2 * P
        Vh = [c(NT, 64) for a in range(2)]
        Kh = [c(T) for a in range(2)]
        Q, K, PT, V, posb = Qh[0], Kh[0], PTh[0], Vh[0], Qh[0]
        memf = c(KD, MEM)
        c.at = max(c.at, lat_end)
        mgate = c(NW, T)
        xgate = c(NW, T)
        kr = c(T)
        trig = c(2, T)
        causal = kr
        st = c(24)
        xprobs = [p[:, 2:4, :].rearrange("p a (b m) -> p (a b) m", m=MEM) for p in PTh]
        xV = [v.rearrange("p a b -> p (a b)").rearrange("p (a b) -> p a b", b=P) for v in Vh]
        c = Carve()
        RKV = c(12, T)
        R, RK_, RV = RKV[:, 0:4, :], RKV[:, 4:8, :], RKV[:, 8:12, :]
        KK = c(NW, T)
        BB = c(NW, T)
        TH = c(NW, T)
        rgate = TH
        flat = tmp[:].rearrange("p a b -> p (a b)")
        AR = flat[:, 0:512].rearrange("p (a b c) -> p a b c", a=2, b=2)
        Bt = flat[:, 512:768].rearrange("p (a b) -> p a b", a=2)
        Kt = flat[:, 768:1024].rearrange("p (a b) -> p a b", a=2)
        EP = rstd[:, 0:2 * (P + 1)].rearrange("p (a b) -> p a b", a=2)
        Sm = rstd[:, 260:388].rearrange("p (a b) -> p a b", a=2)
        emid = rstd[:, 388:390]
        TM = c(6, P)
        UM = c(4, 4 * P)
        Tm = c(4, P)
        XZ = c(4, 2, P)
        Qs = c(4, P)
        QC = c(2, P + 1)
        St = c(NW, 64)
        rhs_s = Bt[:, :, :].rearrange("p a b -> p (a b)")
        sa_s = Kt[:, :, :].rearrange("p a b -> p (a b)")
        rkc = Qs[:, 0:2, :]
        EM = XZ[:, 0, :, :]
        QD = XZ[:, 1:4, :, :].rearrange("p a b c -> p (a b c)")[:, 0:2 * (P + 1)].rearrange("p (a b) -> p a b", b=P + 1)
        Vc = c(2, P)
        wa = UM[:, 0, :]
        lora = UM[:, 1, :]

        def col(name, i=0, n=1):
            a = PC1[name][0]
            return par[:, a + i:a + i + n] if isinstance(i, int) else par[:, bass.ds(i + a, n)]

        def tile(t, i):
            return t[:, i, :] if isinstance(i, int) else t[:, bass.ds(i, 1), :].rearrange("p a t -> p (a t)")

        block = ctx.enter_context(nc.Block())

        @block.sync
        def _(sp):
            weight_loader(sp, S, stage, stream, DEPTH * G1)

        @block.gpsimd
        def _(pool):
            def op(ins, *names):
                fin(pool, "pool_self", ins, *names)

            def select(t, pattern, base, mult, compare=ALU.is_ge, fill=0.0, *names):
                op(pool.affine_select(out=t, in_=t, compare_op=compare, fill=fill, base=base, pattern=pattern,
                                      channel_multiplier=mult), *names)

            op(pool.memset(ones[:], 1.0))
            op(pool.memset(ident[:], 0.0))
            select(ident[:], [[-1, P]], 0, 1, ALU.not_equal, 1.0)
            op(pool.memset(halves[:], 1.0))
            select(halves[:, 0:64], [[0, 64]], 63, -1)
            select(halves[:, 64:P], [[0, 64]], -64, 1)
            op(pool.memset(future[:], 0.0))
            select(future[:], [[-1, P]], 0, 1, ALU.is_ge, MASKED)
            op(pool.memset(after[:], 1.0))
            select(after[:, 0, :], [[1, P]], -1, -1)
            select(after[:, 1, :], [[1, P]], 0, -1)
            op(pool.memset(before[:], 1.0))
            select(before[:], [[-1, P]], -1, 1)
            op(pool.memset(rotm[:], 0.0))
            select(rotm[64:96, :], [[-1, 32]], -16, 1, ALU.not_equal, -1.0)
            select(rotm[64:96, :], [[-1, 32]], 16, 1, ALU.not_equal, 1.0)
            for n in range(7):
                b = 1 << n
                m = arena[:, 0:2 * P].rearrange("p (o j h c) -> p o j h c", o=2, h=2, c=b)
                op(pool.memset(arena[:, 0:2 * P], 0.0))
                for o in range(2):
                    v = m[:, o, :, o, :]
                    op(pool.memset(v, 1.0))
                    lo = b * (1 - o)
                    pat = [[-2 * b, P // (2 * b)], [0, b]]
                    select(v, pat, -lo, 1)
                    select(v, [[2 * b, P // (2 * b)], [0, b]], lo + b - 1, -1)
                op(pool.tensor_copy(level[:, n, :, :].rearrange("p a b -> p (a b)"), arena[:, 0:2 * P]))
            give(pool, "consts_pe", "consts_act", "consts_dve")
            weight_remainders(pool, S, give, fin, stage, wh, wl, DEPTH * G1)

        @block.tensor
        def _(pe):
            pe.wait_ge(S["consts_pe"], 1)
            pe.sem_inc(S["consts_pe"], -1)
            proj = Projector(pe, S, wh, wl)
            X = (xh, xl)

            def gates():
                with pe.Fori(0, NW // 2):
                    for s, g in enumerate((g0, g1)):
                        pe.wait_ge(S[f"g{s}_free"], 1)
                        pe.sem_inc(S[f"g{s}_free"], -1)
                        proj.channels(g[:], proj.group(), X, KD, P, done="gate_proj")

            def total(out, tiles, want, done, matrix=ones):
                pe.wait_ge(S[want], 1)
                pe.sem_inc(S[want], -1)
                for n, t in enumerate(tiles):
                    ins = pe.matmul(out, matrix[:], t, start=n == 0, stop=n == len(tiles) - 1)
                ins.then_inc(S[done], 1)

            def layer_norm(tiles):
                total(A[0][:], tiles, "ln_in", "ln_sum")
                for i in range(len(tiles)):
                    pe.wait_ge(S[f"sq{i % 2}_ready"], 1)
                    pe.sem_inc(S[f"sq{i % 2}_ready"], -1)
                    pe.matmul(A[1][:], ones[:], sq[:, i % 2, :], start=i == 0, stop=i == len(tiles) - 1)\
                      .then_inc(S[f"sq{i % 2}_used"], 1)

            def merge(slot):
                for s, g in enumerate((g0, g1)):
                    pe.wait_ge(S[f"g{s}_free"], 1)
                    pe.sem_inc(S[f"g{s}_free"], -1)
                    proj.channels(g[:], proj.group(), X, KD, P, done="merge_gate")
                w = proj.group()
                for s, g in enumerate((g0, g1)):
                    pe.wait_ge(S[f"g{s}_free"], 1)
                    pe.sem_inc(S[f"g{s}_free"], -1)
                    proj.channels(g[:], w, (yh[:, 4 * slot:4 * slot + 4, :], yl[:, 4 * slot:4 * slot + 4, :]), NW,
                                  2 * P, c0=s * P, done="merge_proj")

            def merge_quarter(q, chunk):
                group, part = q // 4, q % 4
                slot, step = (2, 0, 1)[group // 3], group % 3
                if part == 0:
                    chunk_w[0] = proj.group()
                s = step if step < 2 else part // 2
                if part == 0 or (step == 2 and part == 2):
                    pe.wait_ge(S[f"g{s}_free"], 1)
                    pe.sem_inc(S[f"g{s}_free"], -1)
                if step < 2:
                    proj.channels((g0, g1)[s][:], chunk_w[0], X, 2, P, c0=2 * part * P, k0=2 * part, more=part < 3,
                                  first=part == 0, done="merge_gate" if part == 3 else None)
                else:
                    k = 2 * (part % 2)
                    proj.channels((g0, g1)[s][:], chunk_w[0], (yh, yl), 2, 2 * P, c0=2 * k * P + s * P,
                                  k0=4 * slot + k, more=k == 0, first=k == 0, done="merge_proj" if k else None)

            chunk_w = [None]

            def mla_pair():
                for a in range(2):
                    h, lo = proj.group()
                    pe.wait_ge(S["g0_free"], 1)
                    pe.sem_inc(S["g0_free"], -1)
                    proj.channels(g0[0:96, :], (h[:, 0:288], lo[:, 0:288]), (yh[:, 4:7, :], yl[:, 4:7, :]), 3, 96,
                                  cn=96, done="q_proj")
                    pe.wait_ge(S["g1_free"], 1)
                    pe.sem_inc(S["g1_free"], -1)
                    proj.channels(g1[:], (h[:, 288:544], lo[:, 288:544]), (yh[:, 8:10, :], yl[:, 8:10, :]), 2, P,
                                  done="kv_proj")
                    pe.wait_ge(S["q_raw"], 1)
                    pe.sem_inc(S["q_raw"], -1)
                    pe.wait_ge(S[f"a{2 + a}_free"], 1)
                    pe.sem_inc(S[f"a{2 + a}_free"], -1)
                    pe.matmul(A[2 + a][64:96, :], rotm[64:96, :], Qh[a][64:96, :], start=True, stop=True)\
                      .then_inc(S["q_rot"], 1)
                for a in range(2):
                    pe.wait_ge(S["v_raw"], 1)
                    pe.sem_inc(S["v_raw"], -1)
                    pe.wait_ge(S[f"a{4 + a}_free"], 1)
                    pe.sem_inc(S[f"a{4 + a}_free"], -1)
                    for t in range(NT):
                        ins = pe.transpose(A[4 + a][:, 64 * t:64 * t + 64], PTh[a][64:P, 0, t * P:(t + 1) * P],
                                           ident[64:P, 64:P])
                    ins.then_inc(S["v_turned"], 1)

                def scores(a, t):
                    n = (t + 1) * P
                    pe.wait_ge(S[f"a{a}_free"], 1)
                    pe.sem_inc(S[f"a{a}_free"], -1)
                    pe.matmul(A[a][:, 0:n], Qh[a][0:96, t * P:n], Kh[a][0:96, 0:n], start=True, stop=True)\
                      .then_inc(S["scores"], 1)

                for a in range(2):
                    pe.wait_ge(S["qk_ready"], 1)
                    pe.sem_inc(S["qk_ready"], -1)
                    pe.wait_ge(S["k_ready"], 1)
                    pe.sem_inc(S["k_ready"], -1)
                    scores(a, 0)
                for t in range(NT):
                    for a in range(2):
                        if t + 1 < NT:
                            scores(a, t + 1)
                        pe.wait_ge(S["probs_ready"], 1)
                        pe.sem_inc(S["probs_ready"], -1)
                        pe.wait_ge(S[f"a{2 + a}_free"], 1)
                        pe.sem_inc(S[f"a{2 + a}_free"], -1)
                        for i in range(t + 1):
                            ins = pe.transpose(A[2 + a][:, i * P:(i + 1) * P], probsh[a][t % 2][:, i * P:(i + 1) * P],
                                               ident[:])
                        ins.then_inc(S["probs_turned"], 1)
                for a in range(2):
                    pe.wait_ge(S["v_ready"], 1)
                    pe.sem_inc(S["v_ready"], -1)
                    pe.wait_ge(S["weights_ready"], 1)
                    pe.sem_inc(S["weights_ready"], -1)
                    pe.wait_ge(S[f"a{4 + a}_free"], 1)
                    pe.sem_inc(S[f"a{4 + a}_free"], -1)
                    for i in range(NT):
                        ins = pe.matmul(A[4 + a][64 * a:64 * a + 64, i * P:T], Vh[a][:, i, :], PTh[a][:, i, i * P:T],
                                        start=i == 0, stop=i == NT - 1)
                    ins.then_inc(S["head_out"], 1)

            def rwkv_half(g, chunk):
                for q in range(6):
                    merge_quarter(18 * g + q, chunk)
                r = [slice(64 * (j % 2), 64 * (j % 2) + 64) for j in range(4)]
                pe.wait_ge(S["ab_ready"], 1)
                pe.sem_inc(S["ab_ready"], -1)
                for j in range(4):
                    pe.wait_ge(S[f"a{j}_free"], 1)
                    pe.sem_inc(S[f"a{j}_free"], -1)
                    x = AR[r[j], j // 2, :, :].rearrange("p a b -> p (a b)")
                    pe.matmul(A[j][:, 0:256], Bt[r[j], j // 2, :], x, start=True, stop=True)
                    pe.matmul(A[j][:, 256:512], Kt[r[j], j // 2, :], x, start=True, stop=True)\
                      .then_inc(S["um_out"], 1)
                for p in range(2):
                    pe.wait_ge(S[f"a{4 + p}_free"], 1)
                    pe.sem_inc(S[f"a{4 + p}_free"], -1)
                    for i in range(2):
                        j = 2 * i + p
                        ins = pe.matmul(A[4 + p][:, i * P:(i + 1) * P], AR[r[j], i, 0, :], Bt[r[j], i, :],
                                        start=True, stop=True)
                    ins.then_inc(S["t_out"], 1)
                pe.wait_ge(S["a0_free"], 1)
                pe.sem_inc(S["a0_free"], -1)
                for i in range(2):
                    pe.transpose(A[0][:, i * P:(i + 1) * P], Vc[:, i, :], ident[:])
                    ins = pe.transpose(A[0][:, (2 + i) * P:(3 + i) * P], Bt[:, i, :], ident[:])
                ins.then_inc(S["turned"], 1)
                pe.wait_ge(S["a1_free"], 1)
                pe.sem_inc(S["a1_free"], -1)
                for i in range(2):
                    pe.transpose(A[1][:, i * P:(i + 1) * P], Kt[:, i, :], ident[:])
                ins = pe.matmul(A[1][:, 256:512], halves[:], rkc.rearrange("p a b -> p (a b)"), start=True, stop=True)
                ins.then_inc(S["turned"], 1)
                pe.wait_ge(S["xz_ready"], 1)
                pe.sem_inc(S["xz_ready"], -1)
                for n in range(1, 7):
                    pe.wait_ge(S["a4_free"], 1)
                    pe.sem_inc(S["a4_free"], -1)
                    for j in range(4):
                        ins = pe.matmul(A[4][:, j * P:(j + 1) * P], Tm[:, j, :], XZ[:, j, 1, :], start=True, stop=True)
                    ins.then_inc(S["uz_out"], 1)
                    merge_quarter(18 * g + 4 + 2 * n, chunk)
                    pe.wait_ge(S["uz_ready"], 1)
                    pe.sem_inc(S["uz_ready"], -1)
                    for p, b in ((0, 5), (1, 3)):
                        pe.wait_ge(S[f"a{b}_free"], 1)
                        pe.sem_inc(S[f"a{b}_free"], -1)
                        for q in range(2):
                            j = 2 * p + q
                            pe.matmul(A[b][:, q * 256:q * 256 + P], Qs[:, j, :], XZ[:, j, 0, :], start=True, stop=True)
                            ins = pe.matmul(A[b][:, q * 256 + P:q * 256 + 256], XZ[:, j, 0, :], Qs[:, j, :],
                                            start=True, stop=True)
                        ins.then_inc(S["fill_out"], 1)
                    merge_quarter(18 * g + 5 + 2 * n, chunk)
                    pe.wait_ge(S["xz_ready"], 1)
                    pe.sem_inc(S["xz_ready"], -1)
                pe.wait_ge(S["turned_ready"], 1)
                pe.sem_inc(S["turned_ready"], -1)
                for p in range(2):
                    pe.wait_ge(S[f"a{2 + p}_free"], 1)
                    pe.sem_inc(S[f"a{2 + p}_free"], -1)
                    for j in (p, p + 2):
                        o = A[2 + p][:, 32 * (j - p):32 * (j - p) + 64]
                        pe.matmul(o, UM[:, j, 256:384], TM[:, j // 2, r[j]], start=True, stop=False)
                        ins = pe.matmul(o, AR[r[j], j // 2, 0, :], Sm[r[j], j // 2, :], start=False, stop=True)
                    ins.then_inc(S["rhs_out"], 1)
                pe.wait_ge(S["rhs_ready"], 1)
                pe.sem_inc(S["rhs_ready"], -1)
                pe.wait_ge(S["a0_free"], 1)
                pe.sem_inc(S["a0_free"], -1)
                for j in range(4):
                    ins = pe.matmul(A[0][:, 64 * j:64 * j + 64], XZ[:, j, 1, :], rhs_s[:, 64 * j:64 * j + 64],
                                    start=True, stop=True)
                ins.then_inc(S["sa_out"], 1)
                pe.wait_ge(S["sa_ready"], 1)
                pe.sem_inc(S["sa_ready"], -1)
                pe.wait_ge(S["a4_free"], 1)
                pe.sem_inc(S["a4_free"], -1)
                for j in range(4):
                    o = A[4][r[j], (j // 2) * P:(j // 2 + 1) * P]
                    pe.matmul(o, sa_s[:, 64 * j:64 * j + 64], UM[:, j, 128:256], start=True, stop=False)
                    pe.matmul(o, TM[:, j // 2, r[j]], UM[:, j, 384:512], start=False, stop=False)
                    ins = pe.matmul(o, Sm[r[j], j // 2, :], AR[r[j], j // 2, 1, :], start=False, stop=True)
                ins.then_inc(S["y_out"], 1)
                pe.wait_ge(S["a5_free"], 1)
                pe.sem_inc(S["a5_free"], -1)
                for j in range(4):
                    o = A[5][r[j], (j // 2) * 64:(j // 2 + 1) * 64]
                    pe.matmul(o, TM[:, 2 + j // 2, r[j]], sa_s[:, 64 * j:64 * j + 64], start=True, stop=False)
                    ins = pe.matmul(o, TM[:, 4 + j // 2, r[j]], TM[:, j // 2, r[j]], start=False, stop=True)
                ins.then_inc(S["state_out"], 1)

            with pe.Fori(0, DEPTH) as layer:
                pe.wait_ge(S["x_ready"], 1)
                pe.sem_inc(S["x_ready"], -1)
                with pe.Fori(0, NW):
                    pe.wait_ge(S["g0_free"], 1)
                    pe.sem_inc(S["g0_free"], -1)
                    proj.channels(g0[:], proj.group(), X, KD, P, done="val_proj")
                    pe.wait_ge(S["g1_free"], 1)
                    pe.sem_inc(S["g1_free"], -1)
                    proj.channels(g1[:], proj.group(), X, KD, P, done="gate_proj")
                gates()
                for i in range(2):
                    for j in range(7):
                        pe.wait_ge(S[f"g{j % 2}_free"], 1)
                        pe.sem_inc(S[f"g{j % 2}_free"], -1)
                        proj.channels((g0, g1)[j % 2][:], proj.group(), X, KD, P,
                                      done="lat_proj" if j < 3 else "gate_proj")
                layer_norm([cacc[:, i, :] for i in range(NW)])
                total(A[2][:], [lsq[:, i, :] for i in range(3)], "lat_sq", "lat_sum")
                total(A[3][:], [lsq[:, i, :] for i in (3, 4)], "lat_sq", "lat_sum")
                pe.wait_ge(S["kr_pe"], 1)
                pe.sem_inc(S["kr_pe"], -1)
                pe.matmul(A[4][64:96, :], rotm[64:96, :], kr[64:96, :], start=True, stop=True).then_inc(S["k_rot"], 1)
                pe.wait_ge(S["lat_ready"], 1)
                pe.sem_inc(S["lat_ready"], -1)
                with pe.Fori(0, NW):
                    mla_pair()
                pe.wait_ge(S["mem_ready"], 1)
                pe.sem_inc(S["mem_ready"], -1)
                with pe.Fori(0, NW // 2):
                    mem = [y[:, 4:8, :].rearrange("p a (b m) -> p (a b) m", m=MEM) for y in (yh, yl)]
                    for a in range(2):
                        ga, gb = (g0, g1) if a == 0 else (g1, g0)
                        pe.wait_ge(S[f"g{a}_free"], 1)
                        pe.sem_inc(S[f"g{a}_free"], -1)
                        proj.channels(ga[:], proj.group(), X, KD, P, done="q_proj")
                        pe.wait_ge(S[f"g{1 - a}_free"], 1)
                        pe.sem_inc(S[f"g{1 - a}_free"], -1)
                        proj.channels(gb[:, 0:MEM], proj.group(), mem, KD, P, done="k_proj")
                        pe.wait_ge(S[f"g{a}_free"], 1)
                        pe.sem_inc(S[f"g{a}_free"], -1)
                        proj.channels(ga[:, 0:MEM], proj.group(), mem, KD, P, done="v_proj")
                        pe.wait_ge(S["qk_ready"], 1)
                        pe.sem_inc(S["qk_ready"], -1)
                        for b in range(2):
                            pe.wait_ge(S[f"a{3 * a + b}_free"], 1)
                            pe.sem_inc(S[f"a{3 * a + b}_free"], -1)
                            for t in (2 * b, 2 * b + 1):
                                ins = pe.matmul(A[3 * a + b][:, (t % 2) * MEM:(t % 2 + 1) * MEM],
                                                Qh[a][:, t * P:(t + 1) * P], Kh[a][:, 0:MEM], start=True, stop=True)
                            ins.then_inc(S["scores"], 1)
                        pe.wait_ge(S["v_raw"], 1)
                        pe.sem_inc(S["v_raw"], -1)
                        pe.wait_ge(S[f"a{3 * a + 2}_free"], 1)
                        pe.sem_inc(S[f"a{3 * a + 2}_free"], -1)
                        for t in range(2):
                            ins = pe.transpose(A[3 * a + 2][:, t * P:(t + 1) * P], PTh[a][:, 0, t * P:(t + 1) * P],
                                               ident[:])
                        ins.then_inc(S["v_turned"], 1)
                    for a in range(2):
                        pe.wait_ge(S["probs_ready"], 1)
                        pe.sem_inc(S["probs_ready"], -1)
                        for i in range(2):
                            pe.wait_ge(S[f"a{3 * a + i}_free"], 1)
                            pe.sem_inc(S[f"a{3 * a + i}_free"], -1)
                            for t in range(NT):
                                ins = pe.transpose(A[3 * a + i][:, t * P:(t + 1) * P],
                                                   xprobs[a][:, t, i * P:(i + 1) * P], ident[:])
                            ins.then_inc(S["probs_turned"], 1)
                        pe.wait_ge(S["v_ready"], 1)
                        pe.sem_inc(S["v_ready"], -1)
                        pe.wait_ge(S["weights_ready"], 1)
                        pe.sem_inc(S["weights_ready"], -1)
                        pe.wait_ge(S[f"a{3 * a + 2}_free"], 1)
                        pe.sem_inc(S[f"a{3 * a + 2}_free"], -1)
                        for i in range(2):
                            ins = pe.matmul(A[3 * a + 2][:], xV[a][:, i, :], PTh[a][:, i, :], start=i == 0,
                                            stop=i == 1)
                        ins.then_inc(S["head_out"], 1)
                with pe.Fori(0, 6):
                    for s, g in enumerate((g0, g1)):
                        pe.wait_ge(S[f"g{s}_free"], 1)
                        pe.sem_inc(S[f"g{s}_free"], -1)
                        proj.channels(g[:], proj.group(), X, KD, P, done="rw_proj")
                pe.wait_ge(S["g0_free"], 1)
                pe.sem_inc(S["g0_free"], -1)
                proj.channels(g0[:], proj.group(), X, NW, P, more=True)
                proj.channels(g0[:], proj.group(), X, NW, P, done="rw_proj", k0=NW, first=False)
                pe.wait_ge(S["wa_ready"], 1)
                pe.sem_inc(S["wa_ready"], -1)
                for i in range(NW):
                    pe.wait_ge(S["a0_free"], 1)
                    pe.sem_inc(S["a0_free"], -1)
                    pe.matmul(A[0][:], lora[0:64, i * P:(i + 1) * P], wa[0:64, :], start=True, stop=True)\
                      .then_inc(S["lora_w"], 1)
                    pe.wait_ge(S["a1_free"], 1)
                    pe.sem_inc(S["a1_free"], -1)
                    pe.matmul(A[1][:], lora[64:P, i * P:(i + 1) * P], wa[64:P, :], start=True, stop=True)\
                      .then_inc(S["lora_a"], 1)
                    pe.wait_ge(S["a2_free"], 1)
                    pe.sem_inc(S["a2_free"], -1)
                    total(A[2][:], [sq[:, 0, :]], "kk_sq", "kk_sum", halves)
                with pe.Fori(0, NT // 2) as cc:
                    for u in range(2):
                        chunk = cc * 2 + u
                        for g in range(2):
                            rwkv_half(g, chunk)
                for i in range(NW):
                    total(A[0][:], [R[:, i, :]], "gn_in", "gn_sum", halves)
                    total(A[1][:], [sq[:, 0, :]], "gn_sq", "gn_sumsq", halves)
                gates()
                pe.wait_ge(S["y_ready"], 1)
                pe.sem_inc(S["y_ready"], -1)
                with pe.Fori(0, 2):
                    for u in range(2):
                        merge(0)
                pe.wait_ge(S["merged_ready"], 1)
                pe.sem_inc(S["merged_ready"], -1)
                with pe.Fori(0, KD // 2):
                    for s, g in enumerate((g0, g1)):
                        pe.wait_ge(S[f"g{s}_free"], 1)
                        pe.sem_inc(S[f"g{s}_free"], -1)
                        proj.channels(g[:], proj.group(), (yh, yl), KD, P, done="out_proj")
                layer_norm([hT[:, i, :] for i in range(KD)])

        @block.scalar
        def _(act):
            round_next = rounder(act, S, stage, wh)
            half = lambda t, i: t[:, i:i + 1] if isinstance(i, int) else t[:, bass.ds(i, 1)]

            def op(ins, *names):
                fin(act, "act_self", ins, *names)

            def gates(n=2):
                with act.Fori(0, n):
                    for s, g in enumerate((g0, g1)):
                        round_next()
                        act.wait_ge(S["gate_proj"], 1)
                        act.sem_inc(S["gate_proj"], -1)
                        act.wait_ge(S[f"sq{s}_used"], 1)
                        act.sem_inc(S[f"sq{s}_used"], -1)
                        act.activation(sq[:, s, :], g[:], ACT.Tanh, scale=0.5).then_inc(S["tanh_ready"], 1)

            def root(src, n, e):
                act.activation(rstd[:], src, ACT.Sqrt, scale=1.0 / n, bias=eps[:, e:e + 1]).then_inc(S["root"], 1)

            def norm_squares(tiles, n):
                for i, t in enumerate(tiles):
                    act.wait_ge(S["centered"], 1)
                    act.sem_inc(S["centered"], -1)
                    act.wait_ge(S[f"sq{i % 2}_used"], 1)
                    act.sem_inc(S[f"sq{i % 2}_used"], -1)
                    act.activation(sq[:, i % 2, :], t, ACT.Square).then_inc(S[f"sq{i % 2}_ready"], 1)
                act.wait_ge(S["sq0_used"], 1)
                act.sem_inc(S["sq0_used"], -1)
                act.wait_ge(S["sq1_used"], 1)
                act.sem_inc(S["sq1_used"], -1)
                root(A[1][:], n, 0)
                give(act, "sq0_used", "sq1_used")

            def upper(dst, want, src=None, scale=1.0):
                act.wait_ge(S[want], 1)
                act.sem_inc(S[want], -1)
                act.activation(dst, src, ACT.Copy, scale=scale).then_inc(S["hi_ready"], 1)

            def mla_pair():
                for a in range(2):
                    round_next()
                    act.wait_ge(S["q_proj"], 1)
                    act.sem_inc(S["q_proj"], -1)
                    act.wait_ge(S[f"qk{a}_free"], 1)
                    act.sem_inc(S[f"qk{a}_free"], -1)
                    op(act.activation(Qh[a][0:96, :], g0[0:96, :], ACT.Copy, scale=-96 ** -0.5), "g0_free", "q_raw",
                       "q_dve")
                    act.wait_ge(S["kv_proj"], 1)
                    act.sem_inc(S["kv_proj"], -1)
                    act.wait_ge(S[f"v{a}_free"], 1)
                    act.sem_inc(S[f"v{a}_free"], -1)
                    op(act.activation(PTh[a][64:P, 0, :], g1[64:P, :], ACT.Copy), "v_raw")
                    op(act.activation(Kh[a][0:64, :], g1[0:64, :], ACT.Copy), "g1_free", "k_ready")
                for a in range(2):
                    act.wait_ge(S["v_turned"], 1)
                    act.sem_inc(S["v_turned"], -1)
                    op(act.activation(Vh[a].rearrange("p a b -> p (a b)"), A[4 + a][:, 0:256], ACT.Copy),
                       f"a{4 + a}_free", "v_ready")

                def exponential(a, t):
                    act.wait_ge(S["max_ready"], 1)
                    act.sem_inc(S["max_ready"], -1)
                    n, c = (t + 1) * P, 2 * a + t % 2
                    act.activation(probsh[a][t % 2][:, 0:n], probsh[a][t % 2][:, 0:n], ACT.Exp, scale=-1.0,
                                   bias=st[:, c:c + 1], accum_out=st[:, 4 + c:5 + c]).then_inc(S["exp_ready"], 1)

                exponential(0, 0)
                exponential(1, 0)
                for t in range(NT):
                    for a in range(2):
                        if t + 1 < NT:
                            exponential(a, t + 1)
                        n = (t + 1) * P
                        act.wait_ge(S["probs_turned"], 1)
                        act.sem_inc(S["probs_turned"], -1)
                        op(act.activation(PTh[a][:, 0:t + 1, t * P:n],
                                          A[2 + a][:, 0:n].rearrange("p (a b) -> p a b", b=P), ACT.Copy),
                           f"a{2 + a}_free", f"probs{a}{t % 2}_free", *(["weights_ready"] if t == NT - 1 else []))

            def merge(branch, d0):
                for s, g in enumerate((g0, g1)):
                    round_next()
                    act.wait_ge(S["merge_gate"], 1)
                    act.sem_inc(S["merge_gate"], -1)
                    act.wait_ge(S[f"sq{s}_used"], 1)
                    act.sem_inc(S[f"sq{s}_used"], -1)
                    op(act.activation(sq[:, s, :], g[:], ACT.Tanh, scale=0.5,
                                      bias=der[:, bass.ds(d0 + (32 + 8 * branch + s), 1)]), f"g{s}_free",
                       "tanh_ready")
                round_next()

            def merge_quarter(q, chunk):
                group, part = q // 4, q % 4
                branch, s = group // 3 + 1, group % 3
                if part == 0:
                    round_next()
                if part == 3 and s < 2:
                    act.wait_ge(S["merge_gate"], 1)
                    act.sem_inc(S["merge_gate"], -1)
                    act.wait_ge(S[f"sq{s}_used"], 1)
                    act.sem_inc(S[f"sq{s}_used"], -1)
                    op(act.activation(sq[:, s, :], (g0, g1)[s][:], ACT.Tanh, scale=0.5,
                                      bias=der[:, bass.ds(chunk * 2 + (32 + 8 * branch + s), 1)]), f"g{s}_free",
                       "tanh_ready")

            def rwkv_half(g, chunk):
                cs = bass.ds(chunk * P, P)
                act.wait_ge(S["qd_ready"], 1)
                act.sem_inc(S["qd_ready"], -1)
                act.activation(emid[:, 0:2], QC[:, :, 64], ACT.Exp, scale=-KAPPA)
                act.activation(EP[:, :, :], QD[:, :, :], ACT.Exp, scale=-KAPPA)
                act.activation(EM[:, :, :], QD[:, :, 1:], ACT.Exp, scale=KAPPA)
                op(act.activation(Vc[:, :, :], RV[:, 2 * g:2 * g + 2, cs], ACT.Copy), "exp_ready")
                for q in range(6):
                    merge_quarter(18 * g + q, chunk)
                act.wait_ge(S["turned"], 1)
                act.sem_inc(S["turned"], -1)
                op(act.activation(TM[:, 0:4, :].rearrange("p a b -> p (a b)"), A[0][:], ACT.Copy), "a0_free")
                act.wait_ge(S["turned"], 1)
                act.sem_inc(S["turned"], -1)
                op(act.activation(TM[:, 4:6, :].rearrange("p a b -> p (a b)"), A[1][:, 0:256], ACT.Copy),
                   "bonus_sum", "turned_ready")
                for n in range(1, 7):
                    act.wait_ge(S["uz_out"], 1)
                    act.sem_inc(S["uz_out"], -1)
                    op(act.activation(Qs[:, :, :].rearrange("p a b -> p (a b)"), A[4][:], ACT.Copy), "a4_free",
                       "uz_ready")
                    merge_quarter(18 * g + 4 + 2 * n, chunk)
                    merge_quarter(18 * g + 5 + 2 * n, chunk)
                for p in range(2):
                    act.wait_ge(S["rhs_out"], 1)
                    act.sem_inc(S["rhs_out"], -1)
                    op(act.activation(rhs_s.rearrange("p (a b) -> p a b", b=64)[:, p:4:2, :],
                                      A[2 + p][:, 0:P].rearrange("p (a b) -> p a b", b=64), ACT.Copy),
                       f"a{2 + p}_free", *(["rhs_ready"] if p else []))
                act.wait_ge(S["sa_out"], 1)
                act.sem_inc(S["sa_out"], -1)
                op(act.activation(sa_s, A[0][:, 0:256], ACT.Copy), "a0_free", "sa_ready")
                act.wait_ge(S["y_out"], 1)
                act.sem_inc(S["y_out"], -1)
                op(act.activation(R[:, 2 * g:2 * g + 2, cs], A[4][:, 0:256].rearrange("p (a b) -> p a b", b=P),
                                  ACT.Copy), "a4_free", "y_written")

            act.dma_start(hT[:], x_dram.rearrange("(k p) t -> p k t", p=P)).then_inc(S["x_in"], 16)
            act.wait_ge(S["x_in"], 16)
            act.sem_inc(S["x_in"], -16)
            give(act, "sq0_used", "sq1_used")
            act.activation(xh[:], hT[:], ACT.Copy).then_inc(S["hi_ready"], 1)
            act.wait_ge(S["consts_act"], 1)
            act.sem_inc(S["consts_act"], -1)
            round_next()
            with act.Fori(0, DEPTH) as layer:
                act.wait_ge(S["par_free"], 1)
                act.sem_inc(S["par_free"], -1)
                act.dma_start(par[:], par_dram[bass.ds(layer, 1)].rearrange("a p n -> p (a n)"))\
                   .then_inc(S["par_full"], 16)
                act.wait_ge(S["par_full"], 16)
                act.sem_inc(S["par_full"], -16)
                give(act, "par_dve")
                act.wait_ge(S["derived"], 1)
                act.sem_inc(S["derived"], -1)
                with act.Fori(0, NW):
                    round_next()
                    round_next()
                    act.wait_ge(S["gate_proj"], 1)
                    act.sem_inc(S["gate_proj"], -1)
                    act.wait_ge(S["sq0_used"], 1)
                    act.sem_inc(S["sq0_used"], -1)
                    act.activation(sq[:, 0, :], g1[:], ACT.Tanh, scale=0.5).then_inc(S["tanh_ready"], 1)
                gates()
                for i in range(2):
                    for j in range(7):
                        g = (g0, g1)[j % 2]
                        round_next()
                        if j < 3:
                            n = 3 * i + j
                            act.wait_ge(S["lat_proj"], 1)
                            act.sem_inc(S["lat_proj"], -1)
                            if n < 5:
                                op(act.activation(lsq[:, n, :], g[:], ACT.Square),
                                   *(["lat_sq"] if n in (2, 4) else []))
                            op(act.activation(lat[:, n, :] if n < 5 else kr, g[:], ACT.Copy), f"g{j % 2}_free",
                               *(["kr_pe", "kr_dve"] if n == 5 else []))
                        else:
                            act.wait_ge(S["gate_proj"], 1)
                            act.sem_inc(S["gate_proj"], -1)
                            act.wait_ge(S[f"sq{j % 2}_used"], 1)
                            act.sem_inc(S[f"sq{j % 2}_used"], -1)
                            act.activation(sq[:, j % 2, :], g[:], ACT.Tanh, scale=0.5).then_inc(S["tanh_ready"], 1)
                norm_squares([cacc[:, i, :] for i in range(NW)], W)
                for i in range(NW):
                    act.wait_ge(S["scaled"], 1)
                    act.sem_inc(S["scaled"], -1)
                    op(act.activation(cacc[:, i, :], cacc[:, i, :], ACT.Identity, scale=col("cln_g", i),
                                      bias=col("cln_b", i)))
                    act.wait_ge(S[f"sq{i % 2}_used"], 1)
                    act.sem_inc(S[f"sq{i % 2}_used"], -1)
                    act.activation(sq[:, i % 2, :], cacc[:, i, :], ACT.Tanh, scale=0.5)\
                       .then_inc(S["tanh_ready"], 1)
                    upper(yh[:, i, :], "tmp_ready", tmp[:, i % 2, :])
                act.dma_start(posb[64:96, :].bitcast(I32), bass.AP(pos_dram.tensor, pos_dram.offset, [[0, 32], [1, T]])).then_inc(S["pos_in"], 16)
                act.wait_ge(S["pos_in"], 16)
                act.sem_inc(S["pos_in"], -16)
                give(act, "pos_dve")
                act.wait_ge(S["angle"], 1)
                act.sem_inc(S["angle"], -1)
                op(act.activation(trig[64:96, 1, :], posb[64:96, :], ACT.Sin))
                op(act.activation(trig[64:96, 0, :], posb[64:96, :], ACT.Abs))
                op(act.activation(trig[64:96, 0, :], trig[64:96, 0, :], ACT.Sin, scale=-1.0, bias=eps[64:96, 3:4]),
                   "trig_ready")
                for n, i0, count in ((384, 0, 3), (256, 3, 2)):
                    act.wait_ge(S["lat_sum"], 1)
                    act.sem_inc(S["lat_sum"], -1)
                    root(A[2 + (n == 256)][:], n, 1)
                    for i in range(i0, i0 + count):
                        upper(yh[:, (4 if i < 3 else 5) + i, :], "tmp_ready", tmp[:, i % 2, :])
                with act.Fori(0, NW):
                    mla_pair()
                act.dma_start(memf, mem_dram.rearrange("(k p) m -> p k m", p=P)).then_inc(S["mem_in"], 16)
                upper(yh[:, 8:12, :], "y32_ready", y32)
                act.wait_ge(S["mem_in"], 16)
                act.sem_inc(S["mem_in"], -16)
                act.activation(yh[:, 4:8, :].rearrange("p a t -> p (a t)"), memf.rearrange("p a t -> p (a t)"),
                               ACT.Copy).then_inc(S["hi_ready"], 1)
                with act.Fori(0, NW // 2):
                    def turned(a):
                        for i in range(2):
                            act.wait_ge(S["probs_turned"], 1)
                            act.sem_inc(S["probs_turned"], -1)
                            op(act.activation(PTh[a][:, i, :], A[3 * a + i][:], ACT.Copy), f"a{3 * a + i}_free",
                               *(["weights_ready"] if i else []))

                    for a in range(2):
                        ga, gb = (g0, g1) if a == 0 else (g1, g0)
                        round_next()
                        act.wait_ge(S["q_proj"], 1)
                        act.sem_inc(S["q_proj"], -1)
                        act.wait_ge(S[f"qk{a}_free"], 1)
                        act.sem_inc(S[f"qk{a}_free"], -1)
                        op(act.activation(Qh[a], ga[:], ACT.Copy, scale=-128 ** -0.5), f"g{a}_free")
                        round_next()
                        act.wait_ge(S["k_proj"], 1)
                        act.sem_inc(S["k_proj"], -1)
                        op(act.activation(Kh[a][:, 0:MEM], gb[:, 0:MEM], ACT.Copy), f"g{1 - a}_free", "qk_ready")
                        round_next()
                        act.wait_ge(S["v_proj"], 1)
                        act.sem_inc(S["v_proj"], -1)
                        act.wait_ge(S[f"v{a}_free"], 1)
                        act.sem_inc(S[f"v{a}_free"], -1)
                        op(act.activation(PTh[a][:, 0, 0:MEM], ga[:, 0:MEM], ACT.Copy), f"g{a}_free", "v_raw")
                        act.wait_ge(S["v_turned"], 1)
                        act.sem_inc(S["v_turned"], -1)
                        op(act.activation(xV[a].rearrange("p a b -> p (a b)"), A[3 * a + 2][:, 0:MEM], ACT.Copy),
                           f"a{3 * a + 2}_free", "v_ready")
                        if a:
                            turned(0)
                        for b in range(2):
                            act.wait_ge(S["max_ready"], 1)
                            act.sem_inc(S["max_ready"], -1)
                            for t in (2 * b, 2 * b + 1):
                                ins = act.activation(xprobs[a][:, t, :],
                                                     A[3 * a + b][:, (t % 2) * MEM:(t % 2 + 1) * MEM], ACT.Exp,
                                                     scale=-1.0, bias=st[:, t:t + 1], accum_out=st[:, 4 + t:5 + t])
                            op(ins, f"a{3 * a + b}_free", *(["exp_ready"] if b else []))
                    turned(1)
                upper(yh[:, 4:8, :], "y32_ready", y32)
                act.wait_ge(S["y32_free"], 1)
                act.sem_inc(S["y32_free"], -1)
                with act.Fori(0, 6) as i:
                    for s, g in enumerate((g0, g1)):
                        round_next()
                        act.wait_ge(S["rw_proj"], 1)
                        act.sem_inc(S["rw_proj"], -1)
                        op(act.activation(tile(RKV, i * 2 + s), g[:], ACT.Copy, scale=half(der, i * 2 + s)),
                           "part_ready")
                round_next()
                round_next()
                act.wait_ge(S["rw_proj"], 1)
                act.sem_inc(S["rw_proj"], -1)
                op(act.activation(wa, g0[:], ACT.Copy, scale=der[:, 12:13]), "part_ready")
                act.dma_start(lora, lora_dram[bass.ds(layer, 1)].rearrange("a p n -> p (a n)"))\
                   .then_inc(S["lora_in"], 16)
                act.wait_ge(S["lora_in"], 16)
                act.sem_inc(S["lora_in"], -16)
                act.wait_ge(S["wa_mixed"], 1)
                act.sem_inc(S["wa_mixed"], -1)
                op(act.activation(wa[0:64, :], wa[0:64, :], ACT.Tanh), "wa_ready")
                for i in range(NW):
                    act.wait_ge(S["lora_w"], 1)
                    act.sem_inc(S["lora_w"], -1)
                    op(act.activation(TH[:, i, :], A[0][:], ACT.Tanh, scale=0.5, bias=der[:, 13 + i:14 + i]),
                       "a0_free")
                    act.wait_ge(S["lora_a"], 1)
                    act.sem_inc(S["lora_a"], -1)
                    op(act.activation(BB[:, i, :], A[1][:], ACT.Tanh, scale=0.5, bias=der[:, 17 + i:18 + i]),
                       "a1_free", "a_ready")
                    act.wait_ge(S["kk_ready"], 1)
                    act.sem_inc(S["kk_ready"], -1)
                    act.wait_ge(S["sq0_used"], 1)
                    act.sem_inc(S["sq0_used"], -1)
                    act.activation(sq[:, 0, :], KK[:, i, :], ACT.Square).then_inc(S["kk_sq"], 1)
                    act.wait_ge(S["kk_sum"], 1)
                    act.sem_inc(S["kk_sum"], -1)
                    act.activation(rstd[:], A[2][:], ACT.Sqrt).then_inc(S["root"], 1)
                    give(act, "sq0_used")
                with act.Fori(0, NT // 2) as cc:
                    for u in range(2):
                        chunk = cc * 2 + u
                        for g in range(2):
                            rwkv_half(g, chunk)
                for i in range(NW):
                    act.wait_ge(S["centered"], 1)
                    act.sem_inc(S["centered"], -1)
                    act.wait_ge(S["sq0_used"], 1)
                    act.sem_inc(S["sq0_used"], -1)
                    act.activation(sq[:, 0, :], R[:, i, :], ACT.Square).then_inc(S["gn_sq"], 1)
                    act.wait_ge(S["gn_sumsq"], 1)
                    act.sem_inc(S["gn_sumsq"], -1)
                    root(A[1][:], 64, 2)
                    give(act, "sq0_used")
                    act.wait_ge(S["scaled"], 1)
                    act.sem_inc(S["scaled"], -1)
                    act.activation(R[:, i, :], R[:, i, :], ACT.Identity, scale=col("lnx_g", i),
                                   bias=col("lnx_b", i)).then_inc(S["affine"], 1)
                gates()
                upper(yh[:, 0:4, :], "y32_ready", R)
                with act.Fori(0, 2) as i:
                    for u in range(2):
                        merge(0, i * 4 + 2 * u)
                upper(yh[:, 0:8, :], "y32_ready", hT[:], 0.5)
                with act.Fori(0, KD // 2):
                    round_next()
                    round_next()
                norm_squares([hT[:, i, :] for i in range(KD)], D)
                for i in range(KD):
                    act.wait_ge(S["scaled"], 1)
                    act.sem_inc(S["scaled"], -1)
                    op(act.activation(hT[:, i, :], hT[:, i, :], ACT.Identity, scale=col("ln_g", i),
                                      bias=col("ln_b", i)))
                    act.activation(xh[:, i, :], hT[:, i, :], ACT.Copy).then_inc(S["hi_ready"], 1)

        @block.vector
        def _(dve):
            def op(ins, *names):
                fin(dve, "dve_self", ins, *names)

            def stt(out, in0, scalar, in1, op0, op1, *names):
                op(dve.scalar_tensor_tensor(out=out, in0=in0, scalar=scalar, in1=in1, op0=op0, op1=op1), *names)

            def tt(out, a, b, alu, *names):
                op(dve.tensor_tensor(out, a, b, alu), *names)

            def ts(out, a, s1, s2, op0, op1, *names):
                op(dve.tensor_scalar(out, a, s1, s2, op0, op1) if s2 is not None
                   else dve.tensor_scalar(out, a, s1, None, op0), *names)

            def spread(v, n):
                return bass.AP(v.tensor, v.offset, [*v.ap, [0, n]])

            def again(v, n):
                return bass.AP(v.tensor, v.offset, [v.ap[0], [0, n], *v.ap[1:]])

            def gates(dst):
                with dve.Fori(0, NW // 2) as i:
                    for s, g in enumerate((g0, g1)):
                        dve.wait_ge(S["tanh_ready"], 1)
                        dve.sem_inc(S["tanh_ready"], -1)
                        stt(tile(dst, i * 2 + s), sq[:, s, :], 1.0, g[:], ALU.add, ALU.mult, f"g{s}_free",
                            f"sq{s}_used")

            def lower(h, lo, src, *names, scale=None):
                dve.wait_ge(S["hi_ready"], 1)
                dve.sem_inc(S["hi_ready"], -1)
                if scale is None:
                    tt(lo, src, h.bitcast(F32), ALU.subtract, *names)
                else:
                    stt(lo, src, scale, h.bitcast(F32), ALU.mult, ALU.subtract, *names)

            def layer_norm(tiles, n):
                give(dve, "ln_in")
                dve.wait_ge(S["ln_sum"], 1)
                dve.sem_inc(S["ln_sum"], -1)
                for t in tiles:
                    stt(t, A[0][:], -1.0 / n, t, ALU.mult, ALU.add, "centered")
                dve.wait_ge(S["root"], 1)
                dve.sem_inc(S["root"], -1)
                op(dve.reciprocal(rstd[:], rstd[:]))
                for t in tiles:
                    tt(t, t, rstd[:], ALU.mult, "scaled")

            def mla_pair(i):
                for a in range(2):
                    dve.wait_ge(S["q_dve"], 1)
                    dve.sem_inc(S["q_dve"], -1)
                    dve.wait_ge(S["q_rot"], 1)
                    dve.sem_inc(S["q_rot"], -1)
                    q = Qh[a][64:96, :]
                    tt(tmp[64:96, 1, :], q, trig[64:96, 0, :], ALU.mult)
                    tt(tmp[64:96, 0, :], A[2 + a][64:96, :], trig[64:96, 1, :], ALU.mult, f"a{2 + a}_free")
                    tt(q, tmp[64:96, 1, :], tmp[64:96, 0, :], ALU.add, "qk_ready")

                def maximum(a, t):
                    n, c = (t + 1) * P, 2 * a + t % 2
                    dve.wait_ge(S["scores"], 1)
                    dve.sem_inc(S["scores"], -1)
                    dve.wait_ge(S[f"probs{a}{t % 2}_free"], 1)
                    dve.sem_inc(S[f"probs{a}{t % 2}_free"], -1)
                    op(dve.tensor_tensor_reduce(probsh[a][t % 2][:, 0:n], A[a][:, 0:n], causal[:, T - n:T], 1.0,
                                                3e38, ALU.add, ALU.min, st[:, c:c + 1]),
                       f"a{a}_free", "max_ready", *([f"qk{a}_free"] if t == NT - 1 else []))

                maximum(0, 0)
                maximum(1, 0)
                for t in range(NT):
                    for a in range(2):
                        if t + 1 < NT:
                            maximum(a, t + 1)
                        n, c = (t + 1) * P, 4 + 2 * a + t % 2
                        dve.wait_ge(S["exp_ready"], 1)
                        dve.sem_inc(S["exp_ready"], -1)
                        op(dve.reciprocal(st[:, 8:9], st[:, c:c + 1]))
                        ts(probsh[a][t % 2][:, 0:n], probsh[a][t % 2][:, 0:n], st[:, 8:9], None, ALU.mult, None,
                           "probs_ready")
                for a in range(2):
                    rows = slice(64 * a, 64 * a + 64)
                    dve.wait_ge(S["head_out"], 1)
                    dve.sem_inc(S["head_out"], -1)
                    stt(y32[rows, bass.ds(i, 1), :].rearrange("p a t -> p (a t)"), A[4 + a][rows, :], 0.5,
                        mgate[rows, bass.ds(i, 1), :].rearrange("p a t -> p (a t)"), ALU.mult, ALU.mult,
                        f"a{4 + a}_free", f"v{a}_free")

            def merge(d0):
                for s, g in enumerate((g0, g1)):
                    dve.wait_ge(S["tanh_ready"], 1)
                    dve.sem_inc(S["tanh_ready"], -1)
                    dve.wait_ge(S["merge_proj"], 1)
                    dve.sem_inc(S["merge_proj"], -1)
                    h = tile(hT, d0 + s)
                    stt(sq[:, s, :], sq[:, s, :], 1.0, g[:], ALU.add, ALU.mult, f"g{s}_free")
                    tt(h, h, sq[:, s, :], ALU.add, f"sq{s}_used")

            def merge_quarter(q, chunk):
                group, part = q // 4, q % 4
                if group % 3 < 2 or part % 2 == 0:
                    return
                s = part // 2
                g = (g0, g1)[s]
                dve.wait_ge(S["tanh_ready"], 1)
                dve.sem_inc(S["tanh_ready"], -1)
                dve.wait_ge(S["merge_proj"], 1)
                dve.sem_inc(S["merge_proj"], -1)
                h = tile(hT, chunk * 2 + s)
                if group < 3:
                    stt(h, sq[:, s, :], 1.0, g[:], ALU.add, ALU.mult, f"g{s}_free", f"sq{s}_used")
                else:
                    stt(sq[:, s, :], sq[:, s, :], 1.0, g[:], ALU.add, ALU.mult, f"g{s}_free")
                    tt(h, h, sq[:, s, :], ALU.add, f"sq{s}_used")

            def rwkv_half(g, chunk):
                cs = bass.ds(chunk * P, P)
                two = slice(2 * g, 2 * g + 2)
                for i in range(2):
                    op(dve.tensor_tensor_scan(QC[:, i, 1:], TH[:, 2 * g + i, cs], ones[:], 0.0, ALU.add, ALU.add))
                mid = QC[:, :, 64]
                tt(QD[:, :, :], QC[:, :, :], spread(mid, P + 1), ALU.subtract, "qd_ready")
                dve.wait_ge(S["exp_ready"], 1)
                dve.sem_inc(S["exp_ready"], -1)
                for i in range(2):
                    ts(Sm[:, i, :], St[:, 2 * g + i, :], emid[:, i:i + 1], None, ALU.mult, None)
                stt(AR[:, :, 0, :], KK[:, two, cs], -1.0, EP[:, :, 0:P], ALU.mult, ALU.mult)
                tt(AR[:, :, 1, :], R[:, two, cs], EP[:, :, 1:], ALU.mult)
                stt(Bt[:, :, :], BB[:, two, cs], 0.5, EM[:, :, :], ALU.mult, ALU.mult)
                tt(Kt[:, :, :], RK_[:, two, cs], EM[:, :, :], ALU.mult)
                tt(rkc, R[:, two, cs], RK_[:, two, cs], ALU.mult)
                tt(rkc, rkc, spread(col("r_k", 2 * g, 2), P), ALU.mult, "ab_ready")
                for q in range(6):
                    merge_quarter(18 * g + q, chunk)
                a2 = after[:, :, :].rearrange("p a b -> p (a b)")
                for j in range(4):
                    dve.wait_ge(S["um_out"], 1)
                    dve.sem_inc(S["um_out"], -1)
                    tt(UM[:, j, :].rearrange("p (a b) -> p a b", a=2), A[j][:].rearrange("p (a b) -> p a b", a=2),
                       again(a2, 2), ALU.mult, f"a{j}_free")
                for p in range(2):
                    dve.wait_ge(S["t_out"], 1)
                    dve.sem_inc(S["t_out"], -1)
                    tt(Tm[:, p:4:2, :], A[4 + p][:, 0:256].rearrange("p (a b) -> p a b", a=2), again(before[:], 2),
                       ALU.mult, f"a{4 + p}_free")
                op(dve.tensor_copy(XZ[:, :, :, :].rearrange("p a b c -> p (a b) c"), again(ident[:], 8)))
                op(dve.copy_predicated(XZ[:, :, 0, :], again(level[:, 0, 0, :], 4), Tm[:, :, :]))
                op(dve.copy_predicated(XZ[:, :, 1, :], again(level[:, 0, 1, :], 4), UM[:, :, 0:P]), "xz_ready")
                dve.wait_ge(S["bonus_sum"], 1)
                dve.sem_inc(S["bonus_sum"], -1)
                tt(RK_[:, two, cs], A[1][:, 256:512].rearrange("p (a b) -> p a b", a=2), Vc[:, :, :], ALU.mult,
                   "a1_free")
                for n in range(1, 7):
                    m = level[:, n, :, :].rearrange("p a b -> p (a b)")
                    merge_quarter(18 * g + 4 + 2 * n, chunk)
                    for p, b in ((0, 5), (1, 3)):
                        dve.wait_ge(S["fill_out"], 1)
                        dve.sem_inc(S["fill_out"], -1)
                        op(dve.copy_predicated(XZ[:, 2 * p:2 * p + 2, :, :].rearrange("p a b c -> p a (b c)"),
                                               again(m, 2), A[b][:].rearrange("p (a b) -> p a b", a=2)),
                           f"a{b}_free", *(["xz_ready"] if p else []))
                    merge_quarter(18 * g + 5 + 2 * n, chunk)
                dve.wait_ge(S["y_written"], 1)
                dve.sem_inc(S["y_written"], -1)
                dve.wait_ge(S["state_out"], 1)
                dve.sem_inc(S["state_out"], -1)
                tt(Sm[:, :, :], A[5][:, 0:P].rearrange("p (a b) -> p a b", b=64), Sm[:, :, :], ALU.add, "a5_free")
                for i in range(2):
                    ts(St[:, 2 * g + i, :], Sm[:, i, :], EP[:, i, P:P + 1], None, ALU.mult, None)

            for n, v in enumerate((1e-5, 1e-6, 64e-5, math.pi / 2)):
                op(dve.memset(eps[:, n:n + 1], v))
            lower(xh[:], xl[:], hT[:], "x_ready")
            dve.wait_ge(S["consts_dve"], 1)
            dve.sem_inc(S["consts_dve"], -1)
            give(dve, "g0_free", "g1_free", "par_free", "qk0_free", "qk1_free", "v0_free", "v1_free",
                 "probs00_free", "probs01_free", "probs10_free", "probs11_free",
                 *(f"a{i}_free" for i in range(6)))
            with dve.Fori(0, DEPTH) as layer:
                dve.wait_ge(S["par_dve"], 1)
                dve.sem_inc(S["par_dve"], -1)
                ts(der[:, 0:13], col("mu", 0, 13), -1.0, 1.0, ALU.mult, ALU.add)
                ts(der[:, 13:17], col("w0", 0, 4), 0.5, None, ALU.mult, None)
                ts(der[:, 17:21], col("a0", 0, 4), 0.5, None, ALU.mult, None)
                ts(der[:, 21:25], col("k_a", 0, 4), 0.5, None, ALU.mult, None)
                ts(der[:, 25:29], col("k_a", 0, 4), -0.5, 1.0, ALU.mult, ALU.add)
                ts(der[:, 32:64], col("b_gate", 0, 32), 0.5, None, ALU.mult, None, "derived")
                op(dve.memset(hb[:, :, 0:TAPS - 1], 0.0))
                with dve.Fori(0, NW) as i:
                    dve.wait_ge(S["val_proj"], 1)
                    dve.sem_inc(S["val_proj"], -1)
                    dve.wait_ge(S["tanh_ready"], 1)
                    dve.sem_inc(S["tanh_ready"], -1)
                    stt(hb[:, bass.ds(i, 1), TAPS - 1:TAPS - 1 + T].rearrange("p a t -> p (a t)"), sq[:, 0, :], 1.0,
                        g0[:], ALU.add, ALU.mult, "g0_free", "g1_free", "sq0_used")
                gates(cgate)
                with dve.Fori(0, NW // 2) as i:
                    for k in range(TAPS):
                        for s in range(2):
                            src = hb[:, bass.ds(i * 2 + s, 1), k:k + T].rearrange("p a t -> p (a t)")
                            w = col("conv_w", (i * 2 + s) * TAPS + k)
                            dst = tile(cacc, i * 2 + s)
                            if s == 0 and k in (15, 19, 23, 27):
                                j = (k - 15) // 4
                                u = (j + 1) % 2
                                dve.wait_ge(S["tanh_ready"], 1)
                                dve.sem_inc(S["tanh_ready"], -1)
                                stt(tile((mgate, xgate)[j % 2], i * 2 + j // 2), sq[:, u, :], 1.0, (g0, g1)[u][:],
                                    ALU.add, ALU.mult, f"g{u}_free", f"sq{u}_used")
                            if k == 0:
                                dve.tensor_scalar(dst, src, w, None, ALU.mult).then_inc(S["tap"], 1)
                            else:
                                dve.wait_ge(S["tap"], 1)
                                dve.sem_inc(S["tap"], -1)
                                dve.scalar_tensor_tensor(out=dst, in0=src, scalar=w, in1=dst, op0=ALU.mult,
                                                         op1=ALU.add).then_inc(S["tap"], 1)
                    dve.wait_ge(S["tap"], 2)
                    dve.sem_inc(S["tap"], -2)
                    for s in range(2):
                        dst = tile(cacc, i * 2 + s)
                        ts(dst, dst, 0.5, col("conv_b", i * 2 + s), ALU.mult, ALU.add)
                layer_norm([cacc[:, i, :] for i in range(NW)], W)
                for i in range(NW):
                    t = tmp[:, i % 2, :]
                    dve.wait_ge(S["tanh_ready"], 1)
                    dve.sem_inc(S["tanh_ready"], -1)
                    stt(t, sq[:, i % 2, :], 1.0, cacc[:, i, :], ALU.add, ALU.mult, f"sq{i % 2}_used")
                    stt(t, t, 0.25, cgate[:, i, :], ALU.mult, ALU.mult, "tmp_ready")
                    lower(yh[:, i, :], yl[:, i, :], t)
                dve.wait_ge(S["pos_dve"], 1)
                dve.sem_inc(S["pos_dve"], -1)
                ang, red = posb[64:96, :], trig[64:96, 1, :]
                op(dve.tensor_copy(red, ang.bitcast(I32)))
                ts(ang, red, par[64:96, PC1["inv_freq"][0]:PC1["inv_freq"][0] + 1], None, ALU.mult, None)
                magic, part1, part2 = 1.5 * 2 ** 23, 6.28125, 8117 / 2 ** 22
                ts(red, ang, 1 / (2 * math.pi), magic, ALU.mult, ALU.add)
                ts(red, red, -magic, None, ALU.add, None)
                for part in (part1, part2, 2 * math.pi - part1 - part2):
                    stt(ang, red, -part, ang, ALU.mult, ALU.add)
                ts(ang, ang, 3.1415925, -3.1415925, ALU.min, ALU.max, "angle")
                for i0, count, gain in ((0, 3, "q_norm"), (3, 2, "kv_norm")):
                    dve.wait_ge(S["root"], 1)
                    dve.sem_inc(S["root"], -1)
                    op(dve.reciprocal(rstd[:], rstd[:]))
                    for i in range(i0, i0 + count):
                        t, y = tmp[:, i % 2, :], (4 if i < 3 else 5) + i
                        stt(t, lat[:, i, :], col(gain, i - i0), rstd[:], ALU.mult, ALU.mult, "tmp_ready")
                        lower(yh[:, y, :], yl[:, y, :], t)
                dve.wait_ge(S["trig_ready"], 1)
                dve.sem_inc(S["trig_ready"], -1)
                dve.wait_ge(S["kr_dve"], 1)
                dve.sem_inc(S["kr_dve"], -1)
                dve.wait_ge(S["k_rot"], 1)
                dve.sem_inc(S["k_rot"], -1)
                tt(tmp[64:96, 1, :], kr[64:96, :], trig[64:96, 0, :], ALU.mult)
                tt(tmp[64:96, 0, :], A[4][64:96, :], trig[64:96, 1, :], ALU.mult)
                tt(K[64:96, :], tmp[64:96, 1, :], tmp[64:96, 0, :], ALU.add)
                ts(Kh[1][64:96, :], K[64:96, :], 1.0, None, ALU.mult, None, "lat_ready")
                op(dve.memset(causal[:, 0:T - P], 0.0))
                ts(causal[:, T - P:T], future[:], -1.0, None, ALU.mult, None)
                with dve.Fori(0, NW) as i:
                    mla_pair(i)
                give(dve, "y32_ready")
                lower(yh[:, 8:12, :], yl[:, 8:12, :], y32)
                dve.wait_ge(S["hi_ready"], 1)
                dve.sem_inc(S["hi_ready"], -1)
                op(dve.tensor_tensor(yl[:, 4:8, :].rearrange("p a t -> p (a t)"),
                                     memf.rearrange("p a t -> p (a t)"),
                                     yh[:, 4:8, :].rearrange("p a t -> p (a t)").bitcast(F32), ALU.subtract),
                   "mem_ready")
                with dve.Fori(0, NW // 2) as i:
                    for a in range(2):
                        for b in range(2):
                            dve.wait_ge(S["scores"], 1)
                            dve.sem_inc(S["scores"], -1)
                            op(dve.tensor_reduce(st[:, 2 * b:2 * b + 2],
                                                 A[3 * a + b][:].rearrange("p (a m) -> p a m", a=2), AX, ALU.min),
                               "max_ready")
                        dve.wait_ge(S["exp_ready"], 1)
                        dve.sem_inc(S["exp_ready"], -1)
                        op(dve.reciprocal(st[:, 12:16], st[:, 4:8]))
                        tt(xprobs[a], xprobs[a], spread(st[:, 12:16], MEM), ALU.mult, "probs_ready")
                    for a in range(2):
                        dve.wait_ge(S["head_out"], 1)
                        dve.sem_inc(S["head_out"], -1)
                        stt(tile(y32, i * 2 + a), A[3 * a + 2][:], 0.5, tile(xgate, i * 2 + a), ALU.mult, ALU.mult,
                            f"a{3 * a + 2}_free", f"qk{a}_free", f"v{a}_free")
                give(dve, "y32_ready")
                lower(yh[:, 4:8, :], yl[:, 4:8, :], y32, "y32_free")
                with dve.Fori(0, 6) as i:
                    for s, g in enumerate((g0, g1)):
                        dve.wait_ge(S["part_ready"], 1)
                        dve.sem_inc(S["part_ready"], -1)
                        t = RKV[:, bass.ds(i * 2 + s, 1), 1:T].rearrange("p a t -> p (a t)")
                        stt(t, g[:, 0:T - 1], col("mu", i * 2 + s), t, ALU.mult, ALU.add, f"g{s}_free")
                dve.wait_ge(S["part_ready"], 1)
                dve.sem_inc(S["part_ready"], -1)
                stt(wa[:, 1:T], g0[:, 0:T - 1], col("mu", 12), wa[:, 1:T], ALU.mult, ALU.add, "g0_free", "wa_mixed")
                for i in range(NW):
                    ts(KK[:, i, :], RK_[:, i, :], col("k_k", i), None, ALU.mult, None, "kk_ready")
                    dve.wait_ge(S["a_ready"], 1)
                    dve.sem_inc(S["a_ready"], -1)
                    ts(tmp[:, 0, :], BB[:, i, :], der[:, 21 + i:22 + i], der[:, 25 + i:26 + i], ALU.mult, ALU.add)
                    tt(RK_[:, i, :], RK_[:, i, :], tmp[:, 0, :], ALU.mult)
                    dve.wait_ge(S["root"], 1)
                    dve.sem_inc(S["root"], -1)
                    ts(rstd[:], rstd[:], 1e-12, None, ALU.max, None)
                    op(dve.reciprocal(rstd[:], rstd[:]))
                    tt(KK[:, i, :], KK[:, i, :], rstd[:], ALU.mult)
                    stt(BB[:, i, :], BB[:, i, :], 1.0, KK[:, i, :], ALU.add, ALU.mult, "a2_free")
                op(dve.memset(St[:, :, :], 0.0))
                op(dve.memset(QC[:, :, 0:1], 0.0))
                with dve.Fori(0, NT // 2) as cc:
                    for u in range(2):
                        chunk = cc * 2 + u
                        for g in range(2):
                            rwkv_half(g, chunk)
                for i in range(NW):
                    give(dve, "gn_in")
                    dve.wait_ge(S["gn_sum"], 1)
                    dve.sem_inc(S["gn_sum"], -1)
                    stt(R[:, i, :], A[0][:], -1.0 / 64, R[:, i, :], ALU.mult, ALU.add, "centered")
                    dve.wait_ge(S["root"], 1)
                    dve.sem_inc(S["root"], -1)
                    op(dve.reciprocal(rstd[:], rstd[:]))
                    tt(R[:, i, :], R[:, i, :], rstd[:], ALU.mult, "scaled")
                    dve.wait_ge(S["affine"], 1)
                    dve.sem_inc(S["affine"], -1)
                    tt(R[:, i, :], R[:, i, :], RK_[:, i, :], ALU.add)
                gates(rgate)
                stt(R, R, 0.5, rgate[:, :, :], ALU.mult, ALU.mult, "y32_ready")
                lower(yh[:, 0:4, :], yl[:, 0:4, :], R, "y_ready")
                with dve.Fori(0, 2) as i:
                    for u in range(2):
                        merge(i * 4 + 2 * u)
                give(dve, "y32_ready")
                lower(yh[:, 0:8, :], yl[:, 0:8, :], hT[:], "merged_ready", scale=0.5)
                with dve.Fori(0, KD // 2) as m:
                    for s, g in enumerate((g0, g1)):
                        dve.wait_ge(S["out_proj"], 1)
                        dve.sem_inc(S["out_proj"], -1)
                        h = tile(hT, m * 2 + s)
                        stt(h, tile(xh, m * 2 + s).bitcast(F32), ALPHA, g[:], ALU.mult, ALU.add, f"g{s}_free")
                        stt(h, tile(xl, m * 2 + s).bitcast(F32), ALPHA, h, ALU.mult, ALU.add)
                layer_norm([hT[:, i, :] for i in range(KD)], D)
                for i in range(KD):
                    lower(xh[:, i, :], xl[:, i, :], hT[:, i, :])
                give(dve, "x_ready", "par_free")


def second_block(nc, S, par_dram, stream, out, hT):
    give, fin = helpers(S)
    with ExitStack() as ctx:
        def sb(name, shape, dt=F32):
            return ctx.enter_context(nc.sbuf_tensor(name + "_2", shape, dt))

        bank = [ctx.enter_context(nc.psum_tensor(f"bank{i}_2", [P, 512], F32)) for i in range(8)]
        g0, g1 = bank[0], bank[1]
        A = bank[2:]
        stage = sb("stage", [P, STAGE_SLOTS, GW])
        wh = sb("wh", [P, SPLIT_SLOTS, GW], F32R)
        wl = sb("wl", [P, SPLIT_SLOTS, GW], F32R)
        uh = sb("uh", [P, KD, T], F32R)
        ul = sb("ul", [P, KD, T], F32R)
        hidh = sb("hidh", [P, NF, T], F32R)
        hidl = sb("hidl", [P, NF, T], F32R)
        par = sb("par", [P, NP2])
        der = sb("der", [P, 16])
        ones = sb("ones", [P, P])
        ident = sb("ident", [P, P])
        near = sb("near", [P, T])
        ago = sb("ago", [P, T])
        tmp = sb("tmp", [P, 2, T])
        sq = sb("sq", [P, 2, T])
        rstd = sb("rstd", [P, T])
        gam = sb("gam", [P, T])
        Q = sb("Q", [P, T])
        K = sb("K", [P, T])
        V = sb("V", [P, NT, P])
        gate = sb("gate", [P, T])
        PT = sb("PT", [P, NT, T])
        pr = sb("pr", [P, 2, T])
        st = sb("st", [P, 8])

        def col(name, i=0, n=1):
            a = PC2[name][0]
            return par[:, a + i:a + i + n] if isinstance(i, int) else par[:, bass.ds(i + a, n)]

        block = ctx.enter_context(nc.Block())

        @block.sync
        def _(sp):
            weight_loader(sp, S, stage, stream, DEPTH * G2)
            sp.wait_ge(S["out_ready"], 1)
            sp.sem_inc(S["out_ready"], -1)
            sp.dma_start(out.rearrange("(k p) t -> p k t", p=P), hT[:]).then_inc(S["out_done"], 16)
            sp.wait_ge(S["out_done"], 16)
            sp.sem_inc(S["out_done"], -16)

        @block.gpsimd
        def _(pool):
            fin(pool, "pool_self", pool.memset(ones[:], 1.0))
            fin(pool, "pool_self", pool.memset(ident[:], 0.0))
            fin(pool, "pool_self", pool.affine_select(out=ident[:], in_=ident[:], compare_op=ALU.not_equal,
                                                      fill=1.0, base=0, pattern=[[-1, P]], channel_multiplier=1))
            fin(pool, "pool_self", pool.iota(near[:], [[1, T]], base=P - T, channel_multiplier=-1,
                                             allow_small_or_imprecise_dtypes=True))
            fin(pool, "pool_self", pool.affine_select(out=near[:], in_=near[:], compare_op=ALU.is_ge, fill=MASKED,
                                                      base=T - P, pattern=[[-1, T]], channel_multiplier=1))
            fin(pool, "pool_self", pool.iota(ago[:], [[-1, T]], base=0, channel_multiplier=1,
                                             allow_small_or_imprecise_dtypes=True))
            fin(pool, "pool_self", pool.affine_select(out=ago[:], in_=ago[:], compare_op=ALU.is_ge, fill=MASKED,
                                                      base=0, pattern=[[1, T]], channel_multiplier=-1),
                "consts_pe", "consts_act", "consts_dve")
            weight_remainders(pool, S, give, fin, stage, wh, wl, DEPTH * G2)

        @block.tensor
        def _(pe):
            pe.wait_ge(S["consts_pe"], 1)
            pe.sem_inc(S["consts_pe"], -1)
            proj = Projector(pe, S, wh, wl)

            def norm_sum():
                for i in range(KD):
                    pe.wait_ge(S[f"sq{i % 2}_ready"], 1)
                    pe.sem_inc(S[f"sq{i % 2}_ready"], -1)
                    pe.matmul(A[0][:], ones[:], sq[:, i % 2, :], start=i == 0, stop=i == KD - 1)\
                      .then_inc(S[f"sq{i % 2}_used"], 1)

            def values(out_bank):
                h, lo = proj.group()
                for t in range(NT):
                    c = slice(t * P, (t + 1) * P)
                    proj.product(out_bank[:, c], [((uh[:, k, c], ul[:, k, c]),
                                                   (h[:, k * P:(k + 1) * P], lo[:, k * P:(k + 1) * P]))
                                                  for k in range(KD)], "v_proj" if t == NT - 1 else None)

            def head_norm():
                pe.wait_ge(S["head_sq_ready"], 1)
                pe.sem_inc(S["head_sq_ready"], -1)
                pe.matmul(A[5][:], ones[:], sq[:, 0, :], start=True, stop=True).then_inc(S["head_sumsq"], 1)

            def weighted_values():
                pe.wait_ge(S["head_out_free"], 1)
                pe.sem_inc(S["head_out_free"], -1)
                for i in range(NT):
                    n = pe.matmul(A[4][:, i * P:T], V[:, i, :], PT[:, i, i * P:T], start=i == 0, stop=i == NT - 1)
                n.then_inc(S["head_out"], 1)

            with pe.Fori(0, DEPTH) as layer:
                pe.wait_ge(S["lam_prod"], 1)
                pe.sem_inc(S["lam_prod"], -1)
                pe.matmul(A[1][:, 0:2], ones[0:64, :], der[0:64, 8:10], start=True, stop=True)\
                  .then_inc(S["lam_sums"], 1)
                norm_sum()
                pe.wait_ge(S["u_ready"], 1)
                pe.sem_inc(S["u_ready"], -1)
                with pe.Fori(0, 2) as pair:
                    pe.wait_ge(S["g0_free"], 1)
                    pe.sem_inc(S["g0_free"], -1)
                    proj.channels(g0[:], proj.group(), (uh, ul), KD, P, done="q_proj")
                    pe.wait_ge(S["g1_free"], 1)
                    pe.sem_inc(S["g1_free"], -1)
                    proj.channels(g1[:], proj.group(), (uh, ul), KD, P, done="k_proj")
                    for a in range(2):
                        r = slice(64 * a, 64 * a + 64)
                        pe.wait_ge(S["g0_free"], 1)
                        pe.sem_inc(S["g0_free"], -1)
                        values(g0)
                        pe.wait_ge(S["g1_free"], 1)
                        pe.sem_inc(S["g1_free"], -1)
                        proj.channels(g1[:], proj.group(), (uh, ul), KD, P, done="gate_proj")
                        if a == 0:
                            pe.wait_ge(S["qk_ready"], 1)
                            pe.sem_inc(S["qk_ready"], -1)
                        for i in range(NT):
                            pe.wait_ge(S[f"a{i}_free"], 1)
                            pe.sem_inc(S[f"a{i}_free"], -1)
                            pe.matmul(A[i][:, i * P:T], K[r, i * P:(i + 1) * P], Q[r, i * P:T], start=True,
                                      stop=True).then_inc(S["scores"], 1)
                        pe.wait_ge(S["v_ready"], 1)
                        pe.sem_inc(S["v_ready"], -1)
                        pe.wait_ge(S["weights_ready"], 1)
                        pe.sem_inc(S["weights_ready"], -1)
                        weighted_values()
                        head_norm()
                with pe.Fori(0, 2) as pair:
                    for a in range(2):
                        pe.wait_ge(S["g0_free"], 1)
                        pe.sem_inc(S["g0_free"], -1)
                        proj.channels(g0[:], proj.group(), (uh, ul), KD, P, done="q_proj")
                        pe.wait_ge(S["g1_free"], 1)
                        pe.sem_inc(S["g1_free"], -1)
                        proj.channels(g1[:], proj.group(), (uh, ul), KD, P, done="k_proj")
                        pe.wait_ge(S["g0_free"], 1)
                        pe.sem_inc(S["g0_free"], -1)
                        values(g0)
                        pe.wait_ge(S["qk_ready"], 1)
                        pe.sem_inc(S["qk_ready"], -1)

                        def scores(t):
                            n = (t + 1) * P
                            for j in range(2):
                                b = 2 * (t % 2) + j
                                pe.wait_ge(S[f"a{b}_free"], 1)
                                pe.sem_inc(S[f"a{b}_free"], -1)
                                pe.matmul(A[b][:, 0:n], Q[64 * j:64 * j + 64, t * P:n], K[64 * j:64 * j + 64, 0:n],
                                          start=True, stop=True).then_inc(S["scores"], 1)

                        scores(0)
                        for t in range(NT):
                            if t + 1 < NT:
                                scores(t + 1)
                            pe.wait_ge(S["probs_ready"], 1)
                            pe.sem_inc(S["probs_ready"], -1)
                            pe.wait_ge(S["a5_free"], 1)
                            pe.sem_inc(S["a5_free"], -1)
                            for i in range(t + 1):
                                n = pe.transpose(A[5][:, i * P:(i + 1) * P], pr[:, 0, i * P:(i + 1) * P], ident[:])
                            n.then_inc(S["probs_turned"], 1)
                        pe.wait_ge(S["v_ready"], 1)
                        pe.sem_inc(S["v_ready"], -1)
                        pe.wait_ge(S["weights_ready"], 1)
                        pe.sem_inc(S["weights_ready"], -1)
                        weighted_values()
                        pe.wait_ge(S["a5_free"], 1)
                        pe.sem_inc(S["a5_free"], -1)
                        head_norm()
                pe.wait_ge(S["mix_ready"], 1)
                pe.sem_inc(S["mix_ready"], -1)
                with pe.Fori(0, KD // 2) as m:
                    for s, g in enumerate((g0, g1)):
                        pe.wait_ge(S[f"g{s}_free"], 1)
                        pe.sem_inc(S[f"g{s}_free"], -1)
                        proj.channels(g[:], proj.group(), (hidh, hidl), KD, P, done="out_proj")
                norm_sum()
                pe.wait_ge(S["u_ready"], 1)
                pe.sem_inc(S["u_ready"], -1)
                with pe.Fori(0, NF // 2) as f:
                    for s in range(2):
                        pe.wait_ge(S["g0_free"], 1)
                        pe.sem_inc(S["g0_free"], -1)
                        proj.channels(g0[:], proj.group(), (uh, ul), KD, P, done="gate_proj")
                        pe.wait_ge(S["g1_free"], 1)
                        pe.sem_inc(S["g1_free"], -1)
                        proj.channels(g1[:], proj.group(), (uh, ul), KD, P, done="up_proj")
                pe.wait_ge(S["hidden_ready"], 1)
                pe.sem_inc(S["hidden_ready"], -1)
                with pe.Fori(0, KD // 2) as m:
                    for s, g in enumerate((g0, g1)):
                        pe.wait_ge(S[f"g{s}_free"], 1)
                        pe.sem_inc(S[f"g{s}_free"], -1)
                        for c, n in enumerate((8, 8, NF - 16)):
                            proj.channels(g[:], proj.group(), (hidh, hidl), n, P, done="down_proj" if c == 2 else None,
                                          k0=8 * c, more=c < 2, first=c == 0)
            norm_sum()

        @block.scalar
        def _(act):
            act.wait_ge(S["consts_act"], 1)
            act.sem_inc(S["consts_act"], -1)
            for n in ("sq0_used", "sq1_used"):
                give(act, n)

            round_next = rounder(act, S, stage, wh)
            round_next()

            def squares():
                for i in range(KD):
                    act.wait_ge(S[f"sq{i % 2}_used"], 1)
                    act.sem_inc(S[f"sq{i % 2}_used"], -1)
                    act.activation(sq[:, i % 2, :], hT[:, i, :], ACT.Square).then_inc(S[f"sq{i % 2}_ready"], 1)

            def root(src, n):
                act.activation(rstd[:], src, ACT.Sqrt, scale=1.0 / n, bias=EPS_COL).then_inc(S["root"], 1)

            def normed():
                act.wait_ge(S["h_ready_act"], 1)
                act.sem_inc(S["h_ready_act"], -1)
                squares()
                act.wait_ge(S["sq0_used"], 1)
                act.sem_inc(S["sq0_used"], -1)
                act.wait_ge(S["sq1_used"], 1)
                act.sem_inc(S["sq1_used"], -1)
                root(A[0][:], D)
                for n in ("sq0_used", "sq1_used"):
                    give(act, n)
                for i in range(KD):
                    act.wait_ge(S[f"tmp{i % 2}_ready"], 1)
                    act.sem_inc(S[f"tmp{i % 2}_ready"], -1)
                    act.activation(uh[:, i, :], tmp[:, i % 2, :], ACT.Copy).then_inc(S["hi_ready"], 1)

            def head(a_is_ret):
                act.wait_ge(S["head_out"], 1)
                act.sem_inc(S["head_out"], -1)
                act.wait_ge(S["sq0_used"], 1)
                act.sem_inc(S["sq0_used"], -1)
                act.wait_ge(S["sq1_used"], 1)
                act.sem_inc(S["sq1_used"], -1)
                act.activation(sq[:, 0, :], A[4][:], ACT.Square).then_inc(S["head_sq_ready"], 1)
                act.wait_ge(S["head_sumsq"], 1)
                act.sem_inc(S["head_sumsq"], -1)
                root(A[5][:], P)
                give(act, "sq0_used")
                give(act, "sq1_used")

            eps = der[:, 10:11]
            EPS_COL = eps
            with act.Fori(0, DEPTH) as layer:
                act.wait_ge(S["par_free"], 1)
                act.sem_inc(S["par_free"], -1)
                act.dma_start(par[:], par_dram[bass.ds(layer, 1)].rearrange("a p n -> p (a n)"))\
                   .then_inc(S["par_full"], 16)
                act.wait_ge(S["par_full"], 16)
                act.sem_inc(S["par_full"], -16)
                give(act, "par_dve")
                act.wait_ge(S["lam_sums"], 1)
                act.sem_inc(S["lam_sums"], -1)
                act.activation(der[:, 0:2], A[1][:, 0:2], ACT.Exp).then_inc(S["lam_exp"], 1)
                normed()
                with act.Fori(0, 2) as pair:
                    round_next()
                    act.wait_ge(S["q_proj"], 1)
                    act.sem_inc(S["q_proj"], -1)
                    act.wait_ge(S["qk_free"], 1)
                    act.sem_inc(S["qk_free"], -1)
                    fin(act, "act_self", act.activation(Q[:], g0[:], ACT.Copy, scale=64 ** -0.5), "g0_free")
                    round_next()
                    act.wait_ge(S["k_proj"], 1)
                    act.sem_inc(S["k_proj"], -1)
                    fin(act, "act_self", act.activation(K[:], g1[:], ACT.Copy), "g1_free", "qk_ready")
                    for a in range(2):
                        act.wait_ge(S["gam_free"], 1)
                        act.sem_inc(S["gam_free"], -1)
                        act.activation(gam[:], ago[:], ACT.Exp, scale=col("log_gamma", pair * 2 + a))\
                           .then_inc(S["gam_ready"], 1)
                        round_next()
                        act.wait_ge(S["v_proj"], 1)
                        act.sem_inc(S["v_proj"], -1)
                        act.wait_ge(S["v_free"], 1)
                        act.sem_inc(S["v_free"], -1)
                        fin(act, "act_self", act.activation(V[:].rearrange("p a b -> p (a b)"), g0[:], ACT.Copy),
                            "g0_free", "v_ready")
                        round_next()
                        act.wait_ge(S["gate_proj"], 1)
                        act.sem_inc(S["gate_proj"], -1)
                        act.wait_ge(S["tmp1_free"], 1)
                        act.sem_inc(S["tmp1_free"], -1)
                        act.activation(tmp[:, 1, :], g1[:], ACT.Tanh, scale=0.5).then_inc(S["tanh_ready"], 1)
                        head(True)
                        act.wait_ge(S["tmp0_ready"], 1)
                        act.sem_inc(S["tmp0_ready"], -1)
                        act.activation(hidh[:, bass.ds(pair * 2 + a, 1), :].rearrange("p a t -> p (a t)"),
                                       tmp[:, 0, :], ACT.Copy).then_inc(S["hi_ready"], 1)
                with act.Fori(0, 2) as pair:
                    for a in range(2):
                        round_next()
                        act.wait_ge(S["q_proj"], 1)
                        act.sem_inc(S["q_proj"], -1)
                        act.wait_ge(S["qk_free"], 1)
                        act.sem_inc(S["qk_free"], -1)
                        fin(act, "act_self", act.activation(Q[:], g0[:], ACT.Copy, scale=64 ** -0.5), "g0_free")
                        round_next()
                        act.wait_ge(S["k_proj"], 1)
                        act.sem_inc(S["k_proj"], -1)
                        fin(act, "act_self", act.activation(K[:], g1[:], ACT.Copy), "g1_free", "qk_ready")
                        round_next()
                        act.wait_ge(S["v_proj"], 1)
                        act.sem_inc(S["v_proj"], -1)
                        act.wait_ge(S["v_free"], 1)
                        act.sem_inc(S["v_free"], -1)
                        fin(act, "act_self", act.activation(V[:].rearrange("p a b -> p (a b)"), g0[:], ACT.Copy),
                            "g0_free", "v_ready")
                        for t in range(NT):
                            n = (t + 1) * P
                            for j in range(2):
                                act.wait_ge(S["max_ready"], 1)
                                act.sem_inc(S["max_ready"], -1)
                                act.activation(pr[:, j, 0:n], pr[:, j, 0:n], ACT.Exp, bias=st[:, j:j + 1],
                                               accum_out=st[:, 2 + j:3 + j]).then_inc(S["exp_ready"], 1)
                            act.wait_ge(S["probs_turned"], 1)
                            act.sem_inc(S["probs_turned"], -1)
                            fin(act, "act_self",
                                act.activation(PT[:, 0:t + 1, t * P:n],
                                               A[5][:, 0:n].rearrange("p (a b) -> p a b", b=P), ACT.Copy),
                                "a5_free", "pr0_free", *(["weights_ready"] if t == NT - 1 else []))
                        head(False)
                        give(act, "a5_free")
                        act.wait_ge(S["tmp0_ready"], 1)
                        act.sem_inc(S["tmp0_ready"], -1)
                        act.activation(hidh[:, bass.ds(pair * 2 + a + 4, 1), :].rearrange("p a t -> p (a t)"),
                                       tmp[:, 0, :], ACT.Copy).then_inc(S["hi_ready"], 1)
                with act.Fori(0, KD // 2) as m:
                    round_next()
                    round_next()
                normed()
                with act.Fori(0, NF // 2) as f:
                    for s in range(2):
                        round_next()
                        act.wait_ge(S["gate_proj"], 1)
                        act.sem_inc(S["gate_proj"], -1)
                        act.wait_ge(S["tmp1_free"], 1)
                        act.sem_inc(S["tmp1_free"], -1)
                        act.activation(tmp[:, 1, :], g0[:], ACT.Tanh, scale=0.5).then_inc(S["tanh_ready"], 1)
                        round_next()
                        act.wait_ge(S["tmp0_ready"], 1)
                        act.sem_inc(S["tmp0_ready"], -1)
                        act.activation(hidh[:, bass.ds(f * 2 + s, 1), :].rearrange("p a t -> p (a t)"),
                                       tmp[:, 0, :], ACT.Copy).then_inc(S["hi_ready"], 1)
                with act.Fori(0, KD // 2) as m:
                    for _ in range(6):
                        round_next()
            act.wait_ge(S["h_ready_act"], 1)
            act.sem_inc(S["h_ready_act"], -1)
            squares()
            act.wait_ge(S["sq0_used"], 1)
            act.sem_inc(S["sq0_used"], -1)
            act.wait_ge(S["sq1_used"], 1)
            act.sem_inc(S["sq1_used"], -1)
            root(A[0][:], D)

        @block.vector
        def _(dve):
            dve.wait_ge(S["consts_dve"], 1)
            dve.sem_inc(S["consts_dve"], -1)
            fin(dve, "dve_self", dve.memset(der[:, 10:11], 1e-6))
            for n in ("g0_free", "g1_free", "par_free", "qk_free", "v_free", "gam_free", "tmp1_free", "head_out_free",
                      "a0_free", "a1_free", "a2_free", "a3_free", "a5_free", "pr0_free", "h_ready_act"):
                give(dve, n)

            def dve_op(ins, *names):
                fin(dve, "dve_self", ins, *names)

            def lower(dst_h, dst_l, src, *names):
                dve.wait_ge(S["hi_ready"], 1)
                dve.sem_inc(S["hi_ready"], -1)
                dve_op(dve.tensor_tensor(dst_l, src, dst_h.bitcast(F32), ALU.subtract), *names)

            def normed(gain):
                dve.wait_ge(S["root"], 1)
                dve.sem_inc(S["root"], -1)
                dve_op(dve.reciprocal(rstd[:], rstd[:]))
                for i in range(KD):
                    dve_op(dve.scalar_tensor_tensor(out=tmp[:, i % 2, :], in0=hT[:, i, :], scalar=col(gain, i),
                                                    in1=rstd[:], op0=ALU.mult, op1=ALU.mult), f"tmp{i % 2}_ready")
                    if i:
                        lower(uh[:, i - 1, :], ul[:, i - 1, :], tmp[:, (i - 1) % 2, :])
                lower(uh[:, KD - 1, :], ul[:, KD - 1, :], tmp[:, (KD - 1) % 2, :], "u_ready")

            def head(gain, gated, tile):
                dve.wait_ge(S["root"], 1)
                dve.sem_inc(S["root"], -1)
                dve_op(dve.reciprocal(rstd[:], rstd[:]))
                dve_op(dve.scalar_tensor_tensor(out=tmp[:, 0, :], in0=A[4][:], scalar=gain, in1=rstd[:],
                                                op0=ALU.mult, op1=ALU.mult), "head_out_free",
                       *([] if gated else ["tmp0_ready"]))
                if gated:
                    dve_op(dve.scalar_tensor_tensor(out=tmp[:, 0, :], in0=tmp[:, 0, :], scalar=0.5, in1=gate[:],
                                                    op0=ALU.mult, op1=ALU.mult), "tmp0_ready")
                t = [x[:, bass.ds(tile, 1), :].rearrange("p a t -> p (a t)") for x in (hidh, hidl)]
                lower(t[0], t[1], tmp[:, 0, :])

            with dve.Fori(0, DEPTH) as layer:
                dve.wait_ge(S["par_dve"], 1)
                dve.sem_inc(S["par_dve"], -1)
                lam = PC2["lam"][0]
                dve_op(dve.tensor_tensor(der[0:64, 8:10], par[0:64, lam:lam + 3:2], par[0:64, lam + 1:lam + 4:2],
                                         ALU.mult), "lam_prod")
                dve.wait_ge(S["lam_exp"], 1)
                dve.sem_inc(S["lam_exp"], -1)
                dve_op(dve.tensor_tensor(der[:, 2:3], der[:, 1:2], der[:, 0:1], ALU.subtract))
                dve_op(dve.tensor_tensor(der[:, 3:4], der[:, 2:3], col("lam_init"), ALU.subtract))
                dve_op(dve.tensor_tensor(der[:, 4:5], col("diff_norm"), col("lam_rest"), ALU.mult))
                normed("attn_norm")
                with dve.Fori(0, 2) as pair:
                    for a in range(2):
                        dve.wait_ge(S["tanh_ready"], 1)
                        dve.sem_inc(S["tanh_ready"], -1)
                        dve_op(dve.scalar_tensor_tensor(out=gate[:], in0=tmp[:, 1, :], scalar=1.0, in1=g1[:],
                                                        op0=ALU.add, op1=ALU.mult), "g1_free", "tmp1_free")
                        dve.wait_ge(S["gam_ready"], 1)
                        dve.sem_inc(S["gam_ready"], -1)
                        for i in range(NT):
                            dve.wait_ge(S["scores"], 1)
                            dve.sem_inc(S["scores"], -1)
                            dve_op(dve.tensor_tensor(PT[:, i, i * P:T], A[i][:, i * P:T], gam[:, 0:T - i * P],
                                                     ALU.mult), f"a{i}_free",
                                   *(["gam_free", "weights_ready"] + ["qk_free"] * a if i == NT - 1 else []))
                        head(col("ret_norm"), True, pair * 2 + a)
                        give(dve, "v_free")
                with dve.Fori(0, 2) as pair:
                    for a in range(2):
                        for t in range(NT):
                            n = (t + 1) * P
                            dve.wait_ge(S["pr0_free"], 1)
                            dve.sem_inc(S["pr0_free"], -1)
                            for j in range(2):
                                dve.wait_ge(S["scores"], 1)
                                dve.sem_inc(S["scores"], -1)
                                b = 2 * (t % 2) + j
                                dve_op(dve.scalar_tensor_tensor(
                                    out=pr[:, j, 0:n], in0=near[:, T - n:T], scalar=col("slope", pair * 2 + a),
                                    in1=A[b][:, 0:n], op0=ALU.mult, op1=ALU.add), f"a{b}_free",
                                    *(["qk_free"] if (t, j) == (NT - 1, 1) else []))
                                dve_op(dve.tensor_reduce(st[:, 6:7], pr[:, j, 0:n], AX, ALU.max))
                                dve_op(dve.tensor_scalar(st[:, j:j + 1], st[:, 6:7], -1.0, None, ALU.mult), "max_ready")
                            dve.wait_ge(S["exp_ready"], 1)
                            dve.sem_inc(S["exp_ready"], -1)
                            dve.wait_ge(S["exp_ready"], 1)
                            dve.sem_inc(S["exp_ready"], -1)
                            dve_op(dve.reciprocal(st[:, 4:6], st[:, 2:4]))
                            dve_op(dve.tensor_tensor(st[:, 5:6], st[:, 5:6], der[:, 3:4], ALU.mult))
                            dve_op(dve.tensor_scalar(pr[:, 0, 0:n], pr[:, 0, 0:n], st[:, 4:5], None, ALU.mult))
                            dve_op(dve.scalar_tensor_tensor(out=pr[:, 0, 0:n], in0=pr[:, 1, 0:n], scalar=st[:, 5:6],
                                                            in1=pr[:, 0, 0:n], op0=ALU.mult, op1=ALU.add),
                                   "probs_ready")
                        head(der[:, 4:5], False, pair * 2 + a + 4)
                        give(dve, "v_free")
                give(dve, "mix_ready")
                with dve.Fori(0, KD // 2) as m:
                    for s, g in enumerate((g0, g1)):
                        dve.wait_ge(S["out_proj"], 1)
                        dve.sem_inc(S["out_proj"], -1)
                        h = hT[:, bass.ds(m * 2 + s, 1), :].rearrange("p a t -> p (a t)")
                        dve_op(dve.tensor_tensor(h, g[:], h, ALU.add), f"g{s}_free")
                give(dve, "h_ready_act")
                normed("ffn_norm")
                with dve.Fori(0, NF // 2) as f:
                    for s in range(2):
                        dve.wait_ge(S["tanh_ready"], 1)
                        dve.sem_inc(S["tanh_ready"], -1)
                        dve_op(dve.scalar_tensor_tensor(out=gate[:], in0=tmp[:, 1, :], scalar=1.0, in1=g0[:],
                                                        op0=ALU.add, op1=ALU.mult), "g0_free", "tmp1_free")
                        dve.wait_ge(S["up_proj"], 1)
                        dve.sem_inc(S["up_proj"], -1)
                        dve_op(dve.scalar_tensor_tensor(out=tmp[:, 0, :], in0=g1[:], scalar=0.5, in1=gate[:],
                                                        op0=ALU.mult, op1=ALU.mult), "g1_free", "tmp0_ready")
                        lower(hidh[:, bass.ds(f * 2 + s, 1), :].rearrange("p a t -> p (a t)"),
                              hidl[:, bass.ds(f * 2 + s, 1), :].rearrange("p a t -> p (a t)"), tmp[:, 0, :])
                give(dve, "hidden_ready")
                with dve.Fori(0, KD // 2) as m:
                    for s, g in enumerate((g0, g1)):
                        dve.wait_ge(S["down_proj"], 1)
                        dve.sem_inc(S["down_proj"], -1)
                        h = hT[:, bass.ds(m * 2 + s, 1), :].rearrange("p a t -> p (a t)")
                        dve_op(dve.tensor_tensor(h, g[:], h, ALU.add), f"g{s}_free")
                give(dve, "h_ready_act", "par_free")
            dve.wait_ge(S["root"], 1)
            dve.sem_inc(S["root"], -1)
            dve_op(dve.reciprocal(rstd[:], rstd[:]))
            for i in range(KD):
                dve_op(dve.scalar_tensor_tensor(out=hT[:, i, :], in0=hT[:, i, :], scalar=col("final_norm", i),
                                                in1=rstd[:], op0=ALU.mult, op1=ALU.mult))
            give(dve, "out_ready")


def k_tiles(w, c0, cn=P):
    n, k = w.shape[0], w.shape[1]
    return w[:, :, c0:c0 + cn].reshape(n, k // P, P, cn).transpose(0, 2, 1, 3).reshape(n, P, k // P * cn)


def as_group(a):
    return np.pad(a, ((0, 0), (0, 0), (0, GW - a.shape[2])))


def columns(v):
    return v.reshape(v.shape[0], -1, P).transpose(0, 2, 1)


def pad_stream(s):
    return np.concatenate([s.reshape(-1, P, GW), np.zeros((1, P, GW), np.float32)])


def first_stream(w_in, w_uq, w_ukv, w_mem, w_o, w_out):
    r, o = 0, 1664
    q, kv, kpe, mg, cu, cg, xq, xg, mrg = 2176, 2560, 2816, 2848, 3360, 4384, 4896, 5408, 5920
    x = lambda c0: k_tiles(w_in, c0)
    groups = []
    for i in range(NW):
        groups += [x(cu + P * i), x(cu + W + P * i)]
    groups += [x(cg + P * i) for i in range(NW)]
    latents = [x(q + P * i) for i in range(3)] + [x(kv + P * i) for i in range(2)]
    latents.append(k_tiles(np.concatenate([w_in[:, :, kpe:kpe + 32]] * 4, 2), 0))
    for i in range(2):
        groups += latents[3 * i:3 * i + 3]
        for j in (2 * i, 2 * i + 1):
            groups += [x(mg + P * j), x(xg + P * j)]
    for h in range(8):
        groups.append(as_group(np.concatenate([k_tiles(w_uq, 96 * h, 96), k_tiles(w_ukv, P * h)], 2)))
    for h in range(4):
        groups += [x(xq + P * h), k_tiles(w_mem, P * h), k_tiles(w_mem, W + P * h)]
    groups += [x(P * i) for i in range(12)]
    groups += [as_group(k_tiles(w_in[:, k:k + W], 1536)) for k in (0, W)]

    def merge(n, d):
        return [x(mrg + D * n + P * d), x(mrg + D * n + P * (d + 1)), k_tiles(w_o[:, n], P * d, 2 * P)]

    for chunk in range(NT):
        for n in (1, 2, 3):
            groups += merge(n, 2 * chunk)
    groups += [x(o + P * i) for i in range(NW)]
    for d in range(0, KD, 2):
        groups += merge(0, d)
    groups += [k_tiles(w_out, P * m) for m in range(KD)]
    assert len(groups) == G1
    return pad_stream(np.stack(groups, 1))


def first_params(mu, w0, a0, k_k, k_a, r_k, lnx_g, lnx_b, q_norm, kv_norm, conv_w, conv_b, cln_g, cln_b, b_gate,
                 ln_g, ln_b):
    taps = conv_w.reshape(DEPTH, TAPS, NW, P).transpose(0, 3, 2, 1).reshape(DEPTH, P, NW * TAPS)
    inv_freq = np.float32(10000.0) ** (-np.arange(0, 32, 2, dtype=np.float32) / np.float32(32))
    freq = np.broadcast_to(np.tile(inv_freq, P // 16)[None, :, None], (DEPTH, P, 1))
    cols = [columns(mu), columns(w0), columns(a0), columns(k_k), columns(k_a), columns(r_k.reshape(DEPTH, W)),
            columns(lnx_g), columns(lnx_b), columns(q_norm), columns(kv_norm), taps, columns(conv_b), columns(cln_g),
            columns(cln_b), columns(b_gate.reshape(DEPTH, -1)), columns(ln_g), columns(ln_b), freq]
    return np.ascontiguousarray(np.concatenate(cols, 2), dtype=np.float32)


def second_stream(w_in, w_out, w_gate, w_up, w_down):
    groups = []
    for pair in range(2):
        groups += [k_tiles(w_in, P * pair), k_tiles(w_in, 256 + P * pair)]
        for h in (2 * pair, 2 * pair + 1):
            groups += [k_tiles(w_in, 512 + P * h), k_tiles(w_in, 1024 + P * h)]
    for h in range(4):
        groups += [k_tiles(w_in, 1536 + 512 * i + P * h) for i in range(3)]
    groups += [k_tiles(w_out, P * m) for m in range(KD)]
    for f in range(NF):
        groups += [k_tiles(w_gate, P * f), k_tiles(w_up, P * f)]
    for m in range(KD):
        groups += [as_group(k_tiles(w_down[:, k:k + GW], P * m)) for k in range(0, FFN, GW)]
    assert len(groups) == G2
    s = np.stack(groups, 1)
    return pad_stream(s)


def second_params(attn_norm, ret_norm, diff_norm, ffn_norm, lam, final_norm):
    lam_init = np.array([0.8 - 0.6 * math.exp(-0.3 * i) for i in range(DEPTH)])
    full = lambda v: np.broadcast_to(np.asarray(v, np.float32).reshape(DEPTH, 1, -1), (DEPTH, P, np.size(v) // DEPTH))
    log_gamma = np.tile(-np.log1p(-np.exp2(-5.0 - np.arange(4))), (DEPTH, 1))
    slope = np.tile(np.exp2(-2.0 * np.arange(1, 5)), (DEPTH, 1))
    lams = np.concatenate([np.stack(lam, 2), np.zeros((DEPTH, 64, 4), np.float32)], 1)
    cols = [columns(attn_norm), columns(ret_norm), columns(diff_norm), columns(ffn_norm), lams, full(lam_init),
            full(1.0 - lam_init), np.repeat(columns(final_norm[None]), DEPTH, 0), full(log_gamma), full(slope)]
    return np.ascontiguousarray(np.concatenate(cols, 2), dtype=np.float32)


def build(nc, x, mem, positions, params1, lora, stream1, params2, stream2, out):
    with ExitStack() as ctx:
        hT = ctx.enter_context(nc.sbuf_tensor("hT", [P, KD, T], F32))
        with ExitStack() as first:
            S = Sems(nc, first, "first_")
            first_block(nc, S, x, mem, positions, params1, lora, stream1, hT)
            with nc.Block() as block:
                @block.gpsimd
                def _(pool):
                    for sem in S.all.values():
                        pool.sem_clear(sem)
        second_block(nc, Sems(nc, ctx, "second_"), params2, stream2, out, hT)


def kernel(**inputs):
    import concourse.bacc as bacc
    from concourse.bass_utils import run_bass_kernel_spmd

    v = {n: np.asarray(a) for n, a in inputs.items()}
    arrays = {
        "x": np.ascontiguousarray(v["x"][0].T),
        "mem": np.ascontiguousarray(v["mem"][0].T),
        "positions": v["positions"],
        "params1": first_params(*(v[n] for n in (
            "rwkv_mu", "rwkv_w0", "rwkv_a0", "rwkv_k_k", "rwkv_k_a", "rwkv_r_k", "rwkv_lnx_g", "rwkv_lnx_b",
            "mla_q_norm", "mla_kv_norm", "conv_w", "conv_b", "conv_ln_g", "conv_ln_b", "b_gate", "ln_g", "ln_b"))),
        "lora": np.ascontiguousarray(np.concatenate([v["rwkv_w2"], v["rwkv_a2"]], 1)),
        "stream1": first_stream(*(v[n] for n in ("w_in", "mla_w_uq", "mla_w_ukv", "xattn_w_mem_kv", "w_o_branch",
                                                 "w_out"))),
        "params2": second_params(*(v[n + "_2"] for n in ("attn_norm", "ret_norm", "diff_norm", "ffn_norm")),
                                 [v[f"lambda_{n}_2"] for n in ("q1", "k1", "q2", "k2")], v["final_norm_2"]),
        "stream2": second_stream(*(v[n + "_2"] for n in ("w_in", "w_out", "w_gate", "w_up", "w_down"))),
    }
    nc = bacc.Bacc("TRN2", target_bir_lowering=False, num_devices=1)
    args = [nc.dram_tensor(f"in_{n}", a.shape, mybir.dt.from_np(a.dtype), kind="ExternalInput").ap()
            for n, a in arrays.items()]
    out = nc.dram_tensor("out_x", (D, T), F32, kind="ExternalOutput").ap()
    build(nc, *args, out)
    r = run_bass_kernel_spmd(nc, [{f"in_{n}": a for n, a in arrays.items()}], core_ids=[0])
    return np.ascontiguousarray(r.results[0]["out_x"].T)[None]
```

```python
from contextlib import ExitStack
import math

import numpy as np
import concourse.bass as bass
from concourse import mybir

P = 128
T = 512
NT = T // P
D = 1024
KD = D // P
W = 512
NW = W // P
DEPTH = 2
MEM = 256
GW = 1024
SPLIT_SLOTS = 2
STAGE_SLOTS = 2
TAPS = 31
F32 = mybir.dt.float32
F32R = mybir.dt.float32r
I32 = mybir.dt.int32
ALU = mybir.AluOpType
ACT = mybir.ActivationFunctionType
AX = mybir.AxisListType.X
MASKED = -1e30
ALPHA = (2.0 * DEPTH) ** 0.25
KAPPA = math.exp(-0.5) / 2
CH = P
FFN = 2816
ARENA = 18200
NF = FFN // P

_P1 = [("mu", 13), ("w0", 4), ("a0", 4), ("k_k", 4), ("k_a", 4), ("r_k", 4), ("lnx_g", 4),
       ("lnx_b", 4), ("q_norm", 3), ("kv_norm", 2), ("conv_w", NW * TAPS), ("conv_b", 4),
       ("cln_g", 4), ("cln_b", 4), ("b_gate", 32), ("ln_g", 8), ("ln_b", 8), ("inv_freq", 1)]
_P2 = [("attn_norm", 8), ("ret_norm", 1), ("diff_norm", 1), ("ffn_norm", 8), ("lam", 4),
       ("lam_init", 1), ("lam_rest", 1), ("final_norm", 8), ("log_gamma", 4), ("slope", 4)]


def offsets(spec):
    at, out = 0, {}
    for name, n in spec:
        out[name] = (at, n)
        at += n
    return out, at


PC1, NP1 = offsets(_P1)
PC2, NP2 = offsets(_P2)
G1 = 8 + 4 + 6 + 4 + 8 + 16 + 12 + 2 + 36 + 4 + 12 + 8
G2 = 12 + 12 + 8 + 2 * NF + 24


class Sems:

    def __init__(self, nc, ctx, prefix=""):
        self.nc, self.ctx, self.prefix, self.all = nc, ctx, prefix, {}

    def __getitem__(self, name):
        if name not in self.all:
            self.all[name] = self.ctx.enter_context(self.nc.semaphore(self.prefix + name))
        return self.all[name]


def helpers(S):
    def give(eng, *names):
        for name in names:
            eng.sem_inc(S[name], 1)

    def fin(eng, own, ins, *names):
        ins.then_inc(S[own], 1)
        eng.wait_ge(S[own], 1)
        eng.sem_inc(S[own], -1)
        give(eng, *names)

    return give, fin


def weight_loader(sp, S, stage, stream, groups):
    with sp.Fori(0, groups // STAGE_SLOTS) as g:
        for s in range(STAGE_SLOTS):
            sp.wait_ge(S[f"stage{s}_free"], 1)
            sp.sem_inc(S[f"stage{s}_free"], -1)
            sp.dma_start(stage[:, s, :], stream[bass.ds(g * STAGE_SLOTS + s, 1)].rearrange("a p n -> p (a n)"))\
              .then_inc(S[f"stage{s}_full"], 16)
    sp.wait_ge(S["stage0_free"], 1)
    sp.sem_inc(S["stage0_free"], -1)
    sp.dma_start(stage[:, 0, :], stream[groups]).then_inc(S["stage0_full"], 16)


def weight_remainders(pool, S, give, fin, stage, wh, wl, groups, first=True, last=True):
    if first:
        for s in range(STAGE_SLOTS):
            give(pool, f"stage{s}_free")
        give(pool, "w0_free")
    with pool.Fori(0, groups // STAGE_SLOTS) as g:
        for s in range(STAGE_SLOTS):
            pool.wait_ge(S[f"hi{s}_ready"], 1)
            pool.sem_inc(S[f"hi{s}_ready"], -1)
            fin(pool, "pool_self", pool.tensor_tensor(wl[:, s, :], stage[:, s, :], wh[:, s, :].bitcast(F32),
                                                      ALU.subtract), f"w{s}_ready", f"stage{s}_free")
    if last:
        pool.wait_ge(S["hi0_ready"], 1)
        pool.sem_inc(S["hi0_ready"], -1)


def rounder(act, S, stage, wh):
    slot = [0]

    def round_next():
        s = slot[0]
        slot[0] = 1 - s
        act.wait_ge(S[f"stage{s}_full"], 16)
        act.sem_inc(S[f"stage{s}_full"], -16)
        act.wait_ge(S[f"w{s}_free"], 1)
        act.sem_inc(S[f"w{s}_free"], -1)
        act.activation(wh[:, s, :], stage[:, s, :], ACT.Copy).then_inc(S[f"hi{s}_ready"], 1)

    return round_next


class Projector:

    def __init__(self, pe, S, wh, wl):
        self.pe, self.S, self.wh, self.wl, self.slot, self.release = pe, S, wh, wl, 1, None

    def group(self):
        self.release = f"w{self.slot}_free"
        self.slot = 1 - self.slot
        self.pe.wait_ge(self.S[f"w{self.slot}_ready"], 1)
        self.pe.sem_inc(self.S[f"w{self.slot}_ready"], -1)
        return self.wh[:, self.slot, :], self.wl[:, self.slot, :]

    def product(self, out, terms, done=None, more=False, first=True, each=None):
        steps = [(a, b) for (ah, al), (bh, bl) in terms for a, b in ((ah, bh), (ah, bl), (al, bh))]
        for n, (a, b) in enumerate(steps):
            if each and n % 3 == 0:
                self.pe.wait_ge(self.S[each], 1)
                self.pe.sem_inc(self.S[each], -1)
            ins = self.pe.matmul(out, a, b, start=first and n == 0, stop=not more and n == len(steps) - 1)
            if n == 0 and self.release:
                ins.then_inc(self.S[self.release], 1)
                self.release = None
        if done:
            ins.then_inc(self.S[done], 1)

    def channels(self, out, w, x, kt, width, c0=0, cn=P, done=None, k0=0, more=False, first=True,
                 each=None):
        wh, wl = w
        self.product(out, [((wh[:, k * width + c0:k * width + c0 + cn], wl[:, k * width + c0:k * width + c0 + cn]),
                            (x[0][:, k0 + k, :], x[1][:, k0 + k, :])) for k in range(kt)], done, more, first, each)


def first_block(nc, S, x_dram, mem_dram, pos_dram, par_dram, lora_dram, stream, hT):
    give, fin = helpers(S)
    with ExitStack() as ctx:
        def sb(name, shape, dt=F32):
            return ctx.enter_context(nc.sbuf_tensor(name + "_1", shape, dt))

        bank = [ctx.enter_context(nc.psum_tensor(f"bank{i}_1", [P, 512], F32)) for i in range(8)]
        g0, g1 = bank[0], bank[1]
        A = bank[2:]
        stage = sb("stage", [P, STAGE_SLOTS, GW])
        wh = sb("wh", [P, SPLIT_SLOTS, GW], F32R)
        wl = sb("wl", [P, SPLIT_SLOTS, GW], F32R)
        xh = sb("xh", [P, KD, T], F32R)
        xl = sb("xl", [P, KD, T], F32R)
        yh = sb("yh", [P, 12, T], F32R)
        yl = sb("yl", [P, 12, T], F32R)
        par = sb("par", [P, NP1])
        der = sb("der", [P, 64])
        ones = sb("ones", [P, P])
        ident = sb("ident", [P, P])
        halves = sb("halves", [P, P])
        future = sb("future", [P, P])
        after = sb("after", [P, 2, P])
        before = sb("before", [P, P])
        level = sb("level", [P, 7, 2, P], mybir.dt.uint8)
        rotm = sb("rotm", [P, 32])
        tk = sb("tk", [P, 32])
        eps = sb("eps", [P, 4])
        tmp = sb("tmp", [P, 2, T])
        sq = sb("sq", [P, 2, T])
        rstd = sb("rstd", [P, T])
        arena = sb("arena", [P, ARENA])

        class Carve:

            def __init__(self, at=0):
                self.at = at

            def __call__(self, *shape):
                n = int(np.prod(shape))
                v = arena[:, self.at:self.at + n]
                self.at += n
                assert self.at <= ARENA, self.at
                if len(shape) == 2:
                    v = v.rearrange("p (a b) -> p a b", b=shape[1])
                if len(shape) == 3:
                    v = v.rearrange("p (a b c) -> p a b c", b=shape[1], c=shape[2])
                return v

        c = Carve()
        hb = c(NW, T + 32)
        cacc = c(NW, T)
        cgate = c(NW, T)
        lsq = c(5, T)
        lat = c(5, T)
        lat_end = c.at
        c = Carve()
        y32 = c(NW, T)
        Qh = [c(T) for a in range(2)]
        PTh = [c(NT, T) for a in range(2)]
        probs = c(4 * T)
        probsh = [[probs[:, 7 * P * a + 3 * P * u:7 * P * a + 3 * P * u + (3 + u) * P] for u in range(2)]
                  for a in range(2)]
        c.at -= 2 * P
        Vh = [c(NT, 64) for a in range(2)]
        Kh = [c(T) for a in range(2)]
        Q, K, PT, V, posb = Qh[0], Kh[0], PTh[0], Vh[0], Qh[0]
        memf = c(KD, MEM)
        c.at = max(c.at, lat_end)
        mgate = c(NW, T)
        xgate = c(NW, T)
        kr = c(T)
        trig = c(2, T)
        causal = kr
        st = c(24)
        xprobs = [p[:, 2:4, :].rearrange("p a (b m) -> p (a b) m", m=MEM) for p in PTh]
        xV = [v.rearrange("p a b -> p (a b)").rearrange("p (a b) -> p a b", b=P) for v in Vh]
        c = Carve()
        RKV = c(12, T)
        R, RK_, RV = RKV[:, 0:4, :], RKV[:, 4:8, :], RKV[:, 8:12, :]
        KK = c(NW, T)
        BB = c(NW, T)
        TH = c(NW, T)
        rgate = TH
        flat = tmp[:].rearrange("p a b -> p (a b)")
        AR = flat[:, 0:512].rearrange("p (a b c) -> p a b c", a=2, b=2)
        Bt = flat[:, 512:768].rearrange("p (a b) -> p a b", a=2)
        Kt = flat[:, 768:1024].rearrange("p (a b) -> p a b", a=2)
        EP = rstd[:, 0:2 * (P + 1)].rearrange("p (a b) -> p a b", a=2)
        Sm = rstd[:, 260:388].rearrange("p (a b) -> p a b", a=2)
        emid = rstd[:, 388:390]
        TM = c(6, P)
        UM = c(4, 4 * P)
        Tm = c(4, P)
        XZ = c(4, 2, P)
        Qs = c(4, P)
        QC = c(2, P + 1)
        St = c(NW, 64)
        rhs_s = Bt[:, :, :].rearrange("p a b -> p (a b)")
        sa_s = Kt[:, :, :].rearrange("p a b -> p (a b)")
        rkc = Qs[:, 0:2, :]
        EM = XZ[:, 0, :, :]
        QD = XZ[:, 1:4, :, :].rearrange("p a b c -> p (a b c)")[:, 0:2 * (P + 1)].rearrange("p (a b) -> p a b", b=P + 1)
        Vc = c(2, P)
        wa = UM[:, 0, :]
        lora = UM[:, 1, :]

        def col(name, i=0, n=1):
            a = PC1[name][0]
            return par[:, a + i:a + i + n] if isinstance(i, int) else par[:, bass.ds(i + a, n)]

        def tile(t, i):
            return t[:, i, :] if isinstance(i, int) else t[:, bass.ds(i, 1), :].rearrange("p a t -> p (a t)")

        def over_columns(v, n):
            return bass.AP(v.tensor, v.offset, [v.ap[0], [0, n]])

        block = ctx.enter_context(nc.Block())

        @block.sync
        def _(sp):
            weight_loader(sp, S, stage, stream, DEPTH * G1)

        @block.gpsimd
        def _(pool):
            def op(ins, *names):
                fin(pool, "pool_self", ins, *names)

            def select(t, pattern, base, mult, compare=ALU.is_ge, fill=0.0, *names):
                op(pool.affine_select(out=t, in_=t, compare_op=compare, fill=fill, base=base, pattern=pattern,
                                      channel_multiplier=mult), *names)

            early = 26
            op(pool.memset(ones[:], 1.0))
            op(pool.memset(ident[:], 0.0))
            select(ident[:], [[-1, P]], 0, 1, ALU.not_equal, 1.0, "ones_ready")
            weight_remainders(pool, S, give, fin, stage, wh, wl, early, last=False)
            op(pool.memset(halves[:], 1.0))
            select(halves[:, 0:64], [[0, 64]], 63, -1)
            select(halves[:, 64:P], [[0, 64]], -64, 1)
            op(pool.memset(future[:], 0.0))
            select(future[:], [[-1, P]], 0, 1, ALU.is_ge, MASKED)
            op(pool.memset(after[:], 1.0))
            select(after[:, 0, :], [[1, P]], -1, -1)
            select(after[:, 1, :], [[1, P]], 0, -1)
            op(pool.memset(before[:], 1.0))
            select(before[:], [[-1, P]], -1, 1)
            op(pool.memset(rotm[:], 0.0))
            select(rotm[64:96, :], [[-1, 32]], -16, 1, ALU.not_equal, -1.0)
            select(rotm[64:96, :], [[-1, 32]], 16, 1, ALU.not_equal, 1.0)
            scratch = memf.rearrange("p a b -> p (a b)")[:, KD * MEM - 2 * P:]
            for n in range(7):
                b = 1 << n
                m = scratch.rearrange("p (o j h c) -> p o j h c", o=2, h=2, c=b)
                op(pool.memset(scratch, 0.0))
                for o in range(2):
                    v = m[:, o, :, o, :]
                    op(pool.memset(v, 1.0))
                    lo = b * (1 - o)
                    pat = [[-2 * b, P // (2 * b)], [0, b]]
                    select(v, pat, -lo, 1)
                    select(v, [[2 * b, P // (2 * b)], [0, b]], lo + b - 1, -1)
                op(pool.tensor_copy(level[:, n, :, :].rearrange("p a b -> p (a b)"), scratch))
            for layer in range(DEPTH):
                give(pool, "consts_pe", "consts_act", "consts_dve")
            weight_remainders(pool, S, give, fin, stage, wh, wl, DEPTH * G1 - early, first=False)

        @block.tensor
        def _(pe):
            pe.wait_ge(S["ones_ready"], 1)
            pe.sem_inc(S["ones_ready"], -1)
            proj = Projector(pe, S, wh, wl)
            X = (xh, xl)

            def gates():
                with pe.Fori(0, NW // 2):
                    for s, g in enumerate((g0, g1)):
                        pe.wait_ge(S[f"g{s}_free"], 1)
                        pe.sem_inc(S[f"g{s}_free"], -1)
                        proj.channels(g[:], proj.group(), X, KD, P, done="gate_proj")

            def total(out, tiles, want, done, matrix=ones):
                pe.wait_ge(S[want], 1)
                pe.sem_inc(S[want], -1)
                for n, t in enumerate(tiles):
                    ins = pe.matmul(out, matrix[:], t, start=n == 0, stop=n == len(tiles) - 1)
                ins.then_inc(S[done], 1)

            def spread(out, stats, n, done):
                m = P // n
                for t in range(NT):
                    for j in range(n):
                        ins = pe.matmul(out[j * m:(j + 1) * m, t * P:(t + 1) * P],
                                        over_columns(stats[:, t * n + j:t * n + j + 1], m), ident[:], start=True,
                                        stop=True)
                ins.then_inc(S[done], 1)

            def by_token(out, squares, n, columns, first, last, *then):
                for t in range(NT):
                    ins = pe.matmul(out[:, t * n:(t + 1) * n], squares[:, t * P:(t + 1) * P], columns,
                                    start=first and (last or t == 0), stop=last and (first or t == NT - 1))
                ins.then_inc(S[then[0]], 1)

            def layer_norm(summed, count):
                total(A[0][:], summed, "ln_in", "ln_sum")
                for i in range(count):
                    pe.wait_ge(S[f"sq{i % 2}_ready"], 1)
                    pe.sem_inc(S[f"sq{i % 2}_ready"], -1)
                    by_token(A[1], sq[:, i % 2, :], 1, ones[:, 0:1], i == 0, i == count - 1, f"sq{i % 2}_used")
                pe.wait_ge(S["rstd_ready"], 1)
                pe.sem_inc(S["rstd_ready"], -1)
                spread(A[5], tk, 1, "rstd_spread")

            def merge(slot):
                for s, g in enumerate((g0, g1)):
                    pe.wait_ge(S[f"g{s}_free"], 1)
                    pe.sem_inc(S[f"g{s}_free"], -1)
                    proj.channels(g[:], proj.group(), X, KD, P, done="merge_gate")
                pe.wait_ge(S["y_ready"], 1)
                pe.sem_inc(S["y_ready"], -1)
                w = proj.group()
                for s, g in enumerate((g0, g1)):
                    pe.wait_ge(S[f"g{s}_free"], 1)
                    pe.sem_inc(S[f"g{s}_free"], -1)
                    proj.channels(g[:], w, (yh[:, 4 * slot:4 * slot + 4, :], yl[:, 4 * slot:4 * slot + 4, :]), NW,
                                  2 * P, c0=s * P, done="merge_proj")

            def merge_quarter(q, chunk):
                group, part = q // 4, q % 4
                slot, step = (2, 0, 1)[group // 3], group % 3
                if part == 0:
                    chunk_w[0] = proj.group()
                s = step if step < 2 else part // 2
                if part == 0 or (step == 2 and part == 2):
                    pe.wait_ge(S[f"g{s}_free"], 1)
                    pe.sem_inc(S[f"g{s}_free"], -1)
                if step < 2:
                    proj.channels((g0, g1)[s][:], chunk_w[0], X, 2, P, c0=2 * part * P, k0=2 * part, more=part < 3,
                                  first=part == 0, done="merge_gate" if part == 3 else None)
                else:
                    k = 2 * (part % 2)
                    proj.channels((g0, g1)[s][:], chunk_w[0], (yh, yl), 2, 2 * P, c0=2 * k * P + s * P,
                                  k0=4 * slot + k, more=k == 0, first=k == 0, done="merge_proj" if k else None)

            chunk_w = [None]

            def mla_pair():
                for a in range(2):
                    h, lo = proj.group()
                    pe.wait_ge(S["g0_free"], 1)
                    pe.sem_inc(S["g0_free"], -1)
                    proj.channels(g0[0:96, :], (h[:, 0:288], lo[:, 0:288]), (yh[:, 4:7, :], yl[:, 4:7, :]), 3, 96,
                                  cn=96, done="q_proj")
                    pe.wait_ge(S["g1_free"], 1)
                    pe.sem_inc(S["g1_free"], -1)
                    proj.channels(g1[:], (h[:, 288:544], lo[:, 288:544]), (yh[:, 8:10, :], yl[:, 8:10, :]), 2, P,
                                  done="kv_proj")
                    pe.wait_ge(S["q_raw"], 1)
                    pe.sem_inc(S["q_raw"], -1)
                    pe.wait_ge(S[f"a{2 + a}_free"], 1)
                    pe.sem_inc(S[f"a{2 + a}_free"], -1)
                    pe.matmul(A[2 + a][64:96, :], rotm[64:96, :], Qh[a][64:96, :], start=True, stop=True)\
                      .then_inc(S["q_rot"], 1)
                for a in range(2):
                    pe.wait_ge(S["v_raw"], 1)
                    pe.sem_inc(S["v_raw"], -1)
                    pe.wait_ge(S[f"a{4 + a}_free"], 1)
                    pe.sem_inc(S[f"a{4 + a}_free"], -1)
                    for t in range(NT):
                        ins = pe.transpose(A[4 + a][:, 64 * t:64 * t + 64], PTh[a][64:P, 0, t * P:(t + 1) * P],
                                           ident[64:P, 64:P])
                    ins.then_inc(S["v_turned"], 1)

                def scores(a, t):
                    n = (t + 1) * P
                    pe.wait_ge(S[f"a{a}_free"], 1)
                    pe.sem_inc(S[f"a{a}_free"], -1)
                    pe.matmul(A[a][:, 0:n], Qh[a][0:96, t * P:n], Kh[a][0:96, 0:n], start=True, stop=True)\
                      .then_inc(S["scores"], 1)

                for a in range(2):
                    pe.wait_ge(S["qk_ready"], 1)
                    pe.sem_inc(S["qk_ready"], -1)
                    pe.wait_ge(S["k_ready"], 1)
                    pe.sem_inc(S["k_ready"], -1)
                    scores(a, 0)
                for t in range(NT):
                    if t + 1 < NT:
                        for a in range(2):
                            scores(a, t + 1)
                    for a in range(2):
                        pe.wait_ge(S["probs_ready"], 1)
                        pe.sem_inc(S["probs_ready"], -1)
                        pe.wait_ge(S[f"a{2 + a}_free"], 1)
                        pe.sem_inc(S[f"a{2 + a}_free"], -1)
                        for i in range(t + 1):
                            ins = pe.transpose(A[2 + a][:, i * P:(i + 1) * P], probsh[a][t % 2][:, i * P:(i + 1) * P],
                                               ident[:])
                        ins.then_inc(S["probs_turned"], 1)
                for a in range(2):
                    pe.wait_ge(S["v_ready"], 1)
                    pe.sem_inc(S["v_ready"], -1)
                    pe.wait_ge(S["weights_ready"], 1)
                    pe.sem_inc(S["weights_ready"], -1)
                    pe.wait_ge(S[f"a{4 + a}_free"], 1)
                    pe.sem_inc(S[f"a{4 + a}_free"], -1)
                    for i in range(NT):
                        ins = pe.matmul(A[4 + a][64 * a:64 * a + 64, i * P:T], Vh[a][:, i, :], PTh[a][:, i, i * P:T],
                                        start=i == 0, stop=i == NT - 1)
                    ins.then_inc(S["head_out"], 1)

            def rwkv_half(g, chunk):
                for q in range(6):
                    merge_quarter(18 * g + q, chunk)
                r = [slice(64 * (j % 2), 64 * (j % 2) + 64) for j in range(4)]
                pe.wait_ge(S["ab_ready"], 1)
                pe.sem_inc(S["ab_ready"], -1)
                for j in range(4):
                    pe.wait_ge(S[f"a{j}_free"], 1)
                    pe.sem_inc(S[f"a{j}_free"], -1)
                    x = AR[r[j], j // 2, :, :].rearrange("p a b -> p (a b)")
                    pe.matmul(A[j][:, 0:256], Bt[r[j], j // 2, :], x, start=True, stop=True)
                    pe.matmul(A[j][:, 256:512], Kt[r[j], j // 2, :], x, start=True, stop=True)\
                      .then_inc(S["um_out"], 1)
                for p in range(2):
                    pe.wait_ge(S[f"a{4 + p}_free"], 1)
                    pe.sem_inc(S[f"a{4 + p}_free"], -1)
                    for i in range(2):
                        j = 2 * i + p
                        ins = pe.matmul(A[4 + p][:, i * P:(i + 1) * P], AR[r[j], i, 0, :], Bt[r[j], i, :],
                                        start=True, stop=True)
                    ins.then_inc(S["t_out"], 1)
                pe.wait_ge(S["a0_free"], 1)
                pe.sem_inc(S["a0_free"], -1)
                for i in range(2):
                    pe.transpose(A[0][:, i * P:(i + 1) * P], Vc[:, i, :], ident[:])
                    ins = pe.transpose(A[0][:, (2 + i) * P:(3 + i) * P], Bt[:, i, :], ident[:])
                ins.then_inc(S["turned"], 1)
                pe.wait_ge(S["a1_free"], 1)
                pe.sem_inc(S["a1_free"], -1)
                for i in range(2):
                    pe.transpose(A[1][:, i * P:(i + 1) * P], Kt[:, i, :], ident[:])
                pe.wait_ge(S["rk_ready"], 1)
                pe.sem_inc(S["rk_ready"], -1)
                ins = pe.matmul(A[1][:, 256:512], halves[:], rkc.rearrange("p a b -> p (a b)"), start=True, stop=True)
                ins.then_inc(S["turned"], 1)
                pe.wait_ge(S["xz_ready"], 1)
                pe.sem_inc(S["xz_ready"], -1)
                for n in range(1, 7):
                    pe.wait_ge(S["a4_free"], 1)
                    pe.sem_inc(S["a4_free"], -1)
                    for j in range(4):
                        ins = pe.matmul(A[4][:, j * P:(j + 1) * P], Tm[:, j, :], XZ[:, j, 1, :], start=True, stop=True)
                    ins.then_inc(S["uz_out"], 1)
                    merge_quarter(18 * g + 4 + 2 * n, chunk)
                    pe.wait_ge(S["uz_ready"], 1)
                    pe.sem_inc(S["uz_ready"], -1)
                    for p, b in ((0, 5), (1, 3)):
                        pe.wait_ge(S[f"a{b}_free"], 1)
                        pe.sem_inc(S[f"a{b}_free"], -1)
                        for q in range(2):
                            j = 2 * p + q
                            pe.matmul(A[b][:, q * 256:q * 256 + P], Qs[:, j, :], XZ[:, j, 0, :], start=True, stop=True)
                            ins = pe.matmul(A[b][:, q * 256 + P:q * 256 + 256], XZ[:, j, 0, :], Qs[:, j, :],
                                            start=True, stop=True)
                        ins.then_inc(S["fill_out"], 1)
                    merge_quarter(18 * g + 5 + 2 * n, chunk)
                    pe.wait_ge(S["xz_ready"], 1)
                    pe.sem_inc(S["xz_ready"], -1)
                pe.wait_ge(S["turned_ready"], 1)
                pe.sem_inc(S["turned_ready"], -1)
                pe.wait_ge(S["sm_ready"], 1)
                pe.sem_inc(S["sm_ready"], -1)
                for p in range(2):
                    pe.wait_ge(S[f"a{2 + p}_free"], 1)
                    pe.sem_inc(S[f"a{2 + p}_free"], -1)
                    for j in (p, p + 2):
                        o = A[2 + p][:, 32 * (j - p):32 * (j - p) + 64]
                        pe.matmul(o, UM[:, j, 256:384], TM[:, j // 2, r[j]], start=True, stop=False)
                        ins = pe.matmul(o, AR[r[j], j // 2, 0, :], Sm[r[j], j // 2, :], start=False, stop=True)
                    ins.then_inc(S["rhs_out"], 1)
                pe.wait_ge(S["rhs_ready"], 1)
                pe.sem_inc(S["rhs_ready"], -1)
                pe.wait_ge(S["a0_free"], 1)
                pe.sem_inc(S["a0_free"], -1)
                for j in range(4):
                    ins = pe.matmul(A[0][:, 64 * j:64 * j + 64], XZ[:, j, 1, :], rhs_s[:, 64 * j:64 * j + 64],
                                    start=True, stop=True)
                ins.then_inc(S["sa_out"], 1)
                pe.wait_ge(S["sa_ready"], 1)
                pe.sem_inc(S["sa_ready"], -1)
                pe.wait_ge(S["a4_free"], 1)
                pe.sem_inc(S["a4_free"], -1)
                for j in range(4):
                    o = A[4][r[j], (j // 2) * P:(j // 2 + 1) * P]
                    pe.matmul(o, sa_s[:, 64 * j:64 * j + 64], UM[:, j, 128:256], start=True, stop=False)
                    pe.matmul(o, TM[:, j // 2, r[j]], UM[:, j, 384:512], start=False, stop=False)
                    ins = pe.matmul(o, Sm[r[j], j // 2, :], AR[r[j], j // 2, 1, :], start=False, stop=True)
                ins.then_inc(S["y_out"], 1)
                pe.wait_ge(S["a5_free"], 1)
                pe.sem_inc(S["a5_free"], -1)
                for j in range(4):
                    o = A[5][r[j], (j // 2) * 64:(j // 2 + 1) * 64]
                    pe.matmul(o, TM[:, 2 + j // 2, r[j]], sa_s[:, 64 * j:64 * j + 64], start=True, stop=False)
                    ins = pe.matmul(o, TM[:, 4 + j // 2, r[j]], TM[:, j // 2, r[j]], start=False, stop=True)
                ins.then_inc(S["state_out"], 1)

            with pe.Fori(0, DEPTH) as layer:
                for i in range(NW):
                    s = i % 2
                    pe.wait_ge(S[("g0_free", "a2_free")[s]], 1)
                    pe.sem_inc(S[("g0_free", "a2_free")[s]], -1)
                    proj.channels((g0, A[2])[s][:], proj.group(), X, KD, P, done="val_proj",
                                  each=None if i else "x_ready")
                    pe.wait_ge(S[("g1_free", "a3_free")[s]], 1)
                    pe.sem_inc(S[("g1_free", "a3_free")[s]], -1)
                    proj.channels((g1, A[3])[s][:], proj.group(), X, KD, P, done="gate_proj")
                gates()
                for i in range(2):
                    for j in range(7):
                        pe.wait_ge(S[f"g{j % 2}_free"], 1)
                        pe.sem_inc(S[f"g{j % 2}_free"], -1)
                        proj.channels((g0, g1)[j % 2][:], proj.group(), X, KD, P,
                                      done="lat_proj" if j < 3 else "gate_proj")
                layer_norm([cacc[:, i, :] for i in range(NW)], NW)
                for b, tiles in ((2, range(3)), (3, range(3, 5))):
                    pe.wait_ge(S["lat_sq"], 1)
                    pe.sem_inc(S["lat_sq"], -1)
                    pe.wait_ge(S[f"a{b}_free"], 1)
                    pe.sem_inc(S[f"a{b}_free"], -1)
                    for t in range(NT):
                        for i in tiles:
                            ins = pe.matmul(A[b][:, t:t + 1], lsq[:, i, t * P:(t + 1) * P], ones[:, 0:1],
                                            start=i == tiles[0], stop=i == tiles[-1])
                    ins.then_inc(S["lat_sum"], 1)
                pe.wait_ge(S["rstd_ready"], 1)
                pe.sem_inc(S["rstd_ready"], -1)
                for b in range(2):
                    spread(A[2 + b], tk[:, NT * b:NT * b + NT], 1, "rstd_spread")
                pe.wait_ge(S["kr_pe"], 1)
                pe.sem_inc(S["kr_pe"], -1)
                pe.wait_ge(S["consts_pe"], 1)
                pe.sem_inc(S["consts_pe"], -1)
                pe.wait_ge(S["a4_free"], 1)
                pe.sem_inc(S["a4_free"], -1)
                pe.matmul(A[4][64:96, :], rotm[64:96, :], kr[64:96, :], start=True, stop=True).then_inc(S["k_rot"], 1)
                pe.wait_ge(S["lat_ready"], 1)
                pe.sem_inc(S["lat_ready"], -1)
                with pe.Fori(0, NW):
                    mla_pair()
                pe.wait_ge(S["mem_ready"], 1)
                pe.sem_inc(S["mem_ready"], -1)
                with pe.Fori(0, NW // 2):
                    mem = [y[:, 4:8, :].rearrange("p a (b m) -> p (a b) m", m=MEM) for y in (yh, yl)]
                    for a in range(2):
                        ga, gb = (g0, g1) if a == 0 else (g1, g0)
                        pe.wait_ge(S[f"g{a}_free"], 1)
                        pe.sem_inc(S[f"g{a}_free"], -1)
                        proj.channels(ga[:], proj.group(), X, KD, P, done="q_proj")
                        pe.wait_ge(S[f"g{1 - a}_free"], 1)
                        pe.sem_inc(S[f"g{1 - a}_free"], -1)
                        proj.channels(gb[:, 0:MEM], proj.group(), mem, KD, P, done="k_proj")
                        pe.wait_ge(S[f"g{a}_free"], 1)
                        pe.sem_inc(S[f"g{a}_free"], -1)
                        proj.channels(ga[:, 0:MEM], proj.group(), mem, KD, P, done="v_proj")
                        pe.wait_ge(S["qk_ready"], 1)
                        pe.sem_inc(S["qk_ready"], -1)
                        for b in range(2):
                            pe.wait_ge(S[f"a{3 * a + b}_free"], 1)
                            pe.sem_inc(S[f"a{3 * a + b}_free"], -1)
                            for t in (2 * b, 2 * b + 1):
                                ins = pe.matmul(A[3 * a + b][:, (t % 2) * MEM:(t % 2 + 1) * MEM],
                                                Qh[a][:, t * P:(t + 1) * P], Kh[a][:, 0:MEM], start=True, stop=True)
                            ins.then_inc(S["scores"], 1)
                        pe.wait_ge(S["v_raw"], 1)
                        pe.sem_inc(S["v_raw"], -1)
                        pe.wait_ge(S[f"a{3 * a + 2}_free"], 1)
                        pe.sem_inc(S[f"a{3 * a + 2}_free"], -1)
                        for t in range(2):
                            ins = pe.transpose(A[3 * a + 2][:, t * P:(t + 1) * P], PTh[a][:, 0, t * P:(t + 1) * P],
                                               ident[:])
                        ins.then_inc(S["v_turned"], 1)
                    for a in range(2):
                        pe.wait_ge(S["probs_ready"], 1)
                        pe.sem_inc(S["probs_ready"], -1)
                        for i in range(2):
                            pe.wait_ge(S[f"a{3 * a + i}_free"], 1)
                            pe.sem_inc(S[f"a{3 * a + i}_free"], -1)
                            for t in range(NT):
                                ins = pe.transpose(A[3 * a + i][:, t * P:(t + 1) * P],
                                                   xprobs[a][:, t, i * P:(i + 1) * P], ident[:])
                            ins.then_inc(S["probs_turned"], 1)
                        pe.wait_ge(S["v_ready"], 1)
                        pe.sem_inc(S["v_ready"], -1)
                        pe.wait_ge(S["weights_ready"], 1)
                        pe.sem_inc(S["weights_ready"], -1)
                        pe.wait_ge(S[f"a{3 * a + 2}_free"], 1)
                        pe.sem_inc(S[f"a{3 * a + 2}_free"], -1)
                        for i in range(2):
                            ins = pe.matmul(A[3 * a + 2][:], xV[a][:, i, :], PTh[a][:, i, :], start=i == 0,
                                            stop=i == 1)
                        ins.then_inc(S["head_out"], 1)
                with pe.Fori(0, 6):
                    for s, g in enumerate((g0, g1)):
                        pe.wait_ge(S[f"g{s}_free"], 1)
                        pe.sem_inc(S[f"g{s}_free"], -1)
                        proj.channels(g[:], proj.group(), X, KD, P, done="rw_proj")
                pe.wait_ge(S["g0_free"], 1)
                pe.sem_inc(S["g0_free"], -1)
                proj.channels(g0[:], proj.group(), X, NW, P, more=True)
                proj.channels(g0[:], proj.group(), X, NW, P, done="rw_proj", k0=NW, first=False)
                pe.wait_ge(S["a2_free"], 1)
                pe.sem_inc(S["a2_free"], -1)
                pe.wait_ge(S["wa_ready"], 1)
                pe.sem_inc(S["wa_ready"], -1)
                for i in range(NW):
                    pe.wait_ge(S["a0_free"], 1)
                    pe.sem_inc(S["a0_free"], -1)
                    pe.matmul(A[0][:], lora[0:64, i * P:(i + 1) * P], wa[0:64, :], start=True, stop=True)\
                      .then_inc(S["lora_w"], 1)
                    pe.wait_ge(S["a1_free"], 1)
                    pe.sem_inc(S["a1_free"], -1)
                    pe.matmul(A[1][:], lora[64:P, i * P:(i + 1) * P], wa[64:P, :], start=True, stop=True)\
                      .then_inc(S["lora_a"], 1)
                    pe.wait_ge(S[f"sq{i % 2}_ready"], 1)
                    pe.sem_inc(S[f"sq{i % 2}_ready"], -1)
                    by_token(A[2][:, 8 * i:8 * i + 8], sq[:, i % 2, :], 2, halves[:, 0:P:64], True, True,
                             f"sq{i % 2}_used")
                pe.wait_ge(S["rstd_ready"], 1)
                pe.sem_inc(S["rstd_ready"], -1)
                for i in range(NW):
                    if i:
                        pe.wait_ge(S[f"a{2 + i}_free"], 1)
                        pe.sem_inc(S[f"a{2 + i}_free"], -1)
                    spread(A[2 + i], tk[:, 8 * i:8 * i + 8], 2, "rstd_spread")
                with pe.Fori(0, NT // 2) as cc:
                    for u in range(2):
                        chunk = cc * 2 + u
                        for g in range(2):
                            rwkv_half(g, chunk)
                def gate_pair():
                    for s, g in enumerate((g0, g1)):
                        pe.wait_ge(S[f"g{s}_free"], 1)
                        pe.sem_inc(S[f"g{s}_free"], -1)
                        proj.channels(g[:], proj.group(), X, KD, P, done="gate_proj")

                pe.wait_ge(S["gn_in"], 1)
                pe.sem_inc(S["gn_in"], -1)
                for i in range(NW):
                    pe.wait_ge(S[f"a{i}_free"], 1)
                    pe.sem_inc(S[f"a{i}_free"], -1)
                    pe.matmul(A[i][:], halves[:], R[:, i, :], start=True, stop=True).then_inc(S["gn_sum"], 1)
                gate_pair()
                pe.wait_ge(S["a4_free"], 1)
                pe.sem_inc(S["a4_free"], -1)
                for i in range(NW):
                    pe.wait_ge(S[f"sq{i % 2}_ready"], 1)
                    pe.sem_inc(S[f"sq{i % 2}_ready"], -1)
                    by_token(A[4][:, 8 * i:8 * i + 8], sq[:, i % 2, :], 2, halves[:, 0:P:64], True, True,
                             f"sq{i % 2}_used")
                pe.wait_ge(S["rstd_ready"], 1)
                pe.sem_inc(S["rstd_ready"], -1)
                for i in range(NW):
                    pe.wait_ge(S[f"a{i}_free"], 1)
                    pe.sem_inc(S[f"a{i}_free"], -1)
                    spread(A[i], tk[:, 8 * i:8 * i + 8], 2, "rstd_spread")
                gate_pair()
                with pe.Fori(0, 2):
                    for u in range(2):
                        merge(0)
                pe.wait_ge(S["merged_ready"], 1)
                pe.sem_inc(S["merged_ready"], -1)
                with pe.Fori(0, KD // 2):
                    for s, g in enumerate((g0, g1)):
                        pe.wait_ge(S[f"g{s}_free"], 1)
                        pe.sem_inc(S[f"g{s}_free"], -1)
                        proj.channels(g[:], proj.group(), (yh, yl), KD, P, done="out_proj", k0=4)
                layer_norm([rstd[:]], KD)

        @block.scalar
        def _(act):
            round_next = rounder(act, S, stage, wh)
            half = lambda t, i: t[:, i:i + 1] if isinstance(i, int) else t[:, bass.ds(i, 1)]

            def op(ins, *names):
                fin(act, "act_self", ins, *names)

            def gates(n=2):
                with act.Fori(0, n):
                    for s, g in enumerate((g0, g1)):
                        round_next()
                        act.wait_ge(S["gate_proj"], 1)
                        act.sem_inc(S["gate_proj"], -1)
                        act.wait_ge(S[f"sq{s}_used"], 1)
                        act.sem_inc(S[f"sq{s}_used"], -1)
                        act.activation(sq[:, s, :], g[:], ACT.Tanh, scale=0.5).then_inc(S["tanh_ready"], 1)

            def norm_squares(tiles, n):
                for i, t in enumerate(tiles):
                    act.wait_ge(S["centered"], 1)
                    act.sem_inc(S["centered"], -1)
                    act.wait_ge(S[f"sq{i % 2}_used"], 1)
                    act.sem_inc(S[f"sq{i % 2}_used"], -1)
                    act.activation(sq[:, i % 2, :], t, ACT.Square).then_inc(S[f"sq{i % 2}_ready"], 1)
                by_token_root(A[1], NT, 1.0 / n, 0)

            def by_token_root(src, count, scale, e):
                act.wait_ge(S["sq0_used"], 1)
                act.sem_inc(S["sq0_used"], -1)
                act.wait_ge(S["sq1_used"], 1)
                act.sem_inc(S["sq1_used"], -1)
                if e is None:
                    act.activation(tk[:, 0:count], src[:, 0:count], ACT.Sqrt).then_inc(S["root"], 1)
                else:
                    act.activation(tk[:, 0:count], src[:, 0:count], ACT.Sqrt, scale=scale, bias=eps[:, e:e + 1])\
                       .then_inc(S["root"], 1)
                give(act, "sq0_used", "sq1_used")

            def upper(dst, want, src=None, scale=1.0):
                act.wait_ge(S[want], 1)
                act.sem_inc(S[want], -1)
                act.activation(dst, src, ACT.Copy, scale=scale).then_inc(S["hi_ready"], 1)

            def mla_pair():
                for a in range(2):
                    round_next()
                    act.wait_ge(S["q_proj"], 1)
                    act.sem_inc(S["q_proj"], -1)
                    act.wait_ge(S[f"qk{a}_free"], 1)
                    act.sem_inc(S[f"qk{a}_free"], -1)
                    op(act.activation(Qh[a][0:96, :], g0[0:96, :], ACT.Copy, scale=-96 ** -0.5), "g0_free", "q_raw",
                       "q_dve")
                    act.wait_ge(S["kv_proj"], 1)
                    act.sem_inc(S["kv_proj"], -1)
                    act.wait_ge(S[f"v{a}_free"], 1)
                    act.sem_inc(S[f"v{a}_free"], -1)
                    op(act.activation(PTh[a][64:P, 0, :], g1[64:P, :], ACT.Copy), "v_raw")
                    op(act.activation(Kh[a][0:64, :], g1[0:64, :], ACT.Copy), "g1_free", "k_ready")
                for a in range(2):
                    act.wait_ge(S["v_turned"], 1)
                    act.sem_inc(S["v_turned"], -1)
                    op(act.activation(Vh[a].rearrange("p a b -> p (a b)"), A[4 + a][:, 0:256], ACT.Copy),
                       f"a{4 + a}_free", "v_ready")

                def exponential(a, t):
                    act.wait_ge(S["max_ready"], 1)
                    act.sem_inc(S["max_ready"], -1)
                    n, c = (t + 1) * P, 2 * a + t % 2
                    act.activation(probsh[a][t % 2][:, 0:n], probsh[a][t % 2][:, 0:n], ACT.Exp, scale=-1.0,
                                   bias=st[:, c:c + 1], accum_out=st[:, 4 + c:5 + c]).then_inc(S["exp_ready"], 1)

                exponential(0, 0)
                exponential(1, 0)
                for t in range(NT):
                    for a in range(2):
                        if t + 1 < NT:
                            exponential(a, t + 1)
                        n = (t + 1) * P
                        act.wait_ge(S["probs_turned"], 1)
                        act.sem_inc(S["probs_turned"], -1)
                        op(act.activation(PTh[a][:, 0:t + 1, t * P:n],
                                          A[2 + a][:, 0:n].rearrange("p (a b) -> p a b", b=P), ACT.Copy),
                           f"a{2 + a}_free", f"probs{a}{t % 2}_free", *(["weights_ready"] if t == NT - 1 else []))

            def merge(branch, d0):
                for s, g in enumerate((g0, g1)):
                    round_next()
                    act.wait_ge(S["merge_gate"], 1)
                    act.sem_inc(S["merge_gate"], -1)
                    act.wait_ge(S[f"sq{s}_used"], 1)
                    act.sem_inc(S[f"sq{s}_used"], -1)
                    op(act.activation(sq[:, s, :], g[:], ACT.Tanh, scale=0.5,
                                      bias=der[:, bass.ds(d0 + (32 + 8 * branch + s), 1)]), f"g{s}_free",
                       "tanh_ready")
                round_next()

            def merge_quarter(q, chunk):
                group, part = q // 4, q % 4
                branch, s = group // 3 + 1, group % 3
                if part == 0:
                    round_next()
                if part == 3 and s < 2:
                    act.wait_ge(S["merge_gate"], 1)
                    act.sem_inc(S["merge_gate"], -1)
                    act.wait_ge(S[f"sq{s}_used"], 1)
                    act.sem_inc(S[f"sq{s}_used"], -1)
                    op(act.activation(sq[:, s, :], (g0, g1)[s][:], ACT.Tanh, scale=0.5,
                                      bias=der[:, bass.ds(chunk * 2 + (32 + 8 * branch + s), 1)]), f"g{s}_free",
                       "tanh_ready")

            def rwkv_half(g, chunk):
                cs = bass.ds(chunk * P, P)
                act.wait_ge(S["qd_ready"], 1)
                act.sem_inc(S["qd_ready"], -1)
                act.activation(emid[:, 0:2], QC[:, :, 64], ACT.Exp, scale=-KAPPA)
                act.activation(EP[:, :, :], QD[:, :, :], ACT.Exp, scale=-KAPPA)
                act.activation(EM[:, :, :], QD[:, :, 1:], ACT.Exp, scale=KAPPA)
                op(act.activation(Vc[:, :, :], RV[:, 2 * g:2 * g + 2, cs], ACT.Copy), "exp_ready")
                for q in range(6):
                    merge_quarter(18 * g + q, chunk)
                act.wait_ge(S["turned"], 1)
                act.sem_inc(S["turned"], -1)
                op(act.activation(TM[:, 0:4, :].rearrange("p a b -> p (a b)"), A[0][:], ACT.Copy), "a0_free")
                act.wait_ge(S["turned"], 1)
                act.sem_inc(S["turned"], -1)
                op(act.activation(TM[:, 4:6, :].rearrange("p a b -> p (a b)"), A[1][:, 0:256], ACT.Copy),
                   "bonus_sum", "turned_ready")
                for n in range(1, 7):
                    act.wait_ge(S["uz_out"], 1)
                    act.sem_inc(S["uz_out"], -1)
                    op(act.activation(Qs[:, :, :].rearrange("p a b -> p (a b)"), A[4][:], ACT.Copy), "a4_free",
                       "uz_ready")
                    merge_quarter(18 * g + 4 + 2 * n, chunk)
                    merge_quarter(18 * g + 5 + 2 * n, chunk)
                for p in range(2):
                    act.wait_ge(S["rhs_out"], 1)
                    act.sem_inc(S["rhs_out"], -1)
                    op(act.activation(rhs_s.rearrange("p (a b) -> p a b", b=64)[:, p:4:2, :],
                                      A[2 + p][:, 0:P].rearrange("p (a b) -> p a b", b=64), ACT.Copy),
                       f"a{2 + p}_free", *(["rhs_ready"] if p else []))
                act.wait_ge(S["sa_out"], 1)
                act.sem_inc(S["sa_out"], -1)
                op(act.activation(sa_s, A[0][:, 0:256], ACT.Copy), "a0_free", "sa_ready")
                act.wait_ge(S["y_out"], 1)
                act.sem_inc(S["y_out"], -1)
                op(act.activation(R[:, 2 * g:2 * g + 2, cs], A[4][:, 0:256].rearrange("p (a b) -> p a b", b=P),
                                  ACT.Copy), "a4_free", "y_written")

            act.dma_start(hT[:], x_dram.rearrange("(k p) t -> p k t", p=P)).then_inc(S["x_in"], 16)
            act.wait_ge(S["x_in"], 16)
            act.sem_inc(S["x_in"], -16)
            give(act, "sq0_used", "sq1_used")
            round_next()
            for i in range(KD):
                act.activation(xh[:, i, :], hT[:, i, :], ACT.Copy).then_inc(S["hi_ready"], 1)
            with act.Fori(0, DEPTH) as layer:
                act.wait_ge(S["par_free"], 1)
                act.sem_inc(S["par_free"], -1)
                act.dma_start(par[:], par_dram[bass.ds(layer, 1)].rearrange("a p n -> p (a n)"))\
                   .then_inc(S["par_full"], 16)
                act.wait_ge(S["par_full"], 16)
                act.sem_inc(S["par_full"], -16)
                give(act, "par_dve")
                act.wait_ge(S["derived"], 1)
                act.sem_inc(S["derived"], -1)
                with act.Fori(0, NW // 2):
                    for s in range(2):
                        round_next()
                        round_next()
                        act.wait_ge(S["gate_proj"], 1)
                        act.sem_inc(S["gate_proj"], -1)
                        act.wait_ge(S[f"sq{s}_used"], 1)
                        act.sem_inc(S[f"sq{s}_used"], -1)
                        act.activation(sq[:, s, :], (g1, A[3])[s][:], ACT.Tanh, scale=0.5)\
                           .then_inc(S["tanh_ready"], 1)
                gates()
                for i in range(2):
                    for j in range(7):
                        g = (g0, g1)[j % 2]
                        round_next()
                        if j < 3:
                            n = 3 * i + j
                            act.wait_ge(S["lat_proj"], 1)
                            act.sem_inc(S["lat_proj"], -1)
                            if n < 5:
                                op(act.activation(lsq[:, n, :], g[:], ACT.Square),
                                   *(["lat_sq"] if n in (2, 4) else []))
                            op(act.activation(lat[:, n, :] if n < 5 else kr, g[:], ACT.Copy), f"g{j % 2}_free",
                               *(["kr_pe", "kr_dve"] if n == 5 else []))
                        else:
                            act.wait_ge(S["gate_proj"], 1)
                            act.sem_inc(S["gate_proj"], -1)
                            act.wait_ge(S[f"sq{j % 2}_used"], 1)
                            act.sem_inc(S[f"sq{j % 2}_used"], -1)
                            act.activation(sq[:, j % 2, :], g[:], ACT.Tanh, scale=0.5).then_inc(S["tanh_ready"], 1)
                norm_squares([cacc[:, i, :] for i in range(NW)], W)
                for i in range(NW):
                    act.wait_ge(S["scaled"], 1)
                    act.sem_inc(S["scaled"], -1)
                    op(act.activation(cacc[:, i, :], cacc[:, i, :], ACT.Identity, scale=col("cln_g", i),
                                      bias=col("cln_b", i)))
                    act.wait_ge(S[f"sq{i % 2}_used"], 1)
                    act.sem_inc(S[f"sq{i % 2}_used"], -1)
                    act.activation(sq[:, i % 2, :], cacc[:, i, :], ACT.Tanh, scale=0.5)\
                       .then_inc(S["tanh_ready"], 1)
                    upper(yh[:, i, :], "tmp_ready", tmp[:, i % 2, :])
                for b, n in enumerate((384, 256)):
                    act.wait_ge(S["lat_sum"], 1)
                    act.sem_inc(S["lat_sum"], -1)
                    act.activation(tk[:, NT * b:NT * b + NT], A[2 + b][:, 0:NT], ACT.Sqrt, scale=1.0 / n,
                                   bias=eps[:, 1:2]).then_inc(S["root"], 1)
                act.dma_start(posb[64:96, :].bitcast(I32), bass.AP(pos_dram.tensor, pos_dram.offset, [[0, 32], [1, T]])).then_inc(S["pos_in"], 16)
                act.wait_ge(S["pos_in"], 16)
                act.sem_inc(S["pos_in"], -16)
                give(act, "pos_dve")
                act.wait_ge(S["angle"], 1)
                act.sem_inc(S["angle"], -1)
                op(act.activation(trig[64:96, 1, :], posb[64:96, :], ACT.Sin))
                op(act.activation(trig[64:96, 0, :], posb[64:96, :], ACT.Abs))
                op(act.activation(trig[64:96, 0, :], trig[64:96, 0, :], ACT.Sin, scale=-1.0, bias=eps[64:96, 3:4]),
                   "trig_ready")
                for i in range(5):
                    upper(yh[:, (4 if i < 3 else 5) + i, :], "tmp_ready", tmp[:, i % 2, :])
                with act.Fori(0, NW):
                    mla_pair()
                act.wait_ge(S["consts_act"], 1)
                act.sem_inc(S["consts_act"], -1)
                act.dma_start(memf, mem_dram.rearrange("(k p) m -> p k m", p=P)).then_inc(S["mem_in"], 16)
                upper(yh[:, 8:12, :], "y32_ready", y32)
                act.wait_ge(S["mem_in"], 16)
                act.sem_inc(S["mem_in"], -16)
                act.activation(yh[:, 4:8, :].rearrange("p a t -> p (a t)"), memf.rearrange("p a t -> p (a t)"),
                               ACT.Copy).then_inc(S["hi_ready"], 1)
                with act.Fori(0, NW // 2):
                    def turned(a):
                        for i in range(2):
                            act.wait_ge(S["probs_turned"], 1)
                            act.sem_inc(S["probs_turned"], -1)
                            op(act.activation(PTh[a][:, i, :], A[3 * a + i][:], ACT.Copy), f"a{3 * a + i}_free",
                               *(["weights_ready"] if i else []))

                    for a in range(2):
                        ga, gb = (g0, g1) if a == 0 else (g1, g0)
                        round_next()
                        act.wait_ge(S["q_proj"], 1)
                        act.sem_inc(S["q_proj"], -1)
                        act.wait_ge(S[f"qk{a}_free"], 1)
                        act.sem_inc(S[f"qk{a}_free"], -1)
                        op(act.activation(Qh[a], ga[:], ACT.Copy, scale=-128 ** -0.5), f"g{a}_free")
                        round_next()
                        act.wait_ge(S["k_proj"], 1)
                        act.sem_inc(S["k_proj"], -1)
                        op(act.activation(Kh[a][:, 0:MEM], gb[:, 0:MEM], ACT.Copy), f"g{1 - a}_free", "qk_ready")
                        round_next()
                        act.wait_ge(S["v_proj"], 1)
                        act.sem_inc(S["v_proj"], -1)
                        act.wait_ge(S[f"v{a}_free"], 1)
                        act.sem_inc(S[f"v{a}_free"], -1)
                        op(act.activation(PTh[a][:, 0, 0:MEM], ga[:, 0:MEM], ACT.Copy), f"g{a}_free", "v_raw")
                        act.wait_ge(S["v_turned"], 1)
                        act.sem_inc(S["v_turned"], -1)
                        op(act.activation(xV[a].rearrange("p a b -> p (a b)"), A[3 * a + 2][:, 0:MEM], ACT.Copy),
                           f"a{3 * a + 2}_free", "v_ready")
                        if a:
                            turned(0)
                        for b in range(2):
                            act.wait_ge(S["max_ready"], 1)
                            act.sem_inc(S["max_ready"], -1)
                            for t in (2 * b, 2 * b + 1):
                                ins = act.activation(xprobs[a][:, t, :],
                                                     A[3 * a + b][:, (t % 2) * MEM:(t % 2 + 1) * MEM], ACT.Exp,
                                                     scale=-1.0, bias=st[:, t:t + 1], accum_out=st[:, 4 + t:5 + t])
                            op(ins, f"a{3 * a + b}_free", *(["exp_ready"] if b else []))
                    turned(1)
                upper(yh[:, 4:8, :], "y32_ready", y32)
                act.wait_ge(S["y32_free"], 1)
                act.sem_inc(S["y32_free"], -1)
                with act.Fori(0, 6) as i:
                    for s, g in enumerate((g0, g1)):
                        round_next()
                        act.wait_ge(S["rw_proj"], 1)
                        act.sem_inc(S["rw_proj"], -1)
                        op(act.activation(tile(RKV, i * 2 + s), g[:], ACT.Copy, scale=half(der, i * 2 + s)),
                           "part_ready")
                round_next()
                round_next()
                act.wait_ge(S["rw_proj"], 1)
                act.sem_inc(S["rw_proj"], -1)
                op(act.activation(wa, g0[:], ACT.Copy, scale=der[:, 12:13]), "part_ready")
                act.dma_start(lora, lora_dram[bass.ds(layer, 1)].rearrange("a p n -> p (a n)"))\
                   .then_inc(S["lora_in"], 16)
                act.wait_ge(S["lora_in"], 16)
                act.sem_inc(S["lora_in"], -16)
                act.wait_ge(S["wa_mixed"], 1)
                act.sem_inc(S["wa_mixed"], -1)
                op(act.activation(wa[0:64, :], wa[0:64, :], ACT.Tanh), "wa_ready")
                for i in range(NW):
                    act.wait_ge(S["lora_w"], 1)
                    act.sem_inc(S["lora_w"], -1)
                    op(act.activation(TH[:, i, :], A[0][:], ACT.Tanh, scale=0.5, bias=der[:, 13 + i:14 + i]),
                       "a0_free")
                    act.wait_ge(S["lora_a"], 1)
                    act.sem_inc(S["lora_a"], -1)
                    op(act.activation(BB[:, i, :], A[1][:], ACT.Tanh, scale=0.5, bias=der[:, 17 + i:18 + i]),
                       "a1_free", "a_ready")
                    act.wait_ge(S["kk_ready"], 1)
                    act.sem_inc(S["kk_ready"], -1)
                    act.wait_ge(S[f"sq{i % 2}_used"], 1)
                    act.sem_inc(S[f"sq{i % 2}_used"], -1)
                    act.activation(sq[:, i % 2, :], KK[:, i, :], ACT.Square).then_inc(S[f"sq{i % 2}_ready"], 1)
                by_token_root(A[2], 32, 1.0, None)
                with act.Fori(0, NT // 2) as cc:
                    for u in range(2):
                        chunk = cc * 2 + u
                        for g in range(2):
                            rwkv_half(g, chunk)
                def gate_pair():
                    for s, g in enumerate((g0, g1)):
                        act.wait_ge(S["gate_proj"], 1)
                        act.sem_inc(S["gate_proj"], -1)
                        act.wait_ge(S[f"sq{s}_used"], 1)
                        act.sem_inc(S[f"sq{s}_used"], -1)
                        act.activation(sq[:, s, :], g[:], ACT.Tanh, scale=0.5).then_inc(S["tanh_ready"], 1)

                round_next()
                for i in range(NW):
                    act.wait_ge(S["centered"], 1)
                    act.sem_inc(S["centered"], -1)
                    act.wait_ge(S[f"sq{i % 2}_used"], 1)
                    act.sem_inc(S[f"sq{i % 2}_used"], -1)
                    act.activation(sq[:, i % 2, :], R[:, i, :], ACT.Square).then_inc(S[f"sq{i % 2}_ready"], 1)
                    if i == 1:
                        round_next()
                by_token_root(A[4], 32, 1.0 / 64, 2)
                give(act, "a4_free")
                gate_pair()
                round_next()
                for i in range(NW):
                    act.wait_ge(S["scaled"], 1)
                    act.sem_inc(S["scaled"], -1)
                    act.activation(R[:, i, :], R[:, i, :], ACT.Identity, scale=col("lnx_g", i),
                                   bias=col("lnx_b", i)).then_inc(S["affine"], 1)
                round_next()
                gate_pair()
                for i in range(NW):
                    upper(yh[:, i, :], "y32_ready", R[:, i, :])
                with act.Fori(0, 2) as i:
                    for u in range(2):
                        merge(0, i * 4 + 2 * u)
                with act.Fori(0, KD // 2):
                    round_next()
                    round_next()
                norm_squares([hT[:, i, :] for i in range(KD)], D)
                for i in range(KD):
                    act.wait_ge(S["scaled"], 1)
                    act.sem_inc(S["scaled"], -1)
                    op(act.activation(hT[:, i, :], hT[:, i, :], ACT.Identity, scale=col("ln_g", i),
                                      bias=col("ln_b", i)))
                    act.activation(xh[:, i, :], hT[:, i, :], ACT.Copy).then_inc(S["hi_ready"], 1)

        @block.vector
        def _(dve):
            def op(ins, *names):
                fin(dve, "dve_self", ins, *names)

            def stt(out, in0, scalar, in1, op0, op1, *names):
                op(dve.scalar_tensor_tensor(out=out, in0=in0, scalar=scalar, in1=in1, op0=op0, op1=op1), *names)

            def tt(out, a, b, alu, *names):
                op(dve.tensor_tensor(out, a, b, alu), *names)

            def ts(out, a, s1, s2, op0, op1, *names):
                op(dve.tensor_scalar(out, a, s1, s2, op0, op1) if s2 is not None
                   else dve.tensor_scalar(out, a, s1, None, op0), *names)

            def spread(v, n):
                return bass.AP(v.tensor, v.offset, [*v.ap, [0, n]])

            def again(v, n):
                return bass.AP(v.tensor, v.offset, [v.ap[0], [0, n], *v.ap[1:]])

            def gates(dst):
                with dve.Fori(0, NW // 2) as i:
                    for s, g in enumerate((g0, g1)):
                        dve.wait_ge(S["tanh_ready"], 1)
                        dve.sem_inc(S["tanh_ready"], -1)
                        stt(tile(dst, i * 2 + s), sq[:, s, :], 1.0, g[:], ALU.add, ALU.mult, f"g{s}_free",
                            f"sq{s}_used")

            def lower(h, lo, src, *names, scale=None):
                dve.wait_ge(S["hi_ready"], 1)
                dve.sem_inc(S["hi_ready"], -1)
                if scale is None:
                    tt(lo, src, h.bitcast(F32), ALU.subtract, *names)
                else:
                    stt(lo, src, scale, h.bitcast(F32), ALU.mult, ALU.subtract, *names)

            def by_token_reciprocal(count):
                dve.wait_ge(S["root"], 1)
                dve.sem_inc(S["root"], -1)
                op(dve.reciprocal(tk[:, 0:count], tk[:, 0:count]), "rstd_ready")

            def layer_norm(tiles, n):
                give(dve, "ln_in")
                dve.wait_ge(S["ln_sum"], 1)
                dve.sem_inc(S["ln_sum"], -1)
                for t in tiles:
                    stt(t, A[0][:], -1.0 / n, t, ALU.mult, ALU.add, "centered")
                by_token_reciprocal(NT)
                dve.wait_ge(S["rstd_spread"], 1)
                dve.sem_inc(S["rstd_spread"], -1)
                for t in tiles:
                    tt(t, t, A[5][:], ALU.mult, "scaled")

            def mla_pair(i):
                for a in range(2):
                    dve.wait_ge(S["q_dve"], 1)
                    dve.sem_inc(S["q_dve"], -1)
                    dve.wait_ge(S["q_rot"], 1)
                    dve.sem_inc(S["q_rot"], -1)
                    q = Qh[a][64:96, :]
                    tt(tmp[64:96, 1, :], q, trig[64:96, 0, :], ALU.mult)
                    tt(tmp[64:96, 0, :], A[2 + a][64:96, :], trig[64:96, 1, :], ALU.mult, f"a{2 + a}_free")
                    tt(q, tmp[64:96, 1, :], tmp[64:96, 0, :], ALU.add, "qk_ready")

                def maximum(a, t):
                    n, c = (t + 1) * P, 2 * a + t % 2
                    dve.wait_ge(S["scores"], 1)
                    dve.sem_inc(S["scores"], -1)
                    dve.wait_ge(S[f"probs{a}{t % 2}_free"], 1)
                    dve.sem_inc(S[f"probs{a}{t % 2}_free"], -1)
                    op(dve.tensor_tensor_reduce(probsh[a][t % 2][:, 0:n], A[a][:, 0:n], causal[:, T - n:T], 1.0,
                                                3e38, ALU.add, ALU.min, st[:, c:c + 1]),
                       f"a{a}_free", "max_ready", *([f"qk{a}_free"] if t == NT - 1 else []))

                maximum(0, 0)
                maximum(1, 0)
                for t in range(NT):
                    for a in range(2):
                        if t + 1 < NT:
                            maximum(a, t + 1)
                        n, c = (t + 1) * P, 4 + 2 * a + t % 2
                        dve.wait_ge(S["exp_ready"], 1)
                        dve.sem_inc(S["exp_ready"], -1)
                        op(dve.reciprocal(st[:, 8:9], st[:, c:c + 1]))
                        ts(probsh[a][t % 2][:, 0:n], probsh[a][t % 2][:, 0:n], st[:, 8:9], None, ALU.mult, None,
                           "probs_ready")
                for a in range(2):
                    rows = slice(64 * a, 64 * a + 64)
                    dve.wait_ge(S["head_out"], 1)
                    dve.sem_inc(S["head_out"], -1)
                    stt(y32[rows, bass.ds(i, 1), :].rearrange("p a t -> p (a t)"), A[4 + a][rows, :], 0.5,
                        mgate[rows, bass.ds(i, 1), :].rearrange("p a t -> p (a t)"), ALU.mult, ALU.mult,
                        f"a{4 + a}_free", f"v{a}_free")

            def merge(d0):
                for s, g in enumerate((g0, g1)):
                    dve.wait_ge(S["tanh_ready"], 1)
                    dve.sem_inc(S["tanh_ready"], -1)
                    dve.wait_ge(S["merge_proj"], 1)
                    dve.sem_inc(S["merge_proj"], -1)
                    h = tile(hT, d0 + s)
                    stt(sq[:, s, :], sq[:, s, :], 1.0, g[:], ALU.add, ALU.mult, f"g{s}_free")
                    tt(h, h, sq[:, s, :], ALU.add, f"sq{s}_used")
                    hi, lo = tile(yh, d0 + s + 4), tile(yl, d0 + s + 4)
                    ts(hi, h, 0.5, None, ALU.mult, None)
                    stt(lo, h, 0.5, hi.bitcast(F32), ALU.mult, ALU.subtract)

            def merge_quarter(q, chunk):
                group, part = q // 4, q % 4
                if group % 3 < 2 or part % 2 == 0:
                    return
                s = part // 2
                g = (g0, g1)[s]
                dve.wait_ge(S["tanh_ready"], 1)
                dve.sem_inc(S["tanh_ready"], -1)
                dve.wait_ge(S["merge_proj"], 1)
                dve.sem_inc(S["merge_proj"], -1)
                h = tile(hT, chunk * 2 + s)
                if group < 3:
                    stt(h, sq[:, s, :], 1.0, g[:], ALU.add, ALU.mult, f"g{s}_free", f"sq{s}_used")
                else:
                    stt(sq[:, s, :], sq[:, s, :], 1.0, g[:], ALU.add, ALU.mult, f"g{s}_free")
                    tt(h, h, sq[:, s, :], ALU.add, f"sq{s}_used")

            def rwkv_half(g, chunk):
                cs = bass.ds(chunk * P, P)
                two = slice(2 * g, 2 * g + 2)
                for i in range(2):
                    op(dve.tensor_tensor_scan(QC[:, i, 1:], TH[:, 2 * g + i, cs], ones[:], 0.0, ALU.add, ALU.add))
                mid = QC[:, :, 64]
                tt(QD[:, :, :], QC[:, :, :], spread(mid, P + 1), ALU.subtract, "qd_ready")
                dve.wait_ge(S["exp_ready"], 1)
                dve.sem_inc(S["exp_ready"], -1)
                dve.scalar_tensor_tensor(out=AR[:, :, 0, :], in0=KK[:, two, cs], scalar=-1.0, in1=EP[:, :, 0:P],
                                         op0=ALU.mult, op1=ALU.mult).then_inc(S["dve_self"], 1)
                dve.tensor_tensor(AR[:, :, 1, :], R[:, two, cs], EP[:, :, 1:], ALU.mult).then_inc(S["dve_self"], 1)
                dve.scalar_tensor_tensor(out=Bt[:, :, :], in0=BB[:, two, cs], scalar=0.5, in1=EM[:, :, :],
                                         op0=ALU.mult, op1=ALU.mult).then_inc(S["dve_self"], 1)
                dve.tensor_tensor(Kt[:, :, :], RK_[:, two, cs], EM[:, :, :], ALU.mult).then_inc(S["dve_self"], 1)
                dve.wait_ge(S["dve_self"], 4)
                dve.sem_inc(S["dve_self"], -4)
                give(dve, "ab_ready")
                tt(rkc, R[:, two, cs], RK_[:, two, cs], ALU.mult)
                tt(rkc, rkc, spread(col("r_k", 2 * g, 2), P), ALU.mult, "rk_ready")
                op(dve.tensor_copy(XZ[:, :, :, :].rearrange("p a b c -> p (a b) c"), again(ident[:], 8)))
                a2 = after[:, :, :].rearrange("p a b -> p (a b)")
                for q in range(6):
                    merge_quarter(18 * g + q, chunk)
                for j in range(4):
                    dve.wait_ge(S["um_out"], 1)
                    dve.sem_inc(S["um_out"], -1)
                    tt(UM[:, j, :].rearrange("p (a b) -> p a b", a=2), A[j][:].rearrange("p (a b) -> p a b", a=2),
                       again(a2, 2), ALU.mult, f"a{j}_free")
                for p in range(2):
                    dve.wait_ge(S["t_out"], 1)
                    dve.sem_inc(S["t_out"], -1)
                    tt(Tm[:, p:4:2, :], A[4 + p][:, 0:256].rearrange("p (a b) -> p a b", a=2), again(before[:], 2),
                       ALU.mult, f"a{4 + p}_free")
                op(dve.copy_predicated(XZ[:, :, 0, :], again(level[:, 0, 0, :], 4), Tm[:, :, :]))
                op(dve.copy_predicated(XZ[:, :, 1, :], again(level[:, 0, 1, :], 4), UM[:, :, 0:P]), "xz_ready")
                for i in range(2):
                    ts(Sm[:, i, :], St[:, 2 * g + i, :], emid[:, i:i + 1], None, ALU.mult, None,
                       *(["sm_ready"] if i else []))
                dve.wait_ge(S["bonus_sum"], 1)
                dve.sem_inc(S["bonus_sum"], -1)
                tt(RK_[:, two, cs], A[1][:, 256:512].rearrange("p (a b) -> p a b", a=2), Vc[:, :, :], ALU.mult,
                   "a1_free")
                for n in range(1, 7):
                    m = level[:, n, :, :].rearrange("p a b -> p (a b)")
                    merge_quarter(18 * g + 4 + 2 * n, chunk)
                    for p, b in ((0, 5), (1, 3)):
                        dve.wait_ge(S["fill_out"], 1)
                        dve.sem_inc(S["fill_out"], -1)
                        op(dve.copy_predicated(XZ[:, 2 * p:2 * p + 2, :, :].rearrange("p a b c -> p a (b c)"),
                                               again(m, 2), A[b][:].rearrange("p (a b) -> p a b", a=2)),
                           f"a{b}_free", *(["xz_ready"] if p else []))
                    merge_quarter(18 * g + 5 + 2 * n, chunk)
                dve.wait_ge(S["y_written"], 1)
                dve.sem_inc(S["y_written"], -1)
                dve.wait_ge(S["state_out"], 1)
                dve.sem_inc(S["state_out"], -1)
                tt(Sm[:, :, :], A[5][:, 0:P].rearrange("p (a b) -> p a b", b=64), Sm[:, :, :], ALU.add, "a5_free")
                for i in range(2):
                    ts(St[:, 2 * g + i, :], Sm[:, i, :], EP[:, i, P:P + 1], None, ALU.mult, None)

            for n, v in enumerate((1e-5, 1e-6, 64e-5, math.pi / 2)):
                op(dve.memset(eps[:, n:n + 1], v))
            for i in range(KD):
                lower(xh[:, i, :], xl[:, i, :], hT[:, i, :], "x_ready")
            give(dve, "g0_free", "g1_free", "par_free", "qk0_free", "qk1_free", "v0_free", "v1_free",
                 "probs00_free", "probs01_free", "probs10_free", "probs11_free",
                 *(f"a{i}_free" for i in range(6)))
            with dve.Fori(0, DEPTH) as layer:
                dve.wait_ge(S["par_dve"], 1)
                dve.sem_inc(S["par_dve"], -1)
                ts(der[:, 0:13], col("mu", 0, 13), -1.0, 1.0, ALU.mult, ALU.add)
                ts(der[:, 13:17], col("w0", 0, 4), 0.5, None, ALU.mult, None)
                ts(der[:, 17:21], col("a0", 0, 4), 0.5, None, ALU.mult, None)
                ts(der[:, 21:25], col("k_a", 0, 4), 0.5, None, ALU.mult, None)
                ts(der[:, 25:29], col("k_a", 0, 4), -0.5, 1.0, ALU.mult, ALU.add)
                ts(der[:, 32:64], col("b_gate", 0, 32), 0.5, None, ALU.mult, None, "derived")
                op(dve.memset(hb[:, :, 0:TAPS - 1], 0.0))
                with dve.Fori(0, NW // 2) as i:
                    for s in range(2):
                        dve.wait_ge(S["val_proj"], 1)
                        dve.sem_inc(S["val_proj"], -1)
                        dve.wait_ge(S["tanh_ready"], 1)
                        dve.sem_inc(S["tanh_ready"], -1)
                        stt(hb[:, bass.ds(i * 2 + s, 1), TAPS - 1:TAPS - 1 + T].rearrange("p a t -> p (a t)"),
                            sq[:, s, :], 1.0, (g0, A[2])[s][:], ALU.add, ALU.mult, ("g0_free", "a2_free")[s],
                            ("g1_free", "a3_free")[s], f"sq{s}_used")
                gates(cgate)
                with dve.Fori(0, NW // 2) as i:
                    for k in range(TAPS):
                        for s in range(2):
                            src = hb[:, bass.ds(i * 2 + s, 1), k:k + T].rearrange("p a t -> p (a t)")
                            w = col("conv_w", (i * 2 + s) * TAPS + k)
                            dst = tile(cacc, i * 2 + s)
                            if s == 0 and k in (15, 19, 23, 27):
                                j = (k - 15) // 4
                                u = (j + 1) % 2
                                dve.wait_ge(S["tanh_ready"], 1)
                                dve.sem_inc(S["tanh_ready"], -1)
                                stt(tile((mgate, xgate)[j % 2], i * 2 + j // 2), sq[:, u, :], 1.0, (g0, g1)[u][:],
                                    ALU.add, ALU.mult, f"g{u}_free", f"sq{u}_used")
                            if k == 0:
                                dve.tensor_scalar(dst, src, w, None, ALU.mult).then_inc(S["tap"], 1)
                            else:
                                dve.wait_ge(S["tap"], 1)
                                dve.sem_inc(S["tap"], -1)
                                dve.scalar_tensor_tensor(out=dst, in0=src, scalar=w, in1=dst, op0=ALU.mult,
                                                         op1=ALU.add).then_inc(S["tap"], 1)
                    dve.wait_ge(S["tap"], 2)
                    dve.sem_inc(S["tap"], -2)
                    for s in range(2):
                        dst = tile(cacc, i * 2 + s)
                        ts(dst, dst, 0.5, col("conv_b", i * 2 + s), ALU.mult, ALU.add)
                layer_norm([cacc[:, i, :] for i in range(NW)], W)
                for i in range(NW):
                    t = tmp[:, i % 2, :]
                    dve.wait_ge(S["tanh_ready"], 1)
                    dve.sem_inc(S["tanh_ready"], -1)
                    stt(t, sq[:, i % 2, :], 1.0, cacc[:, i, :], ALU.add, ALU.mult, f"sq{i % 2}_used")
                    stt(t, t, 0.25, cgate[:, i, :], ALU.mult, ALU.mult, "tmp_ready")
                    if i:
                        lower(yh[:, i - 1, :], yl[:, i - 1, :], tmp[:, (i - 1) % 2, :])
                lower(yh[:, NW - 1, :], yl[:, NW - 1, :], tmp[:, (NW - 1) % 2, :])
                dve.wait_ge(S["pos_dve"], 1)
                dve.sem_inc(S["pos_dve"], -1)
                ang, red = posb[64:96, :], trig[64:96, 1, :]
                op(dve.tensor_copy(red, ang.bitcast(I32)))
                ts(ang, red, par[64:96, PC1["inv_freq"][0]:PC1["inv_freq"][0] + 1], None, ALU.mult, None)
                magic, part1, part2 = 1.5 * 2 ** 23, 6.28125, 8117 / 2 ** 22
                ts(red, ang, 1 / (2 * math.pi), magic, ALU.mult, ALU.add)
                ts(red, red, -magic, None, ALU.add, None)
                for part in (part1, part2, 2 * math.pi - part1 - part2):
                    stt(ang, red, -part, ang, ALU.mult, ALU.add)
                ts(ang, ang, 3.1415925, -3.1415925, ALU.min, ALU.max, "angle")
                dve.wait_ge(S["root"], 1)
                dve.sem_inc(S["root"], -1)
                by_token_reciprocal(2 * NT)
                place = lambda i: (4 if i < 3 else 5) + i
                for i in range(5):
                    if i in (0, 3):
                        dve.wait_ge(S["rstd_spread"], 1)
                        dve.sem_inc(S["rstd_spread"], -1)
                    gain = col("q_norm", i) if i < 3 else col("kv_norm", i - 3)
                    stt(tmp[:, i % 2, :], lat[:, i, :], gain, A[2 + i // 3][:], ALU.mult, ALU.mult, "tmp_ready",
                        *(["a2_free"] if i == 2 else ["a3_free"] if i == 4 else []))
                    if i:
                        lower(yh[:, place(i - 1), :], yl[:, place(i - 1), :], tmp[:, (i - 1) % 2, :])
                lower(yh[:, place(4), :], yl[:, place(4), :], tmp[:, 0, :])
                dve.wait_ge(S["trig_ready"], 1)
                dve.sem_inc(S["trig_ready"], -1)
                dve.wait_ge(S["kr_dve"], 1)
                dve.sem_inc(S["kr_dve"], -1)
                dve.wait_ge(S["k_rot"], 1)
                dve.sem_inc(S["k_rot"], -1)
                tt(tmp[64:96, 1, :], kr[64:96, :], trig[64:96, 0, :], ALU.mult)
                tt(tmp[64:96, 0, :], A[4][64:96, :], trig[64:96, 1, :], ALU.mult, "a4_free")
                tt(K[64:96, :], tmp[64:96, 1, :], tmp[64:96, 0, :], ALU.add)
                ts(Kh[1][64:96, :], K[64:96, :], 1.0, None, ALU.mult, None, "lat_ready")
                dve.wait_ge(S["consts_dve"], 1)
                dve.sem_inc(S["consts_dve"], -1)
                op(dve.memset(causal[:, 0:T - P], 0.0))
                ts(causal[:, T - P:T], future[:], -1.0, None, ALU.mult, None)
                with dve.Fori(0, NW) as i:
                    mla_pair(i)
                give(dve, "y32_ready")
                lower(yh[:, 8:12, :], yl[:, 8:12, :], y32)
                dve.wait_ge(S["hi_ready"], 1)
                dve.sem_inc(S["hi_ready"], -1)
                op(dve.tensor_tensor(yl[:, 4:8, :].rearrange("p a t -> p (a t)"),
                                     memf.rearrange("p a t -> p (a t)"),
                                     yh[:, 4:8, :].rearrange("p a t -> p (a t)").bitcast(F32), ALU.subtract),
                   "mem_ready")
                with dve.Fori(0, NW // 2) as i:
                    for a in range(2):
                        for b in range(2):
                            dve.wait_ge(S["scores"], 1)
                            dve.sem_inc(S["scores"], -1)
                            op(dve.tensor_reduce(st[:, 2 * b:2 * b + 2],
                                                 A[3 * a + b][:].rearrange("p (a m) -> p a m", a=2), AX, ALU.min),
                               "max_ready")
                        dve.wait_ge(S["exp_ready"], 1)
                        dve.sem_inc(S["exp_ready"], -1)
                        op(dve.reciprocal(st[:, 12:16], st[:, 4:8]))
                        tt(xprobs[a], xprobs[a], spread(st[:, 12:16], MEM), ALU.mult, "probs_ready")
                    for a in range(2):
                        dve.wait_ge(S["head_out"], 1)
                        dve.sem_inc(S["head_out"], -1)
                        stt(tile(y32, i * 2 + a), A[3 * a + 2][:], 0.5, tile(xgate, i * 2 + a), ALU.mult, ALU.mult,
                            f"a{3 * a + 2}_free", f"qk{a}_free", f"v{a}_free")
                give(dve, "y32_ready")
                lower(yh[:, 4:8, :], yl[:, 4:8, :], y32, "y32_free")
                with dve.Fori(0, 6) as i:
                    for s, g in enumerate((g0, g1)):
                        dve.wait_ge(S["part_ready"], 1)
                        dve.sem_inc(S["part_ready"], -1)
                        t = RKV[:, bass.ds(i * 2 + s, 1), 1:T].rearrange("p a t -> p (a t)")
                        stt(t, g[:, 0:T - 1], col("mu", i * 2 + s), t, ALU.mult, ALU.add, f"g{s}_free")
                dve.wait_ge(S["part_ready"], 1)
                dve.sem_inc(S["part_ready"], -1)
                stt(wa[:, 1:T], g0[:, 0:T - 1], col("mu", 12), wa[:, 1:T], ALU.mult, ALU.add, "g0_free", "wa_mixed")
                for i in range(NW):
                    ts(KK[:, i, :], RK_[:, i, :], col("k_k", i), None, ALU.mult, None, "kk_ready")
                    dve.wait_ge(S["a_ready"], 1)
                    dve.sem_inc(S["a_ready"], -1)
                    ts(tmp[:, 0, :], BB[:, i, :], der[:, 21 + i:22 + i], der[:, 25 + i:26 + i], ALU.mult, ALU.add)
                    tt(RK_[:, i, :], RK_[:, i, :], tmp[:, 0, :], ALU.mult)
                dve.wait_ge(S["root"], 1)
                dve.sem_inc(S["root"], -1)
                ts(tk[:, 0:32], tk[:, 0:32], 1e-12, None, ALU.max, None)
                op(dve.reciprocal(tk[:, 0:32], tk[:, 0:32]), "rstd_ready")
                for i in range(NW):
                    dve.wait_ge(S["rstd_spread"], 1)
                    dve.sem_inc(S["rstd_spread"], -1)
                    tt(KK[:, i, :], KK[:, i, :], A[2 + i][:], ALU.mult, f"a{2 + i}_free")
                    stt(BB[:, i, :], BB[:, i, :], 1.0, KK[:, i, :], ALU.add, ALU.mult)
                op(dve.memset(St[:, :, :], 0.0))
                op(dve.memset(QC[:, :, 0:1], 0.0))
                with dve.Fori(0, NT // 2) as cc:
                    for u in range(2):
                        chunk = cc * 2 + u
                        for g in range(2):
                            rwkv_half(g, chunk)
                def gate_pair(i):
                    for s, g in enumerate((g0, g1)):
                        dve.wait_ge(S["tanh_ready"], 1)
                        dve.sem_inc(S["tanh_ready"], -1)
                        stt(rgate[:, 2 * i + s, :], sq[:, s, :], 1.0, g[:], ALU.add, ALU.mult, f"g{s}_free",
                            f"sq{s}_used")

                give(dve, "gn_in")
                for i in range(NW):
                    dve.wait_ge(S["gn_sum"], 1)
                    dve.sem_inc(S["gn_sum"], -1)
                    stt(R[:, i, :], A[i][:], -1.0 / 64, R[:, i, :], ALU.mult, ALU.add, f"a{i}_free", "centered")
                by_token_reciprocal(32)
                gate_pair(0)
                for i in range(NW):
                    dve.wait_ge(S["rstd_spread"], 1)
                    dve.sem_inc(S["rstd_spread"], -1)
                    tt(R[:, i, :], R[:, i, :], A[i][:], ALU.mult, f"a{i}_free", "scaled")
                for i in range(NW):
                    dve.wait_ge(S["affine"], 1)
                    dve.sem_inc(S["affine"], -1)
                    tt(R[:, i, :], R[:, i, :], RK_[:, i, :], ALU.add)
                gate_pair(1)
                for i in range(NW):
                    stt(R[:, i, :], R[:, i, :], 0.5, rgate[:, i, :], ALU.mult, ALU.mult, "y32_ready")
                for i in range(NW):
                    lower(yh[:, i, :], yl[:, i, :], R[:, i, :])
                give(dve, "y_ready", "y_ready", "y_ready", "y_ready")
                with dve.Fori(0, 2) as i:
                    for u in range(2):
                        merge(i * 4 + 2 * u)
                give(dve, "merged_ready")
                op(dve.memset(rstd[:], 0.0))
                with dve.Fori(0, KD // 2) as m:
                    for s, g in enumerate((g0, g1)):
                        dve.wait_ge(S["out_proj"], 1)
                        dve.sem_inc(S["out_proj"], -1)
                        h = tile(hT, m * 2 + s)
                        stt(h, tile(xh, m * 2 + s).bitcast(F32), ALPHA, g[:], ALU.mult, ALU.add, f"g{s}_free")
                        stt(h, tile(xl, m * 2 + s).bitcast(F32), ALPHA, h, ALU.mult, ALU.add)
                        tt(rstd[:], rstd[:], h, ALU.add)
                layer_norm([hT[:, i, :] for i in range(KD)], D)
                for i in range(KD):
                    lower(xh[:, i, :], xl[:, i, :], hT[:, i, :], "x_ready")
                give(dve, "par_free")


def second_block(nc, S, par_dram, stream, out, hT):
    give, fin = helpers(S)
    with ExitStack() as ctx:
        def sb(name, shape, dt=F32):
            return ctx.enter_context(nc.sbuf_tensor(name + "_2", shape, dt))

        bank = [ctx.enter_context(nc.psum_tensor(f"bank{i}_2", [P, 512], F32)) for i in range(8)]
        g0, g1 = bank[0], bank[1]
        A = bank[2:]
        stage = sb("stage", [P, STAGE_SLOTS, GW])
        wh = sb("wh", [P, SPLIT_SLOTS, GW], F32R)
        wl = sb("wl", [P, SPLIT_SLOTS, GW], F32R)
        uh = sb("uh", [P, KD, T], F32R)
        ul = sb("ul", [P, KD, T], F32R)
        par = sb("par", [P, NP2])
        der = sb("der", [P, 16])
        ones = sb("ones", [P, P])
        ident = sb("ident", [P, P])
        near = sb("near", [P, T])
        ago = sb("ago", [P, T])
        tmp = sb("tmp", [P, 2, T])
        sq = sb("sq", [P, 2, T])
        squares = sq[:, 0, :]
        rstd = sb("rstd", [P, T])
        QKV2 = sb("QKV2", [P, 6, T])
        hst = sb("hst", [P, 2, NT])
        st = sb("st", [P, 20])

        with ExitStack() as heads_ctx:
            def place(name, shape, dt=F32):
                return heads_ctx.enter_context(nc.sbuf_tensor(name + "_2", shape, dt))

            mixh = place("mixh", [P, KD, T], F32R)
            mixl = place("mixl", [P, KD, T], F32R)
            high = place("high", [P, (NF - KD) * T])
            low = place("low", [P, (NF - KD) * T])
        hidh = sb("hidh", [P, NF, T], F32R)
        hidl = sb("hidl", [P, NF, T], F32R)
        PTh = [low[:, 4 * T * a:4 * T * (a + 1)].rearrange("p (a t) -> p a t", t=T) for a in range(2)]
        Qh, Kh, Vh = ([low[:, (8 + 2 * n + a) * T:(9 + 2 * n + a) * T] for a in range(2)] for n in range(3))
        Q2, K2, V2 = ([QKV2[:, 2 * n + a, :] for a in range(2)] for n in range(3))
        diff_set = [(Qh, Kh, Vh, ("qk0_free", "qk1_free"), ("v0_free", "v1_free")),
                    (Q2, K2, V2, ("qk2_free", "qk3_free"), ("v2_free", "v3_free"))]
        prh = []
        for a in range(2):
            even, odd = 14 * P * a, 14 * P * a + 6 * P
            prh.append([[high[:, even + 3 * P * j:even + 3 * P * (j + 1)] for j in range(2)],
                        [high[:, odd + 4 * P * j:odd + 4 * P * (j + 1)] for j in range(2)]])
        gamh, rsh, gateh = ([high[:, (7 + 2 * n + a) * T:(8 + 2 * n + a) * T] for a in range(2)] for n in range(3))

        def col(name, i=0, n=1):
            a = PC2[name][0]
            return par[:, a + i:a + i + n] if isinstance(i, int) else par[:, bass.ds(i + a, n)]

        def over_columns(v):
            return bass.AP(v.tensor, v.offset, [v.ap[0], [0, P]])

        block = ctx.enter_context(nc.Block())

        @block.sync
        def _(sp):
            weight_loader(sp, S, stage, stream, DEPTH * G2)
            for i in range(KD):
                sp.wait_ge(S["out_ready"], 1)
                sp.sem_inc(S["out_ready"], -1)
                sp.dma_start(out[i * P:(i + 1) * P, :], hT[:, i, :]).then_inc(S["out_done"], 16)
            sp.wait_ge(S["out_done"], 16 * KD)
            sp.sem_inc(S["out_done"], -16 * KD)

        @block.gpsimd
        def _(pool):
            fin(pool, "pool_self", pool.memset(ones[:], 1.0))
            fin(pool, "pool_self", pool.memset(ident[:], 0.0))
            fin(pool, "pool_self", pool.affine_select(out=ident[:], in_=ident[:], compare_op=ALU.not_equal,
                                                      fill=1.0, base=0, pattern=[[-1, P]], channel_multiplier=1),
                "consts_pe")
            fin(pool, "pool_self", pool.iota(ago[:], [[-1, T]], base=0, channel_multiplier=1,
                                             allow_small_or_imprecise_dtypes=True))
            fin(pool, "pool_self", pool.affine_select(out=ago[:], in_=ago[:], compare_op=ALU.is_ge, fill=MASKED,
                                                      base=0, pattern=[[1, T]], channel_multiplier=-1),
                "ago_ready")
            fin(pool, "pool_self", pool.iota(near[:], [[1, T]], base=P - T, channel_multiplier=-1,
                                             allow_small_or_imprecise_dtypes=True))
            fin(pool, "pool_self", pool.affine_select(out=near[:], in_=near[:], compare_op=ALU.is_ge, fill=MASKED,
                                                      base=T - P, pattern=[[-1, T]], channel_multiplier=1),
                "near_ready")
            weight_remainders(pool, S, give, fin, stage, wh, wl, DEPTH * G2)

        @block.tensor
        def _(pe):
            pe.wait_ge(S["consts_pe"], 1)
            pe.sem_inc(S["consts_pe"], -1)
            proj = Projector(pe, S, wh, wl)

            def norm_root():
                pe.wait_ge(S["squares_ready"], 1)
                pe.sem_inc(S["squares_ready"], -1)
                for t in range(NT):
                    n = pe.matmul(A[0][:, t:t + 1], squares[:, t * P:(t + 1) * P], ones[:, 0:1], start=True, stop=True)
                n.then_inc(S["sumsq"], 1)
                pe.wait_ge(S["rstd_ready"], 1)
                pe.sem_inc(S["rstd_ready"], -1)
                for t in range(NT):
                    n = pe.matmul(A[1][:, t * P:(t + 1) * P], over_columns(st[:, t:t + 1]), ident[:], start=True,
                                  stop=True)
                n.then_inc(S["rstd_spread"], 1)

            def values(bank, free, by_channel):
                pe.wait_ge(S["v_raw"], 1)
                pe.sem_inc(S["v_raw"], -1)
                pe.wait_ge(S[free], 1)
                pe.sem_inc(S[free], -1)
                for t in range(NT):
                    n = pe.transpose(bank[:, t * P:(t + 1) * P], by_channel[:, t * P:(t + 1) * P], ident[:])
                n.then_inc(S["v_turned"], 1)

            def outputs(V):
                for a in range(2):
                    pe.wait_ge(S["v_ready"], 1)
                    pe.sem_inc(S["v_ready"], -1)
                    pe.wait_ge(S["weights_ready"], 1)
                    pe.sem_inc(S["weights_ready"], -1)
                    pe.wait_ge(S[f"a{4 + a}_free"], 1)
                    pe.sem_inc(S[f"a{4 + a}_free"], -1)
                    for i in range(NT):
                        n = pe.matmul(A[4 + a][:, i * P:T], V[a][:, i * P:(i + 1) * P], PTh[a][:, i, i * P:T],
                                      start=i == 0, stop=i == NT - 1)
                    n.then_inc(S["head_out"], 1)

            def output_sums(banks, free):
                for a in range(2):
                    pe.wait_ge(S["head_sq_ready"], 1)
                    pe.sem_inc(S["head_sq_ready"], -1)
                    pe.wait_ge(S[free[a]], 1)
                    pe.sem_inc(S[free[a]], -1)
                    pe.matmul(banks[a][:], ones[:], sq[:, a, :], start=True, stop=True).then_inc(S["head_sumsq"], 1)

            with pe.Fori(0, DEPTH) as layer:
                norm_root()
                pe.wait_ge(S["lam_prod"], 1)
                pe.sem_inc(S["lam_prod"], -1)
                pe.matmul(A[2][:, 0:2], ones[0:64, :], der[0:64, 8:10], start=True, stop=True)\
                  .then_inc(S["lam_sums"], 1)
                for pair in range(2):
                    pe.wait_ge(S["g0_free"], 1)
                    pe.sem_inc(S["g0_free"], -1)
                    proj.channels(g0[:], proj.group(), (uh, ul), KD, P, done="q_proj",
                                  each=None if pair else "u_ready")
                    pe.wait_ge(S["g1_free"], 1)
                    pe.sem_inc(S["g1_free"], -1)
                    proj.channels(g1[:], proj.group(), (uh, ul), KD, P, done="k_proj")
                    for a in range(2):
                        r = slice(64 * a, 64 * a + 64)
                        pe.wait_ge(S["g0_free"], 1)
                        pe.sem_inc(S["g0_free"], -1)
                        proj.channels(g0[:], proj.group(), (uh, ul), KD, P, done="v_proj")
                        if a == 0:
                            pe.wait_ge(S["qk_ready"], 1)
                            pe.sem_inc(S["qk_ready"], -1)
                        for i in range(NT):
                            pe.wait_ge(S[f"a{i}_free"], 1)
                            pe.sem_inc(S[f"a{i}_free"], -1)
                            pe.matmul(A[i][:, i * P:T], Kh[0][r, i * P:(i + 1) * P], Qh[0][r, i * P:T], start=True,
                                      stop=True).then_inc(S["scores"], 1)
                        pe.wait_ge(S["g1_free"], 1)
                        pe.sem_inc(S["g1_free"], -1)
                        proj.channels(g1[:], proj.group(), (uh, ul), KD, P, done="gate_proj")
                        values(A[4 + a], f"a{4 + a}_free", high[:, a * T:(a + 1) * T])
                    outputs(Vh)
                    output_sums(A[0:2], ("a0_free", "a1_free"))
                def diff_group(n):
                    a, part = n // 3, n % 3
                    u = (a + part) % 2
                    pe.wait_ge(S[f"g{u}_free"], 1)
                    pe.sem_inc(S[f"g{u}_free"], -1)
                    proj.channels((g0, g1)[u][:], proj.group(), (uh, ul), KD, P,
                                  done=("q_proj", "k_proj", "v_proj")[part])

                def scores(pair, a, t):
                    Q, K = diff_set[pair][0:2]
                    n = (t + 1) * P
                    for j in range(2):
                        pe.wait_ge(S[f"a{2 * a + j}_free"], 1)
                        pe.sem_inc(S[f"a{2 * a + j}_free"], -1)
                        pe.matmul(A[2 * a + j][:, 0:n], Q[a][64 * j:64 * j + 64, t * P:n],
                                  K[a][64 * j:64 * j + 64, 0:n], start=True, stop=True).then_inc(S["scores"], 1)

                def turn(a, t):
                    pe.wait_ge(S["probs_ready"], 1)
                    pe.sem_inc(S["probs_ready"], -1)
                    pe.wait_ge(S[f"a{4 + a}_free"], 1)
                    pe.sem_inc(S[f"a{4 + a}_free"], -1)
                    for i in range(t + 1):
                        n = pe.transpose(A[4 + a][:, i * P:(i + 1) * P], prh[a][t % 2][0][:, i * P:(i + 1) * P],
                                         ident[:])
                    n.then_inc(S["probs_turned"], 1)

                for a in range(2):
                    for n in range(3):
                        diff_group(3 * a + n)
                    pe.wait_ge(S["qk_ready"], 1)
                    pe.sem_inc(S["qk_ready"], -1)
                    scores(0, a, 0)
                    values((g0, g1)[a], f"g{a}_free", tmp[:, a, :])
                for pair in range(2):
                    for t in range(NT):
                        if t + 1 < NT:
                            for a in range(2):
                                scores(pair, a, t + 1)
                        if pair == 0:
                            diff_group((0, 2, 3, 5)[t])
                        turn(0, t)
                        if pair == 0 and t % 2 == 0:
                            diff_group((1, 4)[t // 2])
                        turn(1, t)
                        if pair == 0 and t % 2 == 1:
                            values((g0, g1)[t // 2], f"g{t // 2}_free", tmp[:, t // 2, :])
                    outputs(diff_set[pair][2])
                    if pair == 0:
                        for a in range(2):
                            pe.wait_ge(S["qk_ready"], 1)
                            pe.sem_inc(S["qk_ready"], -1)
                            scores(1, a, 0)
                    for a, g in enumerate((g0, g1)):
                        pe.wait_ge(S["head_sq_ready"], 1)
                        pe.sem_inc(S["head_sq_ready"], -1)
                        pe.wait_ge(S[f"g{a}_free"], 1)
                        pe.sem_inc(S[f"g{a}_free"], -1)
                        for t in range(NT):
                            n = pe.matmul(g[:, t:t + 1], sq[:, a, t * P:(t + 1) * P], ones[:, 0:1], start=True,
                                          stop=True)
                        n.then_inc(S["head_sumsq"], 1)
                    for a, g in enumerate((g0, g1)):
                        pe.wait_ge(S["head_rstd"], 1)
                        pe.sem_inc(S["head_rstd"], -1)
                        for t in range(NT):
                            n = pe.matmul(g[:, t * P:(t + 1) * P], over_columns(hst[:, a, t:t + 1]), ident[:],
                                          start=True, stop=True)
                        n.then_inc(S["head_spread"], 1)
                pe.wait_ge(S["mix_ready"], 1)
                pe.sem_inc(S["mix_ready"], -1)
                with pe.Fori(0, KD // 2) as m:
                    for s, g in enumerate((g0, g1)):
                        pe.wait_ge(S[f"g{s}_free"], 1)
                        pe.sem_inc(S[f"g{s}_free"], -1)
                        proj.channels(g[:], proj.group(), (mixh, mixl), KD, P, done="out_proj")
                norm_root()

                def hidden_pair(each=None):
                    for s in range(2):
                        pe.wait_ge(S[("g0_free", "a2_free")[s]], 1)
                        pe.sem_inc(S[("g0_free", "a2_free")[s]], -1)
                        proj.channels((g0, A[2])[s][:], proj.group(), (uh, ul), KD, P, done="gate_proj",
                                      each=None if s else each)
                        pe.wait_ge(S[("g1_free", "a3_free")[s]], 1)
                        pe.sem_inc(S[("g1_free", "a3_free")[s]], -1)
                        proj.channels((g1, A[3])[s][:], proj.group(), (uh, ul), KD, P, done="up_proj")

                hidden_pair("u_ready")
                with pe.Fori(0, NF // 2 - 1) as f:
                    hidden_pair()
                pe.wait_ge(S["hidden_ready"], 1)
                pe.sem_inc(S["hidden_ready"], -1)
                with pe.Fori(0, KD // 2) as m:
                    for s, g in enumerate((g0, g1)):
                        pe.wait_ge(S[f"g{s}_free"], 1)
                        pe.sem_inc(S[f"g{s}_free"], -1)
                        for c, n in enumerate((8, 8, NF - 16)):
                            proj.channels(g[:], proj.group(), (hidh, hidl), n, P, done="down_proj" if c == 2 else None,
                                          k0=8 * c, more=c < 2, first=c == 0)
            norm_root()

        @block.scalar
        def _(act):
            for n in ("sq0_used", "sq1_used"):
                give(act, n)

            round_next = rounder(act, S, stage, wh)
            round_next()

            def norm_root():
                act.wait_ge(S["sumsq"], 1)
                act.sem_inc(S["sumsq"], -1)
                act.activation(st[:, 0:NT], A[0][:, 0:NT], ACT.Sqrt, scale=1.0 / D, bias=EPS_COL)\
                   .then_inc(S["root"], 1)

            def normed():
                norm_root()
                for i in range(KD):
                    act.wait_ge(S[f"tmp{i % 2}_ready"], 1)
                    act.sem_inc(S[f"tmp{i % 2}_ready"], -1)
                    act.activation(uh[:, i, :], tmp[:, i % 2, :], ACT.Copy).then_inc(S["hi_ready"], 1)

            def head_squares():
                for a in range(2):
                    act.wait_ge(S["head_out"], 1)
                    act.sem_inc(S["head_out"], -1)
                    act.wait_ge(S[f"sq{a}_used"], 1)
                    act.sem_inc(S[f"sq{a}_used"], -1)
                    act.activation(sq[:, a, :], A[4 + a][:], ACT.Square).then_inc(S["head_sq_ready"], 1)

            def head_roots(banks, free):
                for a in range(2):
                    act.wait_ge(S["head_sumsq"], 1)
                    act.sem_inc(S["head_sumsq"], -1)
                    fin(act, "act_self", act.activation(rsh[a], banks[a][:], ACT.Sqrt, scale=1.0 / P, bias=EPS_COL),
                        "root", free[a], f"sq{a}_used")

            def values(free, g, by_channel):
                act.wait_ge(S["v_proj"], 1)
                act.sem_inc(S["v_proj"], -1)
                act.wait_ge(S[free], 1)
                act.sem_inc(S[free], -1)
                fin(act, "act_self", act.activation(by_channel, (g0, g1)[g][:], ACT.Copy), f"g{g}_free", "v_raw")

            def values_turned(V, bank, free):
                act.wait_ge(S["v_turned"], 1)
                act.sem_inc(S["v_turned"], -1)
                fin(act, "act_self", act.activation(V, bank[:], ACT.Copy), free, "v_ready")

            eps = der[:, 10:11]
            EPS_COL = eps
            act.wait_ge(S["ago_ready"], 1)
            act.sem_inc(S["ago_ready"], -1)
            with act.Fori(0, DEPTH) as layer:
                act.wait_ge(S["par_free"], 1)
                act.sem_inc(S["par_free"], -1)
                act.dma_start(par[:], par_dram[bass.ds(layer, 1)].rearrange("a p n -> p (a n)"))\
                   .then_inc(S["par_full"], 16)
                act.wait_ge(S["par_full"], 16)
                act.sem_inc(S["par_full"], -16)
                give(act, "par_dve")
                norm_root()
                act.wait_ge(S["lam_sums"], 1)
                act.sem_inc(S["lam_sums"], -1)
                act.activation(der[:, 0:2], A[2][:, 0:2], ACT.Exp).then_inc(S["lam_exp"], 1)
                for i in range(KD):
                    act.wait_ge(S[f"tmp{i % 2}_ready"], 1)
                    act.sem_inc(S[f"tmp{i % 2}_ready"], -1)
                    act.activation(uh[:, i, :], tmp[:, i % 2, :], ACT.Copy).then_inc(S["hi_ready"], 1)
                with act.Fori(0, 2) as pair:
                    round_next()
                    act.wait_ge(S["q_proj"], 1)
                    act.sem_inc(S["q_proj"], -1)
                    act.wait_ge(S["qk0_free"], 1)
                    act.sem_inc(S["qk0_free"], -1)
                    fin(act, "act_self", act.activation(Qh[0], g0[:], ACT.Copy, scale=64 ** -0.5), "g0_free")
                    round_next()
                    for a in range(2):
                        act.wait_ge(S[f"gam{a}_free"], 1)
                        act.sem_inc(S[f"gam{a}_free"], -1)
                        act.activation(gamh[a], ago[:], ACT.Exp, scale=col("log_gamma", pair * 2 + a))\
                           .then_inc(S["gam_ready"], 1)
                    act.wait_ge(S["k_proj"], 1)
                    act.sem_inc(S["k_proj"], -1)
                    fin(act, "act_self", act.activation(Kh[0], g1[:], ACT.Copy), "g1_free", "qk_ready")
                    for a in range(2):
                        round_next()
                        values(f"v{a}_free", 0, high[:, a * T:(a + 1) * T])
                        round_next()
                        act.wait_ge(S["gate_proj"], 1)
                        act.sem_inc(S["gate_proj"], -1)
                        act.wait_ge(S[f"tmp{a}_free"], 1)
                        act.sem_inc(S[f"tmp{a}_free"], -1)
                        act.activation(tmp[:, a, :], g1[:], ACT.Tanh, scale=0.5).then_inc(S["tanh_ready"], 1)
                        values_turned(Vh[a], A[4 + a], f"a{4 + a}_free")
                    head_squares()
                    head_roots(A[0:2], ("a0_free", "a1_free"))
                def exponentials(a, t):
                    n, u = (t + 1) * P, t % 2
                    for j in range(2):
                        c = 4 * a + 2 * u + j
                        act.wait_ge(S["max_ready"], 1)
                        act.sem_inc(S["max_ready"], -1)
                        act.activation(prh[a][u][j][:, 0:n], prh[a][u][j][:, 0:n], ACT.Exp, scale=-1.0,
                                       bias=st[:, c:c + 1], accum_out=st[:, 8 + c:9 + c]).then_inc(S["exp_ready"], 1)

                def diff_copy(pair, n):
                    Q, K, V, qk_free, v_free = diff_set[pair]
                    a, part = n // 3, n % 3
                    u = (a + part) % 2
                    if part == 0:
                        act.wait_ge(S["q_proj"], 1)
                        act.sem_inc(S["q_proj"], -1)
                        act.wait_ge(S[qk_free[a]], 1)
                        act.sem_inc(S[qk_free[a]], -1)
                        fin(act, "act_self", act.activation(Q[a], (g0, g1)[u][:], ACT.Copy, scale=-64 ** -0.5),
                            f"g{u}_free")
                    elif part == 1:
                        act.wait_ge(S["k_proj"], 1)
                        act.sem_inc(S["k_proj"], -1)
                        fin(act, "act_self", act.activation(K[a], (g0, g1)[u][:], ACT.Copy), f"g{u}_free", "qk_ready")
                    else:
                        act.wait_ge(S[f"tmp{a}_free"], 1)
                        act.sem_inc(S[f"tmp{a}_free"], -1)
                        values(v_free[a], u, tmp[:, a, :])

                def diff_values(pair, a):
                    values_turned(diff_set[pair][2][a], (g0, g1)[a], f"g{a}_free")
                    give(act, f"tmp{a}_free")

                def turned(a, t):
                    n = (t + 1) * P
                    act.wait_ge(S["probs_turned"], 1)
                    act.sem_inc(S["probs_turned"], -1)
                    fin(act, "act_self",
                        act.activation(PTh[a][:, 0:t + 1, t * P:n],
                                       A[4 + a][:, 0:n].rearrange("p (a b) -> p a b", b=P), ACT.Copy),
                        f"a{4 + a}_free", f"pr{a}{t % 2}_free", *(["weights_ready"] if t == NT - 1 else []))

                for a in range(2):
                    for n in range(3):
                        round_next()
                        diff_copy(0, 3 * a + n)
                    diff_values(0, a)
                    exponentials(a, 0)
                for pair in range(2):
                    for t in range(NT):
                        if pair == 0:
                            round_next()
                        if t + 1 < NT:
                            for a in range(2):
                                exponentials(a, t + 1)
                        if pair == 0:
                            diff_copy(1, (0, 2, 3, 5)[t])
                        turned(0, t)
                        if pair == 0 and t % 2 == 0:
                            round_next()
                            diff_copy(1, (1, 4)[t // 2])
                        turned(1, t)
                        if pair == 0 and t % 2 == 1:
                            diff_values(1, t // 2)
                    head_squares()
                    if pair == 0:
                        exponentials(0, 0)
                        exponentials(1, 0)
                    for a, g in enumerate((g0, g1)):
                        act.wait_ge(S["head_sumsq"], 1)
                        act.sem_inc(S["head_sumsq"], -1)
                        fin(act, "act_self", act.activation(hst[:, a, :], g[:, 0:NT], ACT.Sqrt, scale=1.0 / P,
                                                            bias=EPS_COL), "root", f"sq{a}_used")
                    for a, g in enumerate((g0, g1)):
                        act.wait_ge(S["head_spread"], 1)
                        act.sem_inc(S["head_spread"], -1)
                        fin(act, "act_self", act.activation(rsh[a], g[:], ACT.Copy), "rsh_ready", f"g{a}_free")
                with act.Fori(0, KD // 2) as m:
                    round_next()
                    round_next()
                normed()
                with act.Fori(0, NF // 2) as f:
                    for s in range(2):
                        round_next()
                        act.wait_ge(S["gate_proj"], 1)
                        act.sem_inc(S["gate_proj"], -1)
                        act.wait_ge(S["tmp1_free"], 1)
                        act.sem_inc(S["tmp1_free"], -1)
                        act.activation(tmp[:, 1, :], (g0, A[2])[s][:], ACT.Tanh, scale=0.5).then_inc(S["tanh_ready"], 1)
                        round_next()
                        act.wait_ge(S["tmp0_ready"], 1)
                        act.sem_inc(S["tmp0_ready"], -1)
                        act.activation(hidh[:, bass.ds(f * 2 + s, 1), :].rearrange("p a t -> p (a t)"),
                                       tmp[:, 0, :], ACT.Copy).then_inc(S["hi_ready"], 1)
                with act.Fori(0, KD // 2) as m:
                    for _ in range(6):
                        round_next()
            norm_root()

        @block.vector
        def _(dve):
            fin(dve, "dve_self", dve.memset(der[:, 10:11], 1e-6))
            for n in ("g0_free", "g1_free", "par_free", "qk0_free", "qk1_free", "qk2_free", "qk3_free",
                      "v0_free", "v1_free", "v2_free", "v3_free", "gam0_free",
                      "gam1_free", "tmp0_free", "tmp1_free", "a0_free", "a1_free", "a2_free", "a3_free", "a4_free",
                      "a5_free", "pr00_free", "pr01_free", "pr10_free", "pr11_free"):
                give(dve, n)

            def dve_op(ins, *names):
                fin(dve, "dve_self", ins, *names)

            def lower(dst_h, dst_l, src, *names):
                dve.wait_ge(S["hi_ready"], 1)
                dve.sem_inc(S["hi_ready"], -1)
                dve_op(dve.tensor_tensor(dst_l, src, dst_h.bitcast(F32), ALU.subtract), *names)

            def add_square(h, first=False):
                dve_op(dve.tensor_tensor(squares if first else sq[:, 1, :], h, h, ALU.mult))
                if not first:
                    dve_op(dve.tensor_tensor(squares, squares, sq[:, 1, :], ALU.add))

            def norm_root():
                give(dve, "squares_ready")
                dve.wait_ge(S["root"], 1)
                dve.sem_inc(S["root"], -1)
                dve_op(dve.reciprocal(st[:, 0:NT], st[:, 0:NT]), "rstd_ready")
                dve.wait_ge(S["rstd_spread"], 1)
                dve.sem_inc(S["rstd_spread"], -1)

            def normed(gain):
                norm_root()
                for i in range(KD):
                    dve_op(dve.scalar_tensor_tensor(out=tmp[:, i % 2, :], in0=hT[:, i, :], scalar=col(gain, i),
                                                    in1=A[1][:], op0=ALU.mult, op1=ALU.mult), f"tmp{i % 2}_ready")
                    if i:
                        lower(uh[:, i - 1, :], ul[:, i - 1, :], tmp[:, (i - 1) % 2, :], "u_ready")
                lower(uh[:, KD - 1, :], ul[:, KD - 1, :], tmp[:, (KD - 1) % 2, :], "u_ready")

            def heads(gain, gated, tile, v_free=("v0_free", "v1_free")):
                if not gated:
                    for a in range(2):
                        dve.wait_ge(S["root"], 1)
                        dve.sem_inc(S["root"], -1)
                        dve_op(dve.reciprocal(hst[:, a, :], hst[:, a, :]), "head_rstd")
                for a in range(2):
                    t, hi, lo = tmp[:, a, :], *(x[:, tile + a, :] if isinstance(tile, int) else
                                                x[:, bass.ds(tile + a, 1), :].rearrange("p a t -> p (a t)")
                                                for x in (mixh, mixl))
                    if gated:
                        dve.wait_ge(S["root"], 1)
                        dve.sem_inc(S["root"], -1)
                        dve_op(dve.reciprocal(rsh[a], rsh[a]))
                    else:
                        dve.wait_ge(S["rsh_ready"], 1)
                        dve.sem_inc(S["rsh_ready"], -1)
                    dve_op(dve.scalar_tensor_tensor(out=t, in0=A[4 + a][:], scalar=gain, in1=rsh[a], op0=ALU.mult,
                                                    op1=ALU.mult), f"a{4 + a}_free", v_free[a])
                    if gated:
                        dve_op(dve.scalar_tensor_tensor(out=t, in0=t, scalar=0.5, in1=gateh[a], op0=ALU.mult,
                                                        op1=ALU.mult))
                    dve_op(dve.tensor_copy(hi, t))
                    dve_op(dve.tensor_tensor(lo, t, hi.bitcast(F32), ALU.subtract),
                           *([f"tmp{a}_free"] if gated else []))

            for i in range(KD):
                add_square(hT[:, i, :], i == 0)
            dve.wait_ge(S["near_ready"], 1)
            dve.sem_inc(S["near_ready"], -1)
            with dve.Fori(0, DEPTH) as layer:
                dve.wait_ge(S["par_dve"], 1)
                dve.sem_inc(S["par_dve"], -1)
                lam = PC2["lam"][0]
                dve_op(dve.tensor_tensor(der[0:64, 8:10], par[0:64, lam:lam + 3:2], par[0:64, lam + 1:lam + 4:2],
                                         ALU.mult), "lam_prod")
                normed("attn_norm")
                dve.wait_ge(S["lam_exp"], 1)
                dve.sem_inc(S["lam_exp"], -1)
                dve_op(dve.tensor_tensor(der[:, 2:3], der[:, 1:2], der[:, 0:1], ALU.subtract))
                dve_op(dve.tensor_tensor(der[:, 3:4], der[:, 2:3], col("lam_init"), ALU.subtract))
                dve_op(dve.tensor_tensor(der[:, 4:5], col("diff_norm"), col("lam_rest"), ALU.mult))
                with dve.Fori(0, 2) as pair:
                    for a in range(2):
                        dve.wait_ge(S["gam_ready"], 1)
                        dve.sem_inc(S["gam_ready"], -1)
                        for i in range(NT):
                            dve.wait_ge(S["scores"], 1)
                            dve.sem_inc(S["scores"], -1)
                            dve_op(dve.tensor_tensor(PTh[a][:, i, i * P:T], A[i][:, i * P:T], gamh[a][:, 0:T - i * P],
                                                     ALU.mult), f"a{i}_free",
                                   *([f"gam{a}_free", "weights_ready"] + ["qk0_free"] * a if i == NT - 1 else []))
                        dve.wait_ge(S["tanh_ready"], 1)
                        dve.sem_inc(S["tanh_ready"], -1)
                        dve_op(dve.scalar_tensor_tensor(out=gateh[a], in0=tmp[:, a, :], scalar=1.0, in1=g1[:],
                                                        op0=ALU.add, op1=ALU.mult), "g1_free")
                    heads(col("ret_norm"), True, pair * 2)
                def maxima(pair, a, t):
                    n, u = (t + 1) * P, t % 2
                    dve.wait_ge(S[f"pr{a}{u}_free"], 1)
                    dve.sem_inc(S[f"pr{a}{u}_free"], -1)
                    for j in range(2):
                        c = 4 * a + 2 * u + j
                        dve.wait_ge(S["scores"], 1)
                        dve.sem_inc(S["scores"], -1)
                        dve_op(dve.tensor_tensor_reduce(prh[a][u][j][:, 0:n], A[2 * a + j][:, 0:n],
                                                        gamh[a][:, T - n:T], 1.0, 3e38, ALU.add, ALU.min,
                                                        st[:, c:c + 1]), f"a{2 * a + j}_free", "max_ready",
                               *([diff_set[pair][3][a]] if (t, j) == (NT - 1, 1) else []))

                def first_maxima(pair):
                    for a in range(2):
                        dve_op(dve.tensor_scalar(gamh[a], near[:], col("slope", pair * 2 + a), -1.0, ALU.mult,
                                                 ALU.mult))
                    maxima(pair, 0, 0)
                    maxima(pair, 1, 0)

                first_maxima(0)
                for pair in range(2):
                    for t in range(NT):
                        for a in range(2):
                            if t + 1 < NT:
                                maxima(pair, a, t + 1)
                            n, u = (t + 1) * P, t % 2
                            c = 8 + 4 * a + 2 * u
                            p0, p1 = (x[:, 0:n] for x in prh[a][u])
                            dve.wait_ge(S["exp_ready"], 2)
                            dve.sem_inc(S["exp_ready"], -2)
                            dve_op(dve.reciprocal(st[:, 16:18], st[:, c:c + 2]))
                            dve_op(dve.tensor_tensor(st[:, 17:18], st[:, 17:18], der[:, 3:4], ALU.mult))
                            dve_op(dve.tensor_scalar(p0, p0, st[:, 16:17], None, ALU.mult))
                            dve_op(dve.scalar_tensor_tensor(out=p0, in0=p1, scalar=st[:, 17:18], in1=p0, op0=ALU.mult,
                                                            op1=ALU.add), "probs_ready")
                    if pair == 0:
                        first_maxima(1)
                    heads(der[:, 4:5], False, pair * 2 + 4, diff_set[pair][4])
                give(dve, "mix_ready")
                dve_op(dve.memset(squares, 0.0))
                with dve.Fori(0, KD // 2) as m:
                    for s, g in enumerate((g0, g1)):
                        dve.wait_ge(S["out_proj"], 1)
                        dve.sem_inc(S["out_proj"], -1)
                        h = hT[:, bass.ds(m * 2 + s, 1), :].rearrange("p a t -> p (a t)")
                        dve_op(dve.tensor_tensor(h, g[:], h, ALU.add), f"g{s}_free")
                        add_square(h)
                normed("ffn_norm")
                with dve.Fori(0, NF // 2) as f:
                    for s in range(2):
                        dve.wait_ge(S["tanh_ready"], 1)
                        dve.sem_inc(S["tanh_ready"], -1)
                        dve_op(dve.scalar_tensor_tensor(out=rstd[:], in0=tmp[:, 1, :], scalar=1.0,
                                                        in1=(g0, A[2])[s][:], op0=ALU.add, op1=ALU.mult),
                               ("g0_free", "a2_free")[s], "tmp1_free")
                        dve.wait_ge(S["up_proj"], 1)
                        dve.sem_inc(S["up_proj"], -1)
                        dve_op(dve.scalar_tensor_tensor(out=tmp[:, 0, :], in0=(g1, A[3])[s][:], scalar=0.5,
                                                        in1=rstd[:], op0=ALU.mult, op1=ALU.mult),
                               ("g1_free", "a3_free")[s], "tmp0_ready")
                        lower(hidh[:, bass.ds(f * 2 + s, 1), :].rearrange("p a t -> p (a t)"),
                              hidl[:, bass.ds(f * 2 + s, 1), :].rearrange("p a t -> p (a t)"), tmp[:, 0, :])
                give(dve, "hidden_ready")
                dve_op(dve.memset(squares, 0.0))
                with dve.Fori(0, KD // 2) as m:
                    for s, g in enumerate((g0, g1)):
                        dve.wait_ge(S["down_proj"], 1)
                        dve.sem_inc(S["down_proj"], -1)
                        h = hT[:, bass.ds(m * 2 + s, 1), :].rearrange("p a t -> p (a t)")
                        dve_op(dve.tensor_tensor(h, g[:], h, ALU.add), f"g{s}_free")
                        add_square(h)
                give(dve, "par_free")
            norm_root()
            for i in range(KD):
                dve_op(dve.scalar_tensor_tensor(out=hT[:, i, :], in0=hT[:, i, :], scalar=col("final_norm", i),
                                                in1=A[1][:], op0=ALU.mult, op1=ALU.mult), "out_ready")


def k_tiles(w, c0, cn=P):
    n, k = w.shape[0], w.shape[1]
    return w[:, :, c0:c0 + cn].reshape(n, k // P, P, cn).transpose(0, 2, 1, 3).reshape(n, P, k // P * cn)


def as_group(a):
    return np.pad(a, ((0, 0), (0, 0), (0, GW - a.shape[2])))


def columns(v):
    return v.reshape(v.shape[0], -1, P).transpose(0, 2, 1)


def pad_stream(s):
    return np.concatenate([s.reshape(-1, P, GW), np.zeros((1, P, GW), np.float32)])


def first_stream(w_in, w_uq, w_ukv, w_mem, w_o, w_out):
    r, o = 0, 1664
    q, kv, kpe, mg, cu, cg, xq, xg, mrg = 2176, 2560, 2816, 2848, 3360, 4384, 4896, 5408, 5920
    x = lambda c0: k_tiles(w_in, c0)
    groups = []
    for i in range(NW):
        groups += [x(cu + P * i), x(cu + W + P * i)]
    groups += [x(cg + P * i) for i in range(NW)]
    latents = [x(q + P * i) for i in range(3)] + [x(kv + P * i) for i in range(2)]
    latents.append(k_tiles(np.concatenate([w_in[:, :, kpe:kpe + 32]] * 4, 2), 0))
    for i in range(2):
        groups += latents[3 * i:3 * i + 3]
        for j in (2 * i, 2 * i + 1):
            groups += [x(mg + P * j), x(xg + P * j)]
    for h in range(8):
        groups.append(as_group(np.concatenate([k_tiles(w_uq, 96 * h, 96), k_tiles(w_ukv, P * h)], 2)))
    for h in range(4):
        groups += [x(xq + P * h), k_tiles(w_mem, P * h), k_tiles(w_mem, W + P * h)]
    groups += [x(P * i) for i in range(12)]
    groups += [as_group(k_tiles(w_in[:, k:k + W], 1536)) for k in (0, W)]

    def merge(n, d):
        return [x(mrg + D * n + P * d), x(mrg + D * n + P * (d + 1)), k_tiles(w_o[:, n], P * d, 2 * P)]

    for chunk in range(NT):
        for n in (1, 2, 3):
            groups += merge(n, 2 * chunk)
    groups += [x(o + P * i) for i in range(NW)]
    for d in range(0, KD, 2):
        groups += merge(0, d)
    groups += [k_tiles(w_out, P * m) for m in range(KD)]
    assert len(groups) == G1
    return pad_stream(np.stack(groups, 1))


def first_params(mu, w0, a0, k_k, k_a, r_k, lnx_g, lnx_b, q_norm, kv_norm, conv_w, conv_b, cln_g, cln_b, b_gate,
                 ln_g, ln_b):
    taps = conv_w.reshape(DEPTH, TAPS, NW, P).transpose(0, 3, 2, 1).reshape(DEPTH, P, NW * TAPS)
    inv_freq = np.float32(10000.0) ** (-np.arange(0, 32, 2, dtype=np.float32) / np.float32(32))
    freq = np.broadcast_to(np.tile(inv_freq, P // 16)[None, :, None], (DEPTH, P, 1))
    cols = [columns(mu), columns(w0), columns(a0), columns(k_k), columns(k_a), columns(r_k.reshape(DEPTH, W)),
            columns(lnx_g), columns(lnx_b), columns(q_norm), columns(kv_norm), taps, columns(conv_b), columns(cln_g),
            columns(cln_b), columns(b_gate.reshape(DEPTH, -1)), columns(ln_g), columns(ln_b), freq]
    return np.ascontiguousarray(np.concatenate(cols, 2), dtype=np.float32)


def second_stream(w_in, w_out, w_gate, w_up, w_down):
    groups = []
    for pair in range(2):
        groups += [k_tiles(w_in, P * pair), k_tiles(w_in, 256 + P * pair)]
        for h in (2 * pair, 2 * pair + 1):
            groups += [k_tiles(w_in, 512 + P * h), k_tiles(w_in, 1024 + P * h)]
    for h in range(4):
        groups += [k_tiles(w_in, 1536 + 512 * i + P * h) for i in range(3)]
    groups += [k_tiles(w_out, P * m) for m in range(KD)]
    for f in range(NF):
        groups += [k_tiles(w_gate, P * f), k_tiles(w_up, P * f)]
    for m in range(KD):
        groups += [as_group(k_tiles(w_down[:, k:k + GW], P * m)) for k in range(0, FFN, GW)]
    assert len(groups) == G2
    s = np.stack(groups, 1)
    return pad_stream(s)


def second_params(attn_norm, ret_norm, diff_norm, ffn_norm, lam, final_norm):
    lam_init = np.array([0.8 - 0.6 * math.exp(-0.3 * i) for i in range(DEPTH)])
    full = lambda v: np.broadcast_to(np.asarray(v, np.float32).reshape(DEPTH, 1, -1), (DEPTH, P, np.size(v) // DEPTH))
    log_gamma = np.tile(-np.log1p(-np.exp2(-5.0 - np.arange(4))), (DEPTH, 1))
    slope = np.tile(np.exp2(-2.0 * np.arange(1, 5)), (DEPTH, 1))
    lams = np.concatenate([np.stack(lam, 2), np.zeros((DEPTH, 64, 4), np.float32)], 1)
    cols = [columns(attn_norm), columns(ret_norm), columns(diff_norm), columns(ffn_norm), lams, full(lam_init),
            full(1.0 - lam_init), np.repeat(columns(final_norm[None]), DEPTH, 0), full(log_gamma), full(slope)]
    return np.ascontiguousarray(np.concatenate(cols, 2), dtype=np.float32)


def build(nc, x, mem, positions, params1, lora, stream1, params2, stream2, out):
    with ExitStack() as ctx:
        hT = ctx.enter_context(nc.sbuf_tensor("hT", [P, KD, T], F32))
        with ExitStack() as first:
            S = Sems(nc, first, "first_")
            first_block(nc, S, x, mem, positions, params1, lora, stream1, hT)
            with nc.Block() as block:
                @block.gpsimd
                def _(pool):
                    for sem in S.all.values():
                        pool.sem_clear(sem)
        second_block(nc, Sems(nc, ctx, "second_"), params2, stream2, out, hT)


def kernel(**inputs):
    import concourse.bacc as bacc
    from concourse.bass_utils import run_bass_kernel_spmd

    v = {n: np.asarray(a) for n, a in inputs.items()}
    arrays = {
        "x": np.ascontiguousarray(v["x"][0].T),
        "mem": np.ascontiguousarray(v["mem"][0].T),
        "positions": v["positions"],
        "params1": first_params(*(v[n] for n in (
            "rwkv_mu", "rwkv_w0", "rwkv_a0", "rwkv_k_k", "rwkv_k_a", "rwkv_r_k", "rwkv_lnx_g", "rwkv_lnx_b",
            "mla_q_norm", "mla_kv_norm", "conv_w", "conv_b", "conv_ln_g", "conv_ln_b", "b_gate", "ln_g", "ln_b"))),
        "lora": np.ascontiguousarray(np.concatenate([v["rwkv_w2"], v["rwkv_a2"]], 1)),
        "stream1": first_stream(*(v[n] for n in ("w_in", "mla_w_uq", "mla_w_ukv", "xattn_w_mem_kv", "w_o_branch",
                                                 "w_out"))),
        "params2": second_params(*(v[n + "_2"] for n in ("attn_norm", "ret_norm", "diff_norm", "ffn_norm")),
                                 [v[f"lambda_{n}_2"] for n in ("q1", "k1", "q2", "k2")], v["final_norm_2"]),
        "stream2": second_stream(*(v[n + "_2"] for n in ("w_in", "w_out", "w_gate", "w_up", "w_down"))),
    }
    nc = bacc.Bacc("TRN2", target_bir_lowering=False, num_devices=1)
    args = [nc.dram_tensor(f"in_{n}", a.shape, mybir.dt.from_np(a.dtype), kind="ExternalInput").ap()
            for n, a in arrays.items()]
    out = nc.dram_tensor("out_x", (D, T), F32, kind="ExternalOutput").ap()
    build(nc, *args, out)
    r = run_bass_kernel_spmd(nc, [{f"in_{n}": a for n, a in arrays.items()}], core_ids=[0])
    return np.ascontiguousarray(r.results[0]["out_x"].T)[None]
```
